# Optimizing a Trainium2 kernel written in Bass

```python
import math
import jax
import jax.numpy as jnp
from jax import lax
import numpy as np
import jax, jax.numpy as jnp

D_MODEL = 1024
BATCH = 1
SEQ = 256
DEPTH = 1

GRID_W = 64
CTX_LEN = 256
N_MIXERS = 4
N_MOD = 6
EPS = 1e-6
FFN_HIDDEN = -(-8 * D_MODEL // (3 * 256)) * 256

GLA_HEADS = 4
GLA_QK = D_MODEL // 2
GLA_VD = D_MODEL
GLA_DK = GLA_QK // GLA_HEADS
GLA_DV = GLA_VD // GLA_HEADS
GLA_RANK = 16
GLA_GATE_NORM = 16.0
GLA_CHUNK = 64
GLA_IN = 2 * GLA_QK + GLA_VD + D_MODEL + 2 * GLA_RANK

HY_SHORT = 3
HY_BANDS = 16
HY_EMB = 1 + 2 * HY_BANDS
HY_FILTER_DIM = 64
HY_DECAY_TARGET = 1e-2
HY_FAST_DECAY = 0.3
HY_SLOW_DECAY = 1.5

ML_HEADS = 4
ML_INNER = 2 * D_MODEL
ML_DH = ML_INNER // ML_HEADS
ML_BLOCK = 4
ML_NBLOCKS = ML_INNER // ML_BLOCK
ML_CONV = 3
ML_CHUNK = 64

S5_GROUP = 16
S5_GROUPS = D_MODEL // S5_GROUP
S5_STATE = 64
S5_DT_MIN = 1e-3
S5_DT_MAX = 1e-1

N_GLA = (DEPTH + 3) // N_MIXERS
N_HY = (DEPTH + 2) // N_MIXERS
N_ML = (DEPTH + 1) // N_MIXERS
N_S5 = DEPTH // N_MIXERS


def rms_norm(x, g):
    x = x.astype(jnp.float32)
    return x * lax.rsqrt(jnp.mean(x * x, axis=-1, keepdims=True) + EPS) * g.astype(jnp.float32)

def head_rms_norm(o, g):
    bsz, length, heads, d = o.shape
    o = o * lax.rsqrt(jnp.mean(o * o, axis=-1, keepdims=True) + EPS) * g
    return o.reshape(bsz, length, heads * d)

def multihead_layer_norm(o, g):
    bsz, length, heads, d = o.shape
    o = o - jnp.mean(o, axis=-1, keepdims=True)
    o = o * lax.rsqrt(jnp.mean(o * o, axis=-1, keepdims=True) + EPS)
    return o.reshape(bsz, length, heads * d) * g

def modulate(h, shift, scale):
    return h * (1.0 + scale) + shift

def flip_seq(t):
    return jnp.flip(t, axis=1)

def depthwise_conv_centred(x, w, b):
    k = w.shape[0]
    y = lax.conv_general_dilated(x, w.astype(x.dtype)[:, None, :], window_strides=(1,),
                                 padding=[(k // 2, k // 2)], dimension_numbers=('NWC', 'WIO', 'NWC'),
                                 feature_group_count=x.shape[-1])
    return y + b

def to_col_major(x, rows):
    bsz, length, ch = x.shape
    return x.reshape(bsz, rows, GRID_W, ch).transpose(0, 2, 1, 3).reshape(bsz, length, ch)

def from_col_major(x, rows):
    bsz, length, ch = x.shape
    return x.reshape(bsz, GRID_W, rows, ch).transpose(0, 2, 1, 3).reshape(bsz, length, ch)

def swiglu(h, w_in, w_out):
    gate, up = jnp.split(h @ w_in, 2, axis=-1)
    return (jax.nn.silu(gate) * up) @ w_out

def gla_chunk_scan(q, k, v, g, s0):
    bsz, length, heads, _ = q.shape
    dv = v.shape[-1]
    n_chunks = length // GLA_CHUNK

    def chunked(t):
        return t.reshape(bsz, n_chunks, GLA_CHUNK, heads, t.shape[-1]).swapaxes(0, 1)

    causal = jnp.tril(jnp.ones((GLA_CHUNK, GLA_CHUNK), dtype=bool))

    def step(s, inp):
        qc, kc, vc, gc = inp
        b = jnp.cumsum(gc, axis=1)
        b_end = b[:, -1]
        q_dec = qc * jnp.exp(b)
        scores = jnp.einsum('bihd,bjhd->bhij', q_dec, kc * jnp.exp(-b))
        scores = jnp.where(causal, scores, 0.0)
        o = jnp.einsum('bhij,bjhv->bihv', scores, vc) + jnp.einsum('bihd,bhdv->bihv', q_dec, s)
        k_end = kc * jnp.exp(b_end[:, None] - b)
        s = jnp.exp(b_end)[..., None] * s + jnp.einsum('bjhd,bjhv->bhdv', k_end, vc)
        return s, o

    s_end, o = lax.scan(step, s0, (chunked(q), chunked(k), chunked(v), chunked(g)))
    return o.swapaxes(0, 1).reshape(bsz, length, heads, dv), s_end

def gla_mixer(h_lat, h_ctx, w_in, w_gate, b_gate, norm_g, w_out):
    def project(h):
        bsz, length, _ = h.shape
        z = h.astype(jnp.float32) @ w_in
        q, k, v, r, glr = jnp.split(z, [GLA_QK, 2 * GLA_QK, 2 * GLA_QK + GLA_VD,
                                       2 * GLA_QK + GLA_VD + D_MODEL], axis=-1)
        glr = glr.reshape(bsz, length, 2, GLA_RANK)
        g = jax.nn.log_sigmoid(jnp.einsum('blzr,zrk->blzk', glr, w_gate) + b_gate) / GLA_GATE_NORM
        g = g.reshape(bsz, length, 2, GLA_HEADS, GLA_DK)
        q = q.reshape(bsz, length, GLA_HEADS, GLA_DK) * GLA_DK ** -0.5
        k = k.reshape(bsz, length, GLA_HEADS, GLA_DK)
        v = v.reshape(bsz, length, GLA_HEADS, GLA_DV)
        return q, k, v, r, g[:, :, 0], g[:, :, 1]

    def bidirectional(h, s_f0, s_b0):
        q, k, v, r, g_f, g_b = project(h)
        o_f, s_f = gla_chunk_scan(q, k, v, g_f, s_f0)
        o_b, s_b = gla_chunk_scan(flip_seq(q), flip_seq(k), flip_seq(v), flip_seq(g_b), s_b0)
        o = head_rms_norm(o_f + flip_seq(o_b), norm_g)
        return (o * jax.nn.silu(r)) @ w_out, s_f, s_b

    s0 = jnp.zeros((h_ctx.shape[0], GLA_HEADS, GLA_DK, GLA_DV), jnp.float32)
    y_ctx, s_f, s_b = bidirectional(h_ctx, s0, s0)
    y_lat, _, _ = bidirectional(h_lat, s_f, s_b)
    return y_lat, y_ctx

def hyena_filter(length, w1, b1, w2, b2, w3, freq):
    pos = jnp.arange(length, dtype=jnp.float32)
    t = pos / length
    bands = jnp.linspace(1e-4, HY_BANDS - 1, HY_BANDS, dtype=jnp.float32)
    ang = 2.0 * math.pi * t[:, None] * bands[None]
    feats = jnp.concatenate([t[:, None], jnp.cos(ang), -jnp.sin(ang)], axis=-1)
    z = jnp.sin(freq * (feats @ w1 + b1))
    z = jnp.sin(freq * (z @ w2 + b2))
    h = (z @ w3).reshape(length, 2, D_MODEL)
    log_target = math.log(HY_DECAY_TARGET)
    deltas = jnp.abs(jnp.linspace(log_target / HY_SLOW_DECAY, log_target / HY_FAST_DECAY, D_MODEL,
                                  dtype=jnp.float32))
    decay = jnp.exp(-t[:, None] * deltas)
    h = h * decay[:, None]
    return h[:, 0], h[:, 1]

def fft_long_conv(u, h_f, h_b, bias):
    length = u.shape[1]
    h2 = jnp.concatenate([h_f[:1] + h_b[:1], h_f[1:], jnp.zeros_like(h_f[:1]),
                          jnp.flip(h_b[1:], axis=0)], axis=0)
    u_hat = jnp.fft.rfft(u, n=2 * length, axis=1)
    h_hat = jnp.fft.rfft(h2, axis=0)
    y = jnp.fft.irfft(u_hat * h_hat[None], n=2 * length, axis=1)[:, :length]
    return y + u * bias

def hyena_mixer(h_lat, h_ctx, w_in, conv_w, conv_b, f_w1, f_b1, f_w2, f_b2, f_w3, f_freq, f_bias, w_out):
    def run(h):
        length = h.shape[1]
        u = depthwise_conv_centred(h.astype(jnp.float32) @ w_in, conv_w, conv_b)
        x0, x1, v = jnp.split(u, 3, axis=-1)
        h_f, h_b = hyena_filter(length, f_w1, f_b1, f_w2, f_b2, f_w3, f_freq)
        y = x0 * fft_long_conv(v * x1, h_f, h_b, f_bias)
        return y @ w_out

    return run(h_lat), run(h_ctx)

def mlstm_chunk_scan(q, k, v, i_pre, log_f, state):
    bsz, length, heads, _ = q.shape
    n_chunks = length // ML_CHUNK

    def chunked(t):
        return t.reshape((bsz, n_chunks, ML_CHUNK) + t.shape[2:]).swapaxes(0, 1)

    causal = jnp.tril(jnp.ones((ML_CHUNK, ML_CHUNK), dtype=bool))[None, :, :, None]

    def step(carry, inp):
        c_mat, n_vec, m = carry
        qc, kc, vc, ic, fc = inp
        b = jnp.cumsum(fc, axis=1)
        b_end = b[:, -1]
        d_intra = jnp.where(causal, b[:, :, None] - b[:, None] + ic[:, None], -jnp.inf)
        d_inter = b + m[:, None]
        m_tok = jnp.maximum(jnp.max(d_intra, axis=2), d_inter)
        w_inter = jnp.exp(d_inter - m_tok)
        s = jnp.einsum('bihd,bjhd->bijh', qc, kc) * jnp.exp(d_intra - m_tok[:, :, None])
        num = jnp.einsum('bijh,bjhv->bihv', s, vc) + w_inter[..., None] * jnp.einsum('bihd,bhdv->bihv', qc, c_mat)
        den = jnp.sum(s, axis=2) + w_inter * jnp.einsum('bihd,bhd->bih', qc, n_vec)
        h = num / jnp.maximum(jnp.abs(den), jnp.exp(-m_tok))[..., None]
        d_state = b_end[:, None] - b + ic
        m_new = jnp.maximum(b_end + m, jnp.max(d_state, axis=1))
        w_prev = jnp.exp(b_end + m - m_new)
        w_tok = jnp.exp(d_state - m_new[:, None])
        c_mat = w_prev[..., None, None] * c_mat + jnp.einsum('bjh,bjhd,bjhv->bhdv', w_tok, kc, vc)
        n_vec = w_prev[..., None] * n_vec + jnp.einsum('bjh,bjhd->bhd', w_tok, kc)
        return (c_mat, n_vec, m_new), h

    state, h = lax.scan(step, state, (chunked(q), chunked(k), chunked(v), chunked(i_pre), chunked(log_f)))
    return h.swapaxes(0, 1).reshape(bsz, length, heads, v.shape[-1]), state

def mlstm_mixer(h_lat, h_ctx, w_in, conv_w, conv_b, w_q, w_k, w_v, w_gates, b_gates, norm_g, skip, w_out):
    def project(h):
        bsz, length, _ = h.shape
        x_m, z = jnp.split(h.astype(jnp.float32) @ w_in, 2, axis=-1)
        x_c = jax.nn.silu(depthwise_conv_centred(x_m, conv_w, conv_b))

        def block_diag(t, w):
            t = t.reshape(bsz, length, ML_NBLOCKS, ML_BLOCK)
            return jnp.einsum('blnc,ncd->blnd', t, w).reshape(bsz, length, ML_INNER)

        q, k, v = block_diag(x_c, w_q), block_diag(x_c, w_k), block_diag(x_m, w_v)
        gates = jnp.einsum('blc,zcg->blzg', jnp.concatenate([q, k, v], axis=-1), w_gates) + b_gates
        i_pre = gates[..., :ML_HEADS]
        log_f = jax.nn.log_sigmoid(gates[..., ML_HEADS:])
        heads = lambda t: t.reshape(bsz, length, ML_HEADS, ML_DH)
        return heads(q), heads(k) * ML_DH ** -0.5, heads(v), i_pre, log_f, x_c, z

    def bidirectional(h, state_f, state_b):
        q, k, v, i_pre, log_f, x_c, z = project(h)
        h_f, state_f = mlstm_chunk_scan(q, k, v, i_pre[:, :, 0], log_f[:, :, 0], state_f)
        h_b, state_b = mlstm_chunk_scan(flip_seq(q), flip_seq(k), flip_seq(v), flip_seq(i_pre[:, :, 1]),
                                        flip_seq(log_f[:, :, 1]), state_b)
        h_n = multihead_layer_norm(h_f + flip_seq(h_b), norm_g)
        return ((h_n + skip * x_c) * jax.nn.silu(z)) @ w_out, state_f, state_b

    bsz = h_ctx.shape[0]
    state0 = (jnp.zeros((bsz, ML_HEADS, ML_DH, ML_DH), jnp.float32),
              jnp.zeros((bsz, ML_HEADS, ML_DH), jnp.float32),
              jnp.full((bsz, ML_HEADS), -jnp.inf, jnp.float32))
    y_ctx, st_f, st_b = bidirectional(h_ctx, state0, state0)
    y_lat, _, _ = bidirectional(h_lat, st_f, st_b)
    return y_lat, y_ctx

def _linear_recurrence_combine(left, right):
    a_l, b_l = left
    a_r, b_r = right
    return a_l * a_r, a_r * b_l + b_r

def s5_mixer(h_lat, h_ctx, lam_re, lam_im, log_dt, b_re, b_im, c_re, c_im, d_skip, w_glu):
    f32 = jnp.float32
    b_mat = lax.complex(b_re.astype(f32), b_im.astype(f32))
    c_mat = lax.complex(c_re.astype(f32), c_im.astype(f32))

    def discretise(direction):
        lam = lax.complex(lam_re[direction].astype(f32), lam_im[direction].astype(f32))
        lam_bar = jnp.exp(lam * jnp.exp(log_dt[direction].astype(f32))[:, None])
        return lam_bar, ((lam_bar - 1.0) / lam)[..., None] * b_mat

    disc = (discretise(0), discretise(1))

    def scan_readout(u_seq, lam_bar, b_bar, x0):
        bu = jnp.einsum('gpc,lbgc->lbgp', b_bar, u_seq)
        a = jnp.broadcast_to(lam_bar, (u_seq.shape[0], 1) + lam_bar.shape)
        a_cum, xs = lax.associative_scan(_linear_recurrence_combine, (a, bu), axis=0)
        xs = xs + a_cum * x0
        return jnp.real(jnp.einsum('gcp,lbgp->lbgc', c_mat, xs)), xs[-1]

    def bidirectional(h, x0_f, x0_b):
        bsz, length, _ = h.shape
        u = h.astype(f32)
        u_seq = u.swapaxes(0, 1).reshape(length, bsz, S5_GROUPS, S5_GROUP).astype(jnp.complex64)
        y_f, x_f = scan_readout(u_seq, disc[0][0], disc[0][1], x0_f)
        y_b, x_b = scan_readout(jnp.flip(u_seq, axis=0), disc[1][0], disc[1][1], x0_b)
        y = (y_f + jnp.flip(y_b, axis=0)).reshape(length, bsz, D_MODEL).swapaxes(0, 1) + d_skip * u
        val, gate = jnp.split(jax.nn.gelu(y) @ w_glu, 2, axis=-1)
        return val * jax.nn.sigmoid(gate), x_f, x_b

    x0 = jnp.zeros((h_ctx.shape[0], S5_GROUPS, S5_STATE), jnp.complex64)
    y_ctx, x_f, x_b = bidirectional(h_ctx, x0, x0)
    y_lat, _, _ = bidirectional(h_lat, x_f, x_b)
    return y_lat, y_ctx

def first_inputs(seed: int = 0) -> dict:
    key = jax.random.key(seed)
    keys = iter(jax.random.split(key, 96))
    f32 = jnp.float32

    def normal(shape, scale=1.0):
        return scale * jax.random.normal(next(keys), shape, f32)

    def gain(shape):
        return 1.0 + normal(shape, 0.02)

    D, F = D_MODEL, FFN_HIDDEN
    ml_b_i = normal((N_ML, 2, ML_HEADS), 0.1)
    ml_b_f = jnp.linspace(3.0, 6.0, ML_HEADS, dtype=f32) + normal((N_ML, 2, ML_HEADS), 0.1)
    lam_im_init = math.pi * jnp.arange(S5_STATE, dtype=f32)
    return {
        'x': normal((BATCH, SEQ, D)),
        'c': normal((BATCH, D)),
        'ctx': normal((BATCH, CTX_LEN, D)),
        'c_ctx': normal((D,)),
        'mod_w': normal((DEPTH, D, N_MOD * D), D ** -0.5),
        'mod_b': normal((DEPTH, N_MOD * D), 0.01),
        'norm_g': gain((DEPTH, 4, D)),
        'ffn_w_in': normal((DEPTH, D, 2 * F), D ** -0.5),
        'ffn_w_out': normal((DEPTH, F, D), F ** -0.5),
        'gla_w_in': normal((N_GLA, D, GLA_IN), D ** -0.5),
        'gla_w_gate': normal((N_GLA, 2, GLA_RANK, GLA_QK), GLA_RANK ** -0.5),
        'gla_b_gate': normal((N_GLA, 2, GLA_QK), 0.1),
        'gla_norm_g': gain((N_GLA, GLA_DV)),
        'gla_w_out': normal((N_GLA, GLA_VD, D), GLA_VD ** -0.5),
        'hy_w_in': normal((N_HY, D, 3 * D), D ** -0.5),
        'hy_conv_w': normal((N_HY, HY_SHORT, 3 * D), HY_SHORT ** -0.5),
        'hy_conv_b': normal((N_HY, 3 * D), 0.01),
        'hy_f_w1': normal((N_HY, HY_EMB, HY_FILTER_DIM), HY_EMB ** -0.5),
        'hy_f_b1': normal((N_HY, HY_FILTER_DIM), 0.1),
        'hy_f_w2': normal((N_HY, HY_FILTER_DIM, HY_FILTER_DIM), HY_FILTER_DIM ** -0.5),
        'hy_f_b2': normal((N_HY, HY_FILTER_DIM), 0.1),
        'hy_f_w3': normal((N_HY, HY_FILTER_DIM, 2 * D), HY_FILTER_DIM ** -0.5),
        'hy_f_freq': gain((N_HY, HY_FILTER_DIM)),
        'hy_f_bias': normal((N_HY, D), 0.1),
        'hy_w_out': normal((N_HY, D, D), D ** -0.5),
        'ml_w_in': normal((N_ML, D, 2 * ML_INNER), D ** -0.5),
        'ml_conv_w': normal((N_ML, ML_CONV, ML_INNER), ML_CONV ** -0.5),
        'ml_conv_b': normal((N_ML, ML_INNER), 0.01),
        'ml_w_q': normal((N_ML, ML_NBLOCKS, ML_BLOCK, ML_BLOCK), ML_BLOCK ** -0.5),
        'ml_w_k': normal((N_ML, ML_NBLOCKS, ML_BLOCK, ML_BLOCK), ML_BLOCK ** -0.5),
        'ml_w_v': normal((N_ML, ML_NBLOCKS, ML_BLOCK, ML_BLOCK), ML_BLOCK ** -0.5),
        'ml_w_gates': normal((N_ML, 2, 3 * ML_INNER, 2 * ML_HEADS), (3 * ML_INNER) ** -0.5),
        'ml_b_gates': jnp.concatenate([ml_b_i, ml_b_f], axis=-1),
        'ml_norm_g': gain((N_ML, ML_INNER)),
        'ml_skip': gain((N_ML, ML_INNER)),
        'ml_w_out': normal((N_ML, ML_INNER, D), ML_INNER ** -0.5),
        's5_lam_re': -0.5 + normal((N_S5, 2, S5_GROUPS, S5_STATE), 0.01),
        's5_lam_im': lam_im_init + normal((N_S5, 2, S5_GROUPS, S5_STATE), 0.01),
        's5_log_dt': jax.random.uniform(next(keys), (N_S5, 2, S5_GROUPS), f32,
                                        minval=math.log(S5_DT_MIN), maxval=math.log(S5_DT_MAX)),
        's5_b_re': normal((N_S5, S5_GROUPS, S5_STATE, S5_GROUP), (2 * S5_GROUP) ** -0.5),
        's5_b_im': normal((N_S5, S5_GROUPS, S5_STATE, S5_GROUP), (2 * S5_GROUP) ** -0.5),
        's5_c_re': normal((N_S5, S5_GROUPS, S5_GROUP, S5_STATE), (2 * S5_STATE) ** -0.5),
        's5_c_im': normal((N_S5, S5_GROUPS, S5_GROUP, S5_STATE), (2 * S5_STATE) ** -0.5),
        's5_d': normal((N_S5, D)),
        's5_w_glu': normal((N_S5, D, 2 * D), D ** -0.5),
    }

def first_block(x, c, ctx, c_ctx, mod_w, mod_b, norm_g, ffn_w_in, ffn_w_out,
              gla_w_in, gla_w_gate, gla_b_gate, gla_norm_g, gla_w_out,
              hy_w_in, hy_conv_w, hy_conv_b, hy_f_w1, hy_f_b1, hy_f_w2, hy_f_b2, hy_f_w3, hy_f_freq, hy_f_bias,
              hy_w_out,
              ml_w_in, ml_conv_w, ml_conv_b, ml_w_q, ml_w_k, ml_w_v, ml_w_gates, ml_b_gates, ml_norm_g, ml_skip,
              ml_w_out,
              s5_lam_re, s5_lam_im, s5_log_dt, s5_b_re, s5_b_im, s5_c_re, s5_c_im, s5_d, s5_w_glu):
    bsz = x.shape[0]
    rows = x.shape[1] // GRID_W
    lat, cx = x, ctx
    silu_c = jax.nn.silu(c.astype(jnp.float32))
    silu_cc = jax.nn.silu(c_ctx.astype(jnp.float32))
    for i in range(DEPTH):
        kind, j = i % N_MIXERS, i // N_MIXERS
        last = i == DEPTH - 1
        mod_l = (silu_c @ mod_w[i] + mod_b[i]).reshape(bsz, N_MOD, 1, D_MODEL)
        mod_c = (silu_cc @ mod_w[i] + mod_b[i]).reshape(N_MOD, 1, D_MODEL)
        h_lat = modulate(rms_norm(lat, norm_g[i, 0]), mod_l[:, 0], mod_l[:, 1])
        h_ctx = modulate(rms_norm(cx, norm_g[i, 0]), mod_c[0], mod_c[1])
        if kind == 0:
            y_lat, y_ctx = gla_mixer(h_lat, h_ctx, gla_w_in[j], gla_w_gate[j], gla_b_gate[j], gla_norm_g[j],
                                     gla_w_out[j])
        elif kind == 1:
            y_lat, y_ctx = hyena_mixer(h_lat, h_ctx, hy_w_in[j], hy_conv_w[j], hy_conv_b[j], hy_f_w1[j],
                                       hy_f_b1[j], hy_f_w2[j], hy_f_b2[j], hy_f_w3[j], hy_f_freq[j],
                                       hy_f_bias[j], hy_w_out[j])
        elif kind == 2:
            y_lat, y_ctx = mlstm_mixer(to_col_major(h_lat, rows), h_ctx, ml_w_in[j], ml_conv_w[j], ml_conv_b[j],
                                       ml_w_q[j], ml_w_k[j], ml_w_v[j], ml_w_gates[j], ml_b_gates[j],
                                       ml_norm_g[j], ml_skip[j], ml_w_out[j])
            y_lat = from_col_major(y_lat, rows)
        else:
            y_lat, y_ctx = s5_mixer(to_col_major(h_lat, rows), h_ctx, s5_lam_re[j], s5_lam_im[j], s5_log_dt[j],
                                    s5_b_re[j], s5_b_im[j], s5_c_re[j], s5_c_im[j], s5_d[j], s5_w_glu[j])
            y_lat = from_col_major(y_lat, rows)
        lat = lat + (mod_l[:, 2] * rms_norm(y_lat, norm_g[i, 1])).astype(lat.dtype)
        h = modulate(rms_norm(lat, norm_g[i, 2]), mod_l[:, 3], mod_l[:, 4])
        lat = lat + (mod_l[:, 5] * rms_norm(swiglu(h, ffn_w_in[i], ffn_w_out[i]), norm_g[i, 3])).astype(lat.dtype)
        if not last:
            cx = cx + (mod_c[2] * rms_norm(y_ctx, norm_g[i, 1])).astype(cx.dtype)
            hc = modulate(rms_norm(cx, norm_g[i, 2]), mod_c[3], mod_c[4])
            cx = cx + (mod_c[5] * rms_norm(swiglu(hc, ffn_w_in[i], ffn_w_out[i]), norm_g[i, 3])).astype(cx.dtype)
    return lat


CHUNK = 64
A_HEADS = 8
A_DK = 128
A_DV = 128
A_CONV = 4
A_W = A_HEADS * A_DV
B_HEADS = 16
B_DH = 64
B_W = B_HEADS * B_DH
B_PREV_CHUNKS = 8
B_MAX_REL = 256
B_REL_SIZE = CHUNK - 1 + B_MAX_REL + 1
D_FF = 2816
FFN_CONV = 3
N_BRANCHES = 2
IN_SPLITS = (3 * A_W, 4 * A_W, 4 * A_W + A_HEADS, 4 * A_W + 2 * A_HEADS,
             4 * A_W + 2 * A_HEADS + B_W, 4 * A_W + 2 * A_HEADS + 2 * B_W,
             4 * A_W + 2 * A_HEADS + 3 * B_W)
IN_COLS = 4 * A_W + 2 * A_HEADS + 3 * B_W + N_BRANCHES * D_MODEL
DEEPNORM_ALPHA = (2.0 * DEPTH) ** 0.25
DEEPNORM_BETA = (8.0 * DEPTH) ** -0.25
LN_EPS = 1e-5
RMS_EPS = 1e-6
L2_EPS = 1e-6
NEG_INF = -1e30


def layernorm(x, g, b):
    xf = x.astype(jnp.float32)
    mu = jnp.mean(xf, axis=-1, keepdims=True)
    var = jnp.mean(jnp.square(xf - mu), axis=-1, keepdims=True)
    y = (xf - mu) * lax.rsqrt(var + LN_EPS) * g.astype(jnp.float32) + b.astype(jnp.float32)
    return y.astype(x.dtype)

def causal_dwconv(x, w):
    k_width, ch = w.shape
    return lax.conv_general_dilated(
        x, w[:, None, :].astype(x.dtype), window_strides=(1,), padding=[(k_width - 1, 0)],
        dimension_numbers=("NWC", "WIO", "NWC"), feature_group_count=ch)

def l2norm(x):
    return x * lax.rsqrt(jnp.sum(jnp.square(x), axis=-1, keepdims=True) + L2_EPS)

def chunk_gated_delta_rule(q, k, v, g, beta):
    b_, s_, h_, dk = q.shape
    dv = v.shape[-1]
    n_chunks = s_ // CHUNK

    def to_chunks(t):
        return t.reshape(b_, n_chunks, CHUNK, h_, -1).transpose(0, 1, 3, 2, 4)

    q, k, v = to_chunks(q), to_chunks(k), to_chunks(v)
    g = g.reshape(b_, n_chunks, CHUNK, h_).transpose(0, 1, 3, 2)
    beta = beta.reshape(b_, n_chunks, CHUNK, h_).transpose(0, 1, 3, 2)
    g = jnp.cumsum(g, axis=-1)

    causal = jnp.tril(jnp.ones((CHUNK, CHUNK), dtype=bool))
    strict = jnp.tril(jnp.ones((CHUNK, CHUNK), dtype=bool), k=-1)
    diff = g[..., :, None] - g[..., None, :]
    decay = jnp.where(causal, jnp.exp(jnp.where(causal, diff, 0.0)), 0.0)

    k_beta = k * beta[..., None]
    v_beta = v * beta[..., None]
    a_low = jnp.where(strict, jnp.einsum("bnhid,bnhjd->bnhij", k_beta, k) * decay, 0.0)
    eye = jnp.eye(CHUNK, dtype=jnp.float32)
    rhs = jnp.concatenate([v_beta, k_beta * jnp.exp(g)[..., None]], axis=-1)
    sol = lax.linalg.triangular_solve(a_low + eye, rhs, left_side=True, lower=True,
                                      unit_diagonal=True)
    u = sol[..., :dv]
    w = sol[..., dv:]
    qk = jnp.where(causal, jnp.einsum("bnhid,bnhjd->bnhij", q, k) * decay, 0.0)

    def step(state, inp):
        q_n, k_n, u_n, w_n, qk_n, g_n = inp
        v_new = u_n - jnp.einsum("bhck,bhkv->bhcv", w_n, state)
        o_n = (jnp.einsum("bhck,bhkv->bhcv", q_n * jnp.exp(g_n)[..., None], state)
               + jnp.einsum("bhij,bhjv->bhiv", qk_n, v_new))
        g_last = g_n[..., -1]
        k_dec = k_n * jnp.exp(g_last[..., None] - g_n)[..., None]
        state = state * jnp.exp(g_last)[..., None, None] + jnp.einsum("bhck,bhcv->bhkv", k_dec, v_new)
        return state, o_n

    xs = tuple(jnp.moveaxis(t, 1, 0) for t in (q, k, u, w, qk, g))
    state0 = jnp.zeros((b_, h_, dk, dv), jnp.float32)
    _, o = lax.scan(step, state0, xs)
    return o.transpose(1, 0, 3, 2, 4).reshape(b_, s_, h_, dv)

def gated_deltanet(qkv, z, beta_raw, a_raw, conv_w, a_log, dt_bias, norm_w):
    b_, s_, _ = qkv.shape
    qkv = jax.nn.silu(causal_dwconv(qkv, conv_w))
    q, k, v = jnp.split(qkv.astype(jnp.float32), 3, axis=-1)
    q = l2norm(q.reshape(b_, s_, A_HEADS, A_DK)) * (A_DK ** -0.5)
    k = l2norm(k.reshape(b_, s_, A_HEADS, A_DK))
    v = v.reshape(b_, s_, A_HEADS, A_DV)
    beta = jax.nn.sigmoid(beta_raw.astype(jnp.float32))
    g = -jnp.exp(a_log.astype(jnp.float32)) * jax.nn.softplus(
        a_raw.astype(jnp.float32) + dt_bias.astype(jnp.float32))
    o = chunk_gated_delta_rule(q, k, v, g, beta)
    o = o * lax.rsqrt(jnp.mean(jnp.square(o), axis=-1, keepdims=True) + RMS_EPS)
    o = o * norm_w.astype(jnp.float32) * jax.nn.silu(z.astype(jnp.float32).reshape(b_, s_, A_HEADS, A_DV))
    return o.reshape(b_, s_, A_W).astype(qkv.dtype)

def chunk_band_attention(q, k, v, rel_bias):
    b_, s_, h_, dh = q.shape
    n_chunks = s_ // CHUNK
    pad = B_PREV_CHUNKS * CHUNK
    band = (B_PREV_CHUNKS + 1) * CHUNK
    k_pad = jnp.pad(k, ((0, 0), (pad, 0), (0, 0), (0, 0)))
    v_pad = jnp.pad(v, ((0, 0), (pad, 0), (0, 0), (0, 0)))
    qi = np.arange(CHUNK)[:, None]
    kj = np.arange(band)[None, :]
    dist = pad + qi - kj
    idx = np.clip(dist, -(CHUNK - 1), B_MAX_REL) + (CHUNK - 1)
    bias = rel_bias.astype(jnp.float32)[:, idx]
    key_chunk = jnp.arange(band) // CHUNK
    scale = dh ** -0.5

    def one_chunk(n):
        q_n = lax.dynamic_slice_in_dim(q, n * CHUNK, CHUNK, axis=1)
        k_n = lax.dynamic_slice_in_dim(k_pad, n * CHUNK, band, axis=1)
        v_n = lax.dynamic_slice_in_dim(v_pad, n * CHUNK, band, axis=1)
        valid = (n - B_PREV_CHUNKS + key_chunk) >= 0
        s = jnp.einsum("bqhd,bkhd->bhqk", q_n, k_n).astype(jnp.float32) * scale + bias
        s = jnp.where(valid, s, NEG_INF)
        p = jax.nn.softmax(s, axis=-1).astype(v.dtype)
        return jnp.einsum("bhqk,bkhd->bqhd", p, v_n)

    out = lax.map(one_chunk, jnp.arange(n_chunks))
    return out.transpose(1, 0, 2, 3, 4).reshape(b_, s_, h_ * dh)

def second_inputs(seed: int = 0) -> dict:
    key = jax.random.key(seed)
    ks = jax.random.split(key, 24)

    def nrm(k, shape, scale):
        return jax.random.normal(k, shape, jnp.float32) * scale

    L = DEPTH
    x = nrm(ks[0], (BATCH, SEQ, D_MODEL), 1.0)
    c = nrm(ks[1], (BATCH, D_MODEL), 1.0)
    w_ada = nrm(ks[2], (L, D_MODEL, 6 * D_MODEL), D_MODEL ** -0.5)
    b_ada = nrm(ks[3], (L, 6 * D_MODEL), 0.02)
    w_in = nrm(ks[4], (L, D_MODEL, IN_COLS), D_MODEL ** -0.5)
    b_gate = nrm(ks[5], (L, N_BRANCHES * D_MODEL), 0.1)
    conv_a = nrm(ks[6], (L, A_CONV, 3 * A_W), A_CONV ** -0.5)
    a_log = jnp.log(jax.random.uniform(ks[7], (L, A_HEADS), jnp.float32, minval=1.0, maxval=16.0))
    dt = jnp.exp(jax.random.uniform(ks[8], (L, A_HEADS), jnp.float32,
                                    minval=math.log(1e-3), maxval=math.log(1e-1)))
    dt_bias = dt + jnp.log(-jnp.expm1(-dt))
    norm_a = 1.0 + nrm(ks[9], (L, A_DV), 0.05)
    rel_bias = nrm(ks[10], (L, B_HEADS, B_REL_SIZE), 0.2)
    w_branch_a = nrm(ks[11], (L, A_W, D_MODEL), A_W ** -0.5)
    w_branch_b = nrm(ks[12], (L, B_W, D_MODEL), B_W ** -0.5)
    w_o = nrm(ks[13], (L, D_MODEL, D_MODEL), DEEPNORM_BETA * D_MODEL ** -0.5)
    ln1_g = 1.0 + nrm(ks[14], (L, D_MODEL), 0.05)
    ln1_b = nrm(ks[15], (L, D_MODEL), 0.02)
    w_up = nrm(ks[16], (L, D_MODEL, 2 * D_FF), D_MODEL ** -0.5)
    conv_ffn = nrm(ks[17], (L, FFN_CONV, 2 * D_FF), FFN_CONV ** -0.5)
    b_conv_ffn = nrm(ks[18], (L, 2 * D_FF), 0.02)
    w_down = nrm(ks[19], (L, D_FF, D_MODEL), DEEPNORM_BETA * D_FF ** -0.5)
    ln2_g = 1.0 + nrm(ks[20], (L, D_MODEL), 0.05)
    ln2_b = nrm(ks[21], (L, D_MODEL), 0.02)
    return {"x": x, "c": c, "w_ada": w_ada, "b_ada": b_ada, "w_in": w_in, "b_gate": b_gate,
            "conv_a": conv_a, "a_log": a_log, "dt_bias": dt_bias, "norm_a": norm_a,
            "rel_bias": rel_bias, "w_branch_a": w_branch_a, "w_branch_b": w_branch_b, "w_o": w_o,
            "ln1_g": ln1_g, "ln1_b": ln1_b, "w_up": w_up, "conv_ffn": conv_ffn,
            "b_conv_ffn": b_conv_ffn, "w_down": w_down, "ln2_g": ln2_g, "ln2_b": ln2_b}

def second_block(x, c, w_ada, b_ada, w_in, b_gate, conv_a, a_log, dt_bias, norm_a, rel_bias,
              w_branch_a, w_branch_b, w_o, ln1_g, ln1_b, w_up, conv_ffn, b_conv_ffn, w_down,
              ln2_g, ln2_b):
    b_, s_, d_ = x.shape
    c_act = jax.nn.silu(c)
    for l in range(DEPTH):
        mod = (c_act @ w_ada[l] + b_ada[l])[:, None, :]
        shift_t, scale_t, gate_t, shift_f, scale_f, gate_f = jnp.split(mod, 6, axis=-1)

        h = x * (1.0 + scale_t) + shift_t
        proj = h @ w_in[l]
        qkv_a, z_a, beta_raw, a_raw, q_b, k_b, v_b, gates = jnp.split(proj, IN_SPLITS, axis=-1)

        o_a = gated_deltanet(qkv_a, z_a, beta_raw, a_raw, conv_a[l], a_log[l], dt_bias[l], norm_a[l])
        o_b = chunk_band_attention(q_b.reshape(b_, s_, B_HEADS, B_DH),
                                   k_b.reshape(b_, s_, B_HEADS, B_DH),
                                   v_b.reshape(b_, s_, B_HEADS, B_DH), rel_bias[l])

        gate_a, gate_b = jnp.split(jax.nn.sigmoid(gates + b_gate[l]), N_BRANCHES, axis=-1)
        merged = gate_a * (o_a @ w_branch_a[l]) + gate_b * (o_b @ w_branch_b[l])
        mix = merged @ w_o[l]
        x = layernorm(DEEPNORM_ALPHA * x + gate_t * mix, ln1_g[l], ln1_b[l])

        h = x * (1.0 + scale_f) + shift_f
        u = causal_dwconv(h @ w_up[l], conv_ffn[l]) + b_conv_ffn[l]
        u_gate, u_val = jnp.split(u, 2, axis=-1)
        ffn = (jax.nn.silu(u_gate) * u_val) @ w_down[l]
        x = layernorm(DEEPNORM_ALPHA * x + gate_f * ffn, ln2_g[l], ln2_b[l])
    return x


def setup_inputs(seed=0):
    out = dict(first_inputs(seed))
    for name, value in second_inputs(seed + 1).items():
        if name != "x":
            out[name + "_2"] = value
    return out


def reference(
    x, c, ctx, c_ctx, mod_w, mod_b, norm_g, ffn_w_in, ffn_w_out, gla_w_in, gla_w_gate,
    gla_b_gate, gla_norm_g, gla_w_out, hy_w_in, hy_conv_w, hy_conv_b, hy_f_w1, hy_f_b1, hy_f_w2,
    hy_f_b2, hy_f_w3, hy_f_freq, hy_f_bias, hy_w_out, ml_w_in, ml_conv_w, ml_conv_b, ml_w_q,
    ml_w_k, ml_w_v, ml_w_gates, ml_b_gates, ml_norm_g, ml_skip, ml_w_out, s5_lam_re, s5_lam_im,
    s5_log_dt, s5_b_re, s5_b_im, s5_c_re, s5_c_im, s5_d, s5_w_glu, c_2, w_ada_2, b_ada_2,
    w_in_2, b_gate_2, conv_a_2, a_log_2, dt_bias_2, norm_a_2, rel_bias_2, w_branch_a_2,
    w_branch_b_2, w_o_2, ln1_g_2, ln1_b_2, w_up_2, conv_ffn_2, b_conv_ffn_2, w_down_2, ln2_g_2,
    ln2_b_2,
):
    x = first_block(
        x, c, ctx, c_ctx, mod_w, mod_b, norm_g, ffn_w_in, ffn_w_out, gla_w_in, gla_w_gate,
        gla_b_gate, gla_norm_g, gla_w_out, hy_w_in, hy_conv_w, hy_conv_b, hy_f_w1, hy_f_b1,
        hy_f_w2, hy_f_b2, hy_f_w3, hy_f_freq, hy_f_bias, hy_w_out, ml_w_in, ml_conv_w,
        ml_conv_b, ml_w_q, ml_w_k, ml_w_v, ml_w_gates, ml_b_gates, ml_norm_g, ml_skip, ml_w_out,
        s5_lam_re, s5_lam_im, s5_log_dt, s5_b_re, s5_b_im, s5_c_re, s5_c_im, s5_d, s5_w_glu,
    )
    return second_block(
        x, c_2, w_ada_2, b_ada_2, w_in_2, b_gate_2, conv_a_2, a_log_2, dt_bias_2, norm_a_2,
        rel_bias_2, w_branch_a_2, w_branch_b_2, w_o_2, ln1_g_2, ln1_b_2, w_up_2, conv_ffn_2,
        b_conv_ffn_2, w_down_2, ln2_g_2, ln2_b_2,
    )


_drawn_inputs = setup_inputs


def setup_inputs(seed=0):
    import zlib

    import numpy as np

    out = dict(_drawn_inputs(seed))
    spreads = {}
    factors = {'gla_norm_g': 5.529,
     'b_ada_2': 3.086,
     'b_gate_2': 8.0,
     'a_log_2': 5.908,
     'norm_a_2': 8.0,
     'rel_bias_2': 5.005,
     'ln1_b_2': 2.781,
     'b_conv_ffn_2': 7.932,
     'ln2_b_2': 2.849}
    for name, (base, spread) in spreads.items():
        noise = np.random.default_rng([zlib.crc32(name.encode()), seed]).standard_normal(out[name].shape)
        drawn = base * np.exp(spread * noise) if base else spread * noise
        out[name] = jnp.asarray(drawn.astype(out[name].dtype))
    for name, factor in factors.items():
        out[name] = (out[name] * factor).astype(out[name].dtype)
    return out
```

```python
from contextlib import ExitStack

import concourse.bass as bass
from concourse import mybir
import numpy as np

F32 = mybir.dt.float32
F32R = mybir.dt.float32r
I32 = mybir.dt.int32
ALU = mybir.AluOpType
ACT = mybir.ActivationFunctionType
AX_X = mybir.AxisListType.X

P = 128
D = 1024
KT = D // P
T = 256
CHUNK = 64
NCH = T // CHUNK
FFN = 2816
FT = FFN // P
GH, GDK, GDV = 4, 128, 256
DH, DDK = 8, 128
BH, BDH = 16, 64
REL = 320
EPS_RMS, EPS_LN = 1e-6, 1e-5
ALPHA = 2.0 ** 0.25
NEG = -1e30
RAW, PARTS, TURNS = 3, 2, 4

LAYERS = [("mod_first", "matvec", 8), ("gla_k", "split", 2), ("gla_v", "split", 4), ("gla_q", "split", 2),
          ("gla_r", "split", 4), ("mod_rest", "matvec", 16), ("gla_out", "split", 4), ("ffn_in", "both", 22),
          ("ada_tail", "matvec", 2), ("ffn_out", "split", 11), ("qkv", "split", 12), ("z", "split", 4),
          ("band_q", "split", 4), ("band_k", "split", 4), ("band_v", "split", 4), ("gates", "split", 8),
          ("branch_a", "split", 4), ("branch_b", "split", 4), ("mix", "split", 4), ("up", "split", 22),
          ("down", "split", 11)]


def plan_stream():
    stream, first = [], {}
    split = matvec = turn = 0
    for layer, kind, count in LAYERS:
        first[layer] = (split, matvec, turn)
        for _ in range(count):
            if kind in ("split", "both"):
                stream.append(("split", split))
                split += 1
            if kind in ("matvec", "both"):
                stream.append(("matvec", matvec))
                matvec += 1
        if kind in ("split", "both"):
            turn += {"gla_k": 2 * count, "gla_v": 2 * count, "ffn_out": 4, "down": 4}.get(layer, count)
    return stream, first


COLUMNS = [("c", 8), ("c_ctx", 8), ("c_2", 8), ("mod_b", 48), ("norm_g", 32), ("gla_b_gate", 8), ("gla_norm_g", 2),
           ("b_ada_2", 48), ("b_gate_2", 16), ("conv_a_2", 96), ("norm_a_2", 1), ("ln1_g_2", 8), ("ln1_b_2", 8),
           ("ln2_g_2", 8), ("ln2_b_2", 8), ("conv_ffn_2", 132), ("b_conv_ffn_2", 44)]
COL, NCOL = {}, 0
for _name, _n in COLUMNS:
    COL[_name] = NCOL
    NCOL += _n


CONSTANTS = 34
N_SPLIT = sum(count for _, kind, count in LAYERS if kind != "matvec")

SOLVE_COUNTS = {"at_ready": 1, "solve_masked": 1, "solve_copied": 9, "tt_ready": 5}
SOLVE_WAITS = [
    [("at_ready", 1)],
    [("solve_masked", 1)],
    [("solve_masked", 1)],
    [("solve_copied", 1)],
    [("solve_copied", 2)],
    [("tt_ready", 1)],
    [("solve_copied", 3), ("tt_ready", 1)],
    [("solve_copied", 4)],
    [("solve_copied", 5), ("tt_ready", 2)],
    [("tt_ready", 3)],
    [("tt_ready", 3)],
    [("solve_copied", 7)],
    [("tt_ready", 4)],
    [("tt_ready", 4)],
    [("solve_copied", 9)],
]


def two_blocks(nc, panels, x, ctx_x, columns, w_glr, w_gate, w_beta_a, head_rows, rel_bias, out):
    stream, first = plan_stream()
    place = {entry: n for n, entry in enumerate(stream)}

    with ExitStack() as ctx:
        def sb(name, shape, dt=F32, scope=ctx):
            return scope.enter_context(nc.sbuf_tensor(name, shape, dt))

        signals = {}

        def S(name):
            if name not in signals:
                signals[name] = ctx.enter_context(nc.semaphore(name))
            return signals[name]

        PB = ctx.enter_context(nc.psum_tensor("panel_banks", [P, TURNS, 512], F32))
        MB = ctx.enter_context(nc.psum_tensor("work_banks", [P, 4, 512], F32))

        raw = sb("raw", [P, RAW, 2048])
        whi = sb("w_hi", [P, PARTS, 2048], F32R)
        wlo = sb("w_lo", [P, PARTS, 2048], F32R)
        hhi = sb("act_hi", [P, 16, T], F32R)
        hlo = sb("act_lo", [P, 16, T], F32R)
        xt = sb("x_t", [P, KT, T])
        cols = sb("columns", [P, NCOL])
        ident = sb("ident", [P, P])
        ones = sb("ones", [P, P])
        ones_row = sb("ones_row", [P, T])
        mask_up = sb("mask_up", [P, P], I32)
        mask_dn = sb("mask_dn", [P, P], I32)
        causal_t = sb("causal_t", [P, P])
        causal_dn = sb("causal_dn", [P, P])
        m16t = sb("m16t", [P, P])
        m16 = sb("m16", [P, P])
        d32 = sb("d32", [P, P])
        d64 = sb("d64", [P, P])
        modc = sb("mod_cols", [P, 48, 2])
        mod2 = sb("mod2_cols", [P, 48])
        cact = sb("c_act", [P, 3, 8])
        sc_a = sb("scale_a", [P, 2, 8])
        gcol = sb("gate_cols", [P, 8])
        rs = sb("rs", [P, 512])
        eps = sb("eps", [P, 4])
        dec = sb("g_decay", [P, 8, NCH])
        gl_tok = sb("tok_cols", [P, 3, 2, DH])
        gl_end = sb("end_decay", [P, DH, NCH])
        w_ba = sb("w_beta_a", [P, KT, 16])
        hrow = sb("head_rows", [DH, 2])

        def col(name, i=0, n=1):
            return cols[:, COL[name] + i:COL[name] + i + n]

        def arena(name, size, scope):
            tensor, at = sb(name, [P, size], F32, scope), [0]

            def take(*shape, at_=None):
                n = int(np.prod(shape))
                start = at[0] if at_ is None else at_
                if at_ is None:
                    at[0] += n
                assert start + n <= size, (name, start + n, size)
                names = "abcd"[:len(shape)]
                view = tensor[:, start:start + n]
                if len(shape) > 1:
                    view = view.rearrange(f"p ({' '.join(names)}) -> p {' '.join(names)}",
                                          **{k: v for k, v in zip(names, shape)})
                return view
            take.at = at
            return take

        WORK = 25600
        with ExitStack() as scope:
            take = arena("gla_work", WORK, scope)
            g_q = take(GH, T)
            g_k = take(GH, 2 * T)
            g_v = take(4, D)
            g_r = take(KT, T)
            g_x = take(8, 2 * T)
            g_kt = take(4, 8, P, at_=take.at[0] - 4096)
            e_at = take.at[0]
            g_e1 = take(8, T)
            g_e2 = take(8, T)
            g_e3 = take(8, 2 * T)
            s_at = take.at[0]
            g_s = take(8, GDV)
            g_sc = take(16, P)
            g_o = take(GH, 2, T, at_=s_at)
            wgp = take(8 * P, at_=e_at)[0:32, :]
            glr = take(2 * T, at_=e_at + 1024)[0:32, :]
            wgl = take(KT, 32, at_=e_at + 1536)
            xc = take(KT, T, at_=e_at + 2048)
            sq1 = take(KT, 2 * T, at_=e_at + 4096)
            h1 = take(KT, 2 * T, at_=s_at)
            g_sq = take(GH, 2, T, at_=e_at + 2048)
            g_rs = take(GH, T, at_=e_at + 4096)
            assert s_at + 4096 <= WORK
        with ExitStack() as scope:
            fhi = sb("hidden_hi", [P, FT, T], F32R, scope)
            flo = sb("hidden_lo", [P, FT, T], F32R, scope)
            take = arena("ffn_work", 14000, scope)
            y1 = take(KT, T)
            sq2 = take(KT, T)
            h2 = take(KT, T)
            f_s = take(2, T)
            f_g = take(2, T)
            y3 = take(KT, T)
            f_u = take(2, 2, T)
            f_out = take(KT, T)
        with ExitStack() as scope:
            take = arena("mix_work", WORK, scope)
            m_at = take.at[0]
            qkv = take(24, T)
            zs = take(KT, T)
            kb = take(DH, T)
            eg = take(DH, T)
            vb = take(2, D)
            kd = take(2, D)
            dm = kd.rearrange("p a (b c) -> p (a b) c", c=P)
            rs2 = vb.rearrange("p a b -> p (a b)")
            qkt = take(16, P)
            tt_ = take(16, P)
            t_at = take.at[0]
            s_n, s_nt, s_b32, s_b64, s_u = (take(8, P) for _ in range(5))
            s_t = s_nt
            sq3 = take(16, T, at_=t_at)
            h3 = take(KT, T, at_=m_at + 10240)
            cy = take(2, 2, T, at_=m_at + 12288)
            st = take(DH, P, at_=t_at)
            rr = take(D, at_=t_at + 1024)
            vn = take(D, at_=t_at + 2048)
            sel = take(DH, P, at_=t_at)[0:DH]
            hm = take(8, T, at_=m_at + 16384)[0:DH]
            vt_ = qkv[:, 16:24, :]
            od = take(DH, T, at_=m_at + 4096)
            odq = take(DH, T, at_=m_at)
            bq = take(KT, T, at_=m_at)
            bk = take(KT, T, at_=m_at + 2048)
            bv = take(2, D, at_=m_at + 4096)
            bx = take(BH, T, at_=m_at + 8192)
            bp = take(2, 384, at_=m_at + 12288)
            bpt = take(2, 384, at_=m_at + 13056)
            bst = take(2, 8, at_=m_at + 13824)
            ga = take(16, T, at_=m_at + 14336)
            ya = take(KT, T, at_=m_at + 18432)
            yb = take(KT, T, at_=m_at + 20480)
            ob = take(KT, T, at_=m_at + 22528)

        block = ctx.enter_context(nc.Block())

        @block.sync
        def _(sp):
            for n in range(len(stream)):
                if n >= RAW:
                    kind, i = stream[n - RAW]
                    sp.wait_ge(S("parts_ready" if kind == "split" else "matvec_done"), i + 1)
                sp.dma_start(raw[:, n % RAW], panels[n]).then_inc(S(f"landed{n % RAW}"), 16)
            sp.wait_ge(S("out_ready"), 1)
            sp.dma_start(out, f_out).then_inc(S("out_stored"), 16)
            sp.wait_ge(S("out_stored"), 16)

        @block.gpsimd
        def _(pool):
            made = [0]

            def step(ins):
                made[0] += 1
                ins.then_inc(S("constants"), 1)
                pool.wait_ge(S("constants"), made[0])

            def keep(t, compare, base, pattern, cm, fill=0.0):
                step(pool.affine_select(out=t, in_=t, compare_op=compare, fill=fill, base=base,
                                        pattern=pattern, channel_multiplier=cm))

            def same_block(t, size):
                v = t.rearrange("p (b c) -> p b c", c=size)
                keep(v, ALU.is_ge, 0, [[-size, P // size], [0, size]], 1)
                keep(v, ALU.is_ge, size - 1, [[size, P // size], [0, size]], -1)

            step(pool.memset(ones[:], 1.0))
            step(pool.memset(ones_row[:], 1.0))
            step(pool.memset(ident[:], 0.0))
            keep(ident[:], ALU.not_equal, 0, [[-1, P]], 1, 1.0)
            for t, base, pattern, cm, size in (
                    (causal_t, 0, [[1, P]], -1, 64), (causal_dn, 0, [[-1, P]], 1, 64), (m16t, -1, [[1, P]], -1, 16), (m16, -1, [[-1, P]], 1, 16),
                    (d32, 0, None, 0, 32), (d64, 0, None, 0, 64)):
                step(pool.memset(t[:], 1.0))
                same_block(t[:], size)
                if pattern:
                    keep(t[:], ALU.is_ge, base, pattern, cm)
                else:
                    v = t[:].rearrange("p (b c) -> p b c", c=size)
                    keep(v, ALU.is_ge, -(size // 2), [[-size, P // size], [0, size]], 1)
                    keep(v, ALU.is_ge, size // 2 - 1, [[0, P // size], [-1, size]], 0)
            step(pool.memset(eps[:, 0:1], EPS_RMS))
            step(pool.memset(eps[:, 1:2], EPS_LN))
            step(pool.memset(eps[:, 2:3], 1.0))
            step(pool.memset(wgp, 0.0))
            assert made[0] == CONSTANTS, made[0]
            for d in range(2):
                pool.dma_start(wgp[16 * d:16 * d + 16, 512 * d:512 * d + 512], w_gate[d])\
                    .then_inc(S("gate_w_landed"), 16)
            pool.wait_ge(S("h1_lo"), 1)
            pool.wait_ge(S("glr_sum"), 1)
            pool.memset(g_sc, 0.0).then_inc(S("scores_zeroed"), 1)
            pool.wait_ge(S("qk_sums"), 2)
            pool.memset(sel, 1.0).then_inc(S("selectors"), 1)
            pool.wait_ge(S("selectors"), 1)
            pool.affine_select(out=sel, in_=sel, compare_op=ALU.is_equal, fill=0.0, base=0,
                               pattern=[[-1, DH], [0, P]], channel_multiplier=1).then_inc(S("selectors"), 1)

        @block.tensor
        def _(pe):
            split = [0]
            turn = [0]

            def open_panel(j):
                pe.wait_ge(S("parts_ready"), j + 1)
                return j % PARTS

            def take_turn():
                t = turn[0]
                turn[0] += 1
                if t >= TURNS:
                    pe.wait_ge(S("panel_evacuated"), t - TURNS + 1)
                return t % TURNS

            def three_pass(out_, ks, weights, moving, start=True, stop=True):
                ks = list(ks)
                for n, k in enumerate(ks):
                    (a_hi, a_lo), (b_hi, b_lo) = weights(k), moving(k)
                    for p, (a, b) in enumerate(((a_hi, b_hi), (a_hi, b_lo), (a_lo, b_hi))):
                        ins = pe.matmul(out_, a, b, start=start and n == 0 and p == 0,
                                        stop=stop and n == len(ks) - 1 and p == 2, skip_group_check=True)
                return ins

            def panel(j, x_unit, nf=1):
                s = open_panel(j)
                b = None
                for m in range(2):
                    if nf == 2 or m == 0:
                        b = take_turn()
                    o = PB[:, b, :] if nf == 2 else PB[:, b, m * T:m * T + T]
                    ins = three_pass(
                        o, range(KT),
                        lambda k: tuple(w[:, s, k * 256 + m * P:k * 256 + m * P + P] for w in (whi, wlo)),
                        lambda k: tuple(h[:, x_unit(k):x_unit(k) + nf, :] for h in (hhi, hlo)))
                    if nf == 2 and m == 0:
                        ins.then_inc(S("half_multiplied"), 1)
                ins.then_inc(S("multiplied"), 1)

            def token_panel(j, x_unit, tiles):
                s = open_panel(j)
                for n, (unit, t0) in enumerate(tiles):
                    if n % 2 == 0:
                        b = take_turn()
                    ins = three_pass(
                        PB[:, b, (n % 2) * 256:(n % 2) * 256 + 256], range(KT),
                        lambda k: tuple(h[:, x_unit(k) + unit, t0:t0 + P] for h in (hhi, hlo)),
                        lambda k: tuple(w[:, s, k * 256:k * 256 + 256] for w in (whi, wlo)))
                    if n == 1 and len(tiles) == 4:
                        ins.then_inc(S("half_multiplied"), 1)
                ins.then_inc(S("multiplied"), 1)

            def matvec(a, bank, cvec, n):
                at = place[("matvec", a)]
                pe.wait_ge(S(f"landed{at % RAW}"), 16 * (at // RAW + 1))
                for m in range(2):
                    tile = (2 * a + m) % 48
                    for k in range(KT):
                        ins = pe.matmul(MB[:, bank, tile * n:tile * n + n],
                                        raw[:, at % RAW, k * 256 + m * P:k * 256 + m * P + P], cvec(k),
                                        start=(k == 0), stop=(k == KT - 1))
                ins.then_inc(S("matvec_done"), 1)

            def sum_tiles(out_, tiles, name):
                for n, tile in enumerate(tiles):
                    ins = pe.matmul(out_, ones[:], tile, start=(n == 0), stop=(n == len(tiles) - 1))
                ins.then_inc(S(name), 1)

            both = lambda k: cact[:, 0:2, k]
            pe.wait_ge(S("constants"), CONSTANTS)
            pe.wait_ge(S("squares"), 1)
            sum_tiles(MB[:, 0, :], [sq1[:, k, :] for k in range(KT)], "norm_sum")
            pe.wait_ge(S("c_ready"), 1)
            for a in range(8):
                matvec(a, 1, both, 2)
            pe.wait_ge(S("wgl_landed"), 16)
            pe.wait_ge(S("h1_ready"), 1)
            pe.wait_ge(S("norm_factor"), 1)
            for k in range(KT):
                ins = pe.matmul(MB[0:32, 0, :], wgl[:, k, :], h1[:, k, :], start=(k == 0), stop=(k == KT - 1))
            ins.then_inc(S("glr_sum"), 1)
            pe.wait_ge(S("h1_lo"), 1)
            pair = lambda k: 2 * k
            j = 0
            for _ in range(2):
                panel(j, pair, 2)
                j += 1
            pe.wait_ge(S("gate_w_landed"), 32)
            pe.wait_ge(S("glr_ready"), 1)
            for i in range(8):
                if i >= 4:
                    pe.wait_ge(S("gate_biased"), i - 3)
                pe.matmul(MB[:, i % 4, :], wgp[:, i * P:i * P + P], glr, start=True, stop=True)\
                    .then_inc(S("gate_sum"), 1)
            for _ in range(4):
                token_panel(j, pair, [(0, 0), (0, P), (1, 0), (1, P)])
                j += 1
            for _ in range(6):
                panel(j, pair)
                j += 1
            pe.wait_ge(S("gate_biased"), 8)
            for a in range(8, 24):
                matvec(a, 1, both, 2)
            pe.wait_ge(S("keys_decayed"), 1)
            for d in range(2):
                for t in range(2):
                    if d * 2 + t == 1:
                        pe.wait_ge(S("mod_ready"), 2)
                    for h in range(GH):
                        ins = pe.matmul(MB[:, d * 2 + t, h * P:h * P + P], g_e2[:, d * 4 + h, t * P:t * P + P],
                                        g_e1[:, d * 4 + h, t * P:t * P + P], start=True, stop=True)
                    ins.then_inc(S("scores"), 1)
            pe.wait_ge(S("end_keys"), 1)
            for n in range(8):
                t, half = (2, 3, 0, 1)[n // 2], n % 2
                if n < 4:
                    pe.wait_ge(S("scores_masked"), n + 1)
                else:
                    pe.wait_ge(S("keys_turned"), n - 3)
                for i in range(4):
                    ins = pe.transpose(MB[:, n % 4, i * P:i * P + P],
                                       g_e3[:, half * 4 + i, t * P:t * P + P], ident[:])
                ins.then_inc(S("keys_transposed"), 1)
            pe.wait_ge(S("panel_evacuated"), 18)
            for h in range(GH):
                begun = False
                for t in range(2):
                    for v in range(2):
                        for d in range(2):
                            pe.matmul(PB[:, h, v * T + t * P:v * T + t * P + P],
                                      g_v[:, t, h * GDV + v * P:h * GDV + v * P + P],
                                      g_sc[:, (d * 2 + t) * 4 + h, :], start=not begun, stop=False,
                                      skip_group_check=True)
                            begun = True
            pe.wait_ge(S("keys_turned"), 8)
            for i in range(8):
                for t in (2, 3):
                    ins = pe.matmul(MB[:, i // 2, (i % 2) * 256:(i % 2) * 256 + 256], g_kt[:, t, i, :],
                                    g_v[:, t, (i % 4) * GDV:(i % 4) * GDV + GDV], start=(t == 2), stop=(t == 3))
                ins.then_inc(S("state_sum"), 1)
            for s in range(NCH):
                for i in range(8):
                    d, h = i // 4, i % 4
                    c = s if d == 0 else NCH - 1 - s
                    pe.wait_ge(S("state_new"), 8 * s + i // 2 * 2 + 2)
                    for v in range(2):
                        ins = pe.matmul(PB[:, h, v * T + c * CHUNK:v * T + c * CHUNK + CHUNK],
                                        g_s[:, i, v * P:v * P + P], g_e1[:, i, c * CHUNK:c * CHUNK + CHUNK],
                                        start=False, stop=(s == NCH - 1 and d == 1), skip_group_check=True)
                    if s < NCH - 1:
                        p0 = CHUNK * (c % 2)
                        ins = pe.matmul(MB[:, i // 2, (i % 2) * 256:(i % 2) * 256 + 256],
                                        g_kt[p0:p0 + CHUNK, c // 2, i, :],
                                        g_v[p0:p0 + CHUNK, c // 2, h * GDV:h * GDV + GDV], start=True, stop=True)
                        ins.then_inc(S("state_sum"), 1)
                    else:
                        ins.then_inc(S("gla_done"), 1)
            pe.wait_ge(S("gla_squares"), 1)
            for h in range(GH):
                for v in range(2):
                    ins = pe.matmul(MB[:, h // 2, (h % 2) * T:(h % 2) * T + T], ones[:], g_sq[:, h, v, :],
                                    start=(v == 0), stop=(v == 1))
            ins.then_inc(S("gla_norm_sum"), 1)
            pe.wait_ge(S("gla_lo"), 1)
            single = lambda k: k
            turn[0] = first["gla_out"][2]
            for n in range(4):
                if n == 0:
                    pe.wait_ge(S("gla_read"), 4)
                panel(j, single)
                j += 1

            def norm(count):
                pe.wait_ge(S("squares"), count)
                sum_tiles(MB[:, 0, 0:T], [sq2[:, k, :] for k in range(KT)], "norm_sum")

            norm(2)
            norm(3)
            pe.wait_ge(S("h2_lo"), 1)
            pe.wait_ge(S("c_ready"), 1)
            second_c = lambda k: cact[:, 2, k:k + 1]
            for i in range(22):
                panel(j, single)
                j += 1
                matvec(24 + i, 3, second_c, 1)
            for a in range(46, 48):
                matvec(a, 3, second_c, 1)

            def project_hidden(j, first_turn, name):
                turn[0] = first_turn
                banks = [take_turn() for _ in range(4)]
                for i in range(11):
                    s = open_panel(j)
                    pe.wait_ge(S(name), 2 * i + 2)
                    for kk in range(2):
                        for m in range(KT):
                            f = 2 * i + kk
                            w0 = (kk * KT + m) * P
                            ins = three_pass(
                                PB[:, banks[m // 2], (m % 2) * T:(m % 2) * T + T], [f],
                                lambda k: (whi[:, s, w0:w0 + P], wlo[:, s, w0:w0 + P]),
                                lambda k: (fhi[:, k, :], flo[:, k, :]),
                                start=(f == 0 and m % 2 == 0), stop=(f == FT - 1))
                    ins.then_inc(S("multiplied"), 1)
                    j += 1
                return j

            j = project_hidden(j, first["ffn_out"][2], "hidden_lo")
            norm(4)

            pe.wait_ge(S("h3_ready"), 1)
            pe.wait_ge(S("small_landed"), 32)
            pe.wait_ge(S("norm_factor"), 4)
            for part in range(2):
                for k in range(KT):
                    ins = pe.matmul(MB[0:DH, 0, part * T:part * T + T], w_ba[:, k, part * 8:part * 8 + 8],
                                    h3[:, k, :], start=(k == 0), stop=(k == KT - 1))
            ins.then_inc(S("beta_a_sum"), 1)
            pe.wait_ge(S("h3_lo"), 1)
            for _ in range(16):
                panel(j, single)
                j += 1
            for part in range(2):
                pe.wait_ge(S("qk_squares"), part + 1)
                pe.wait_ge(S("rows_ready"), 1)
                if part:
                    pe.wait_ge(S("qk_factor"), 1)
                for b in range(4):
                    ins = pe.matmul(MB[:, b, :], ones[:], sq3[:, part * 8 + 2 * b:part * 8 + 2 * b + 2, :],
                                    start=True, stop=True)
                ins.then_inc(S("qk_sums"), 1)
            pe.wait_ge(S("selectors"), 2)
            pe.wait_ge(S("rows_ready"), 2)
            pe.wait_ge(S("rows_act"), 3)
            pe.wait_ge(S("qk_factor"), 2)
            for n, row in enumerate((2, 0, 3)):
                for t in range(2):
                    ins = pe.transpose(MB[:, 0, (n * 2 + t) * DH:(n * 2 + t) * DH + DH],
                                       hm[:, row, t * P:t * P + P], ident[0:DH, 0:DH])
            ins.then_inc(S("tok_rows"), 1)
            pe.wait_ge(S("tok_ready"), 1)
            for n, row in enumerate((2, 0)):
                if n:
                    pe.wait_ge(S("decay_diff"), 1)
                    pe.wait_ge(S("eg_ready"), 1)
                for h in range(DH):
                    ins = pe.matmul(MB[:, h // 2, (h % 2) * T:(h % 2) * T + T], sel[:, h, :], hm[:, row, :],
                                    start=True, stop=True)
                ins.then_inc(S("rows_spread"), 1)
            pe.wait_ge(S("kb_ready"), 1)

            steps = [("A", None, s_u), ("N2", s_nt, s_n), ("N2T", s_n, s_nt), ("T2", s_n, None), ("N4", s_nt, s_n),
                     ("N4T", s_n, s_nt), ("T4", s_n, None), ("N8", s_nt, s_n), ("T8", s_n, None),
                     ("T", None, None), ("U", s_b32, None), ("W", s_t, s_u), ("T", None, None),
                     ("U", s_b64, None), ("W", s_t, s_u)]
            for t in range(2):
                if t:
                    pe.wait_ge(S("tt_ready"), 5)
                    pe.wait_ge(S("solve_copied"), 9)
                for h in range(DH):
                    for n, rhs in enumerate((qkv, kb)):
                        ins = pe.matmul(MB[:, h // 2, (h % 2) * 256 + n * P:(h % 2) * 256 + n * P + P],
                                        qkv[:, 8 + h, t * P:t * P + P], rhs[:, h, t * P:t * P + P],
                                        start=True, stop=True)
                ins.then_inc(S("qk_products"), 1)
                tt_of = lambda m: tt_[:, 8 * t + m, :]
                for p, (name, lhs, rhs) in enumerate(steps):
                    for sem, count in SOLVE_WAITS[p]:
                        pe.wait_ge(S(sem), count + t * SOLVE_COUNTS[sem])
                    bank = 2 * (p % 2)
                    for m in range(8):
                        o = MB[:, bank + m // 4, (m % 4) * P:(m % 4) * P + P]
                        if lhs is None:
                            ins = pe.transpose(o, s_u[:, m, :] if name == "A" else tt_of(m), ident[:])
                        else:
                            ins = pe.matmul(o, lhs[:, m, :], tt_of(m) if rhs is None else rhs[:, m, :],
                                            start=True, stop=True)
                    ins.then_inc(S("solve_product"), 1)
            pe.wait_ge(S("tt_ready"), 10)
            pe.wait_ge(S("solve_copied"), 18)
            for n, base in enumerate((16, 8)):
                for t in range(2):
                    b0 = 2 * (t % 2)
                    if n:
                        pe.wait_ge(S("tok_major"), t + 1)
                    for h in range(DH):
                        ins = pe.transpose(MB[:, b0 + h // 4, (h % 4) * P:(h % 4) * P + P],
                                           qkv[:, base + h, t * P:t * P + P], ident[:])
                    ins.then_inc(S("vk_turned"), 1)
            pe.wait_ge(S("panel_evacuated"), 64)
            pe.wait_ge(S("tok_major"), 4)
            for c in range(NCH):
                p0, t = CHUNK * (c % 2), c // 2
                rows = slice(p0, p0 + CHUNK)
                cs = slice(c * CHUNK, c * CHUNK + CHUNK)
                if c:
                    pe.wait_ge(S("delta_state"), c)
                    for h in range(DH):
                        ins = pe.matmul(MB[rows, h // 4, (h % 4) * P:(h % 4) * P + P], kb[:, h, cs], st[:, h, :],
                                        start=True, stop=True)
                    ins.then_inc(S("predicted"), 1)
                pe.wait_ge(S("rhs_ready"), c + 1)
                for h in range(DH):
                    ins = pe.matmul(MB[rows, 2 + h // 4, (h % 4) * P:(h % 4) * P + P],
                                    tt_[rows, 8 * t + h, p0:p0 + CHUNK], rr[rows, h * P:h * P + P],
                                    start=True, stop=True)
                ins.then_inc(S("corrected"), 1)
                pe.wait_ge(S("v_new"), c + 1)
                for h in range(DH):
                    o = PB[:, h // 2, (h % 2) * T + c * CHUNK:(h % 2) * T + c * CHUNK + CHUNK]
                    if c:
                        pe.matmul(o, st[:, h, :], eg[:, h, cs], start=True, stop=False)
                    ins = pe.matmul(o, vn[rows, h * P:h * P + P], qkt[rows, 8 * t + h, p0:p0 + CHUNK],
                                    start=(c == 0), stop=True)
                ins.then_inc(S("delta_out"), 1)
                if c < NCH - 1:
                    for h in range(DH):
                        ins = pe.matmul(MB[:, h // 4, (h % 4) * P:(h % 4) * P + P], kd[rows, t, h * P:h * P + P],
                                        vn[rows, h * P:h * P + P], start=True, stop=True)
                    ins.then_inc(S("state_step"), 1)
            pe.wait_ge(S("delta_squares"), 1)
            for b in range(4):
                ins = pe.matmul(MB[:, b, :], ones[:], odq[:, 2 * b:2 * b + 2, :], start=True, stop=True)
            ins.then_inc(S("delta_norm_sum"), 1)
            turn[0] = first["band_q"][2]
            pe.wait_ge(S("delta_read"), 1)
            for _ in range(8):
                panel(j, single)
                j += 1
            for _ in range(4):
                token_panel(j, single, [(0, 0), (0, P)])
                j += 1
            pe.wait_ge(S("delta_factor"), 1)
            pe.wait_ge(S("panel_evacuated"), 76)

            def band_scores(h):
                r = slice(BDH * (h % 2), BDH * (h % 2) + BDH)
                if h >= 2:
                    pe.wait_ge(S("band_shifted"), 2 * (h - 1))
                pe.matmul(MB[:, h % 2, 0:P], bq[r, h // 2, 0:P], bk[r, h // 2, 0:P], start=True, stop=True)
                pe.matmul(MB[:, h % 2, P:384], bq[r, h // 2, P:T], bk[r, h // 2, :], start=True, stop=True)\
                    .then_inc(S("band_scores"), 1)

            def band_values(h):
                pe.wait_ge(S("band_probs"), h + 1)
                if h >= 2:
                    pe.wait_ge(S("probs_turned"), h - 1)
                for n in range(3):
                    ins = pe.transpose(MB[:, 2 + h % 2, (0, P, 256)[n]:(0, P, 256)[n] + P],
                                       bp[:, h % 2, n * P:n * P + P], ident[:])
                ins.then_inc(S("probs_transposed"), 1)

            def band_out(h):
                pe.wait_ge(S("probs_turned"), h + 1)
                r = slice(BDH * (h % 2), BDH * (h % 2) + BDH)
                o = PB[r, h // 4, (h // 2 % 2) * T:(h // 2 % 2) * T + T]
                vcols = slice(h * BDH, h * BDH + BDH)
                pe.matmul(o[:, P:T], bv[:, 1, vcols], bpt[:, h % 2, 256:384], start=True, stop=True)
                pe.matmul(o, bv[:, 0, vcols], bpt[:, h % 2, 0:T], start=False, stop=True,
                          skip_group_check=True).then_inc(S("band_out"), 1)

            band_scores(0)
            band_scores(1)
            for h in range(BH):
                band_values(h)
                if h + 2 < BH:
                    band_scores(h + 2)
                band_out(h)
            turn[0] = first["gates"][2]
            pe.wait_ge(S("band_read"), 1)
            for _ in range(8):
                panel(j, single)
                j += 1
            pe.wait_ge(S("oa_lo"), 1)
            upper = lambda k: 8 + k
            for _ in range(4):
                panel(j, upper)
                j += 1
            pe.wait_ge(S("ob_lo"), 1)
            for _ in range(4):
                panel(j, single)
                j += 1
            pe.wait_ge(S("merged_lo"), 1)
            for _ in range(4):
                panel(j, upper)
                j += 1

            def layer_norm(count):
                pe.wait_ge(S("ln_in"), count)
                sum_tiles(MB[:, 0, 0:T], [y3[:, k, :] for k in range(KT)], "ln_sum")
                pe.wait_ge(S("ln_squares"), count)
                sum_tiles(MB[:, 1, 0:T], [sq2[:, k, :] for k in range(KT)], "ln_var")

            layer_norm(1)
            pe.wait_ge(S("h4_lo"), 1)
            for i in range(22):
                panel(j, single)
                j += 1
            j = project_hidden(j, first["down"][2], "hidden2_lo")
            layer_norm(2)
            assert j == len([1 for kind, _ in stream if kind == "split"])

        @block.scalar
        def _(act):
            def exp_table():
                act.preload_act_table_set("natural_log_exp_and_others")

            act.dma_start(xt[:], x).then_inc(S("x_landed"), 16)
            act.dma_start(cols[:], columns).then_inc(S("x_landed"), 16)
            act.dma_start(xc, ctx_x).then_inc(S("x_landed"), 16)
            act.dma_start(wgl, w_glr).then_inc(S("wgl_landed"), 16)
            act.dma_start(w_ba[:], w_beta_a).then_inc(S("small_landed"), 16)
            act.dma_start(hrow[:], head_rows).then_inc(S("small_landed"), 16)

            done = [0]
            steps = [0]

            def then(ins):
                steps[0] += 1
                ins.then_inc(S("act_step"), 1)
                act.wait_ge(S("act_step"), steps[0])

            def upper_parts(last):
                while done[0] <= min(last, N_SPLIT - 1):
                    j = done[0]
                    at = place[("split", j)]
                    act.wait_ge(S(f"landed{at % RAW}"), 16 * (at // RAW + 1))
                    if j >= PARTS:
                        act.wait_ge(S("multiplied"), j - PARTS + 1)
                    act.activation(whi[:, j % PARTS, :], raw[:, at % RAW, :], ACT.Copy).then_inc(S("upper_ready"), 1)
                    done[0] += 1

            def factor(out_, sums, n, which, name):
                exp_table()
                then(act.activation(out_, sums, ACT.Ln, scale=1.0 / n, bias=eps[:, which:which + 1]))
                act.activation(out_, out_, ACT.Exp, scale=-0.5).then_inc(S(name), 1)

            act.wait_ge(S("x_landed"), 48)
            act.wait_ge(S("constants"), CONSTANTS)
            act.activation(sq1[:, :, 0:T], xt[:], ACT.Square)
            act.activation(sq1[:, :, T:2 * T], xc, ACT.Square).then_inc(S("squares"), 1)
            act.activation(cact[:].rearrange("p a b -> p (a b)"), cols[:, 0:24], ACT.Silu).then_inc(S("c_ready"), 1)
            act.wait_ge(S("norm_sum"), 1)
            factor(rs[:], MB[:, 0, :], D, 0, "norm_factor")
            for k in range(KT):
                for s in range(2):
                    act.wait_ge(S("h1_scaled"), 2 * k + s + 1)
                    o = h1[:, k, s * T:s * T + T]
                    ins = act.activation(o, o, ACT.Identity, bias=modc[:, k, s:s + 1])
            ins.then_inc(S("h1_ready"), 1)
            act.wait_ge(S("h1_ready"), 1)
            act.activation(hhi[:].rearrange("p a b -> p (a b)"), h1.rearrange("p a b -> p (a b)"), ACT.Copy)\
                .then_inc(S("h1_hi"), 1)
            upper_parts(1)
            j = 0
            for i in range(2):
                for m in range(2):
                    act.wait_ge(S(("half_multiplied", "multiplied")[m]), j + 1)
                    act.activation(g_k[:, 2 * i + m, :], PB[:, (2 * j + m) % TURNS, :], ACT.Copy)\
                        .then_inc(S("panel_evacuated"), 1)
                upper_parts(j + 2)
                j += 1
            for i in range(4):
                for m in range(2):
                    act.wait_ge(S(("half_multiplied", "multiplied")[m]), j + 1)
                    act.activation(g_v[:, 2 * m:2 * m + 2, i * GDV:i * GDV + GDV],
                                   PB[:, (2 * j + m) % TURNS, :].rearrange("p (a b) -> p a b", a=2), ACT.Copy)\
                        .then_inc(S("panel_evacuated"), 1)
                upper_parts(j + 2)
                j += 1
            act.wait_ge(S("gate_biased"), 8)
            exp_table()
            then(act.activation(g_e3, g_x, ACT.Abs))
            then(act.activation(g_e3, g_e3, ACT.Exp, scale=-1.0))
            act.activation(g_e3, g_e3, ACT.Ln, bias=eps[:, 2:3]).then_inc(S("gate_soft"), 1)
            turn = first["gla_q"][2]

            def bank():
                nonlocal turn
                turn += 1
                return PB[:, (turn - 1) % TURNS, :]

            def pair(b):
                return b.rearrange("p (a b) -> p a b", a=2)

            for dst, func in ((g_q, ACT.Copy), (g_r, ACT.Silu)):
                for i in range(dst.shape[1] // 2):
                    act.wait_ge(S("multiplied"), j + 1)
                    act.activation(dst[:, 2 * i:2 * i + 2, :], pair(bank()), func).then_inc(S("panel_evacuated"), 1)
                    upper_parts(min(j + 2, 11))
                    j += 1
            exp_table()
            act.wait_ge(S("cumulated"), 1)
            act.activation(g_e1, g_x[:, :, 0:T], ACT.Exp, scale=1 / 16).then_inc(S("gate_exp"), 1)
            act.activation(g_e2, g_x[:, :, 0:T], ACT.Exp, scale=-1 / 16).then_inc(S("gate_exp"), 1)
            act.wait_ge(S("end_diff"), 1)
            act.activation(g_e3, g_e3, ACT.Exp, scale=1 / 16).then_inc(S("gate_exp"), 1)
            for n in range(8):
                t, half = (2, 3, 0, 1)[n // 2], n % 2
                act.wait_ge(S("keys_transposed"), n + 1)
                act.activation(g_kt[:, t, half * 4:half * 4 + 4, :].rearrange("p a b -> p (a b)"),
                               MB[:, n % 4, :], ACT.Copy).then_inc(S("keys_turned"), 1)
            act.wait_ge(S("gla_done"), 8)
            for h in range(GH):
                act.activation(g_o[:, h].rearrange("p a b -> p (a b)"), PB[:, h, :], ACT.Copy)\
                    .then_inc(S("gla_read"), 1)
            act.wait_ge(S("gla_read"), 4)
            act.activation(g_sq, g_o, ACT.Square).then_inc(S("gla_squares"), 1)
            upper_parts(13)
            act.wait_ge(S("gla_norm_sum"), 1)
            factor(g_rs.rearrange("p a b -> p (a b)"), MB[:, 0:2, :].rearrange("p a b -> p (a b)"), GDV, 0,
                   "gla_factor")
            act.wait_ge(S("gla_gated"), 1)
            act.activation(hhi[:, 0:8, :].rearrange("p a b -> p (a b)"),
                           g_o.rearrange("p a b c -> p (a b c)"), ACT.Copy).then_inc(S("gla_hi"), 1)
            for i in range(4):
                act.wait_ge(S("multiplied"), j + 1)
                act.activation(y1[:, 2 * i:2 * i + 2, :], pair(bank()), ACT.Copy).then_inc(S("panel_evacuated"), 1)
                upper_parts(j + 2)
                j += 1

            def norm(src, count):
                act.activation(sq2, src, ACT.Square).then_inc(S("squares"), 1)
                act.wait_ge(S("norm_sum"), count)
                factor(rs[:, 0:T], MB[:, 0, 0:T], D, 0, "norm_factor")

            def flat(v):
                return v.rearrange("p a b -> p (a b)")

            act.wait_ge(S("panel_evacuated"), 22)
            norm(y1, 2)
            act.wait_ge(S("x_new"), 1)
            norm(xt[:], 3)
            for k in range(KT):
                act.wait_ge(S("h2_scaled"), k + 1)
                ins = act.activation(h2[:, k, :], h2[:, k, :], ACT.Identity, bias=modc[:, 24 + k, 0:1])
            ins.then_inc(S("h2_ready"), 1)
            act.wait_ge(S("h2_ready"), 1)
            act.activation(flat(hhi[:, 0:8, :]), flat(h2), ACT.Copy).then_inc(S("h2_hi"), 1)

            def hidden_upper(i, name):
                act.wait_ge(S(name), i + 1)
                act.activation(fhi[:, i, :], f_g[:, i % 2, :], ACT.Copy).then_inc(S("panel_evacuated"), 1)

            for i in range(22):
                act.wait_ge(S("multiplied"), j + 1)
                act.activation(f_s[:, i % 2, :], bank()[:, 0:T], ACT.Silu).then_inc(S("hidden_silu"), 1)
                upper_parts(j + 2)
                if i:
                    hidden_upper(i - 1, "hidden_gated")
                j += 1
            hidden_upper(21, "hidden_gated")
            for i in range(11):
                upper_parts(j + 2)
                j += 1
            act.wait_ge(S("multiplied"), j)
            for r in range(4):
                act.activation(y1[:, 2 * r:2 * r + 2, :], pair(bank()), ACT.Copy).then_inc(S("panel_evacuated"), 1)
            act.wait_ge(S("panel_evacuated"), turn)
            norm(y1, 4)

            act.wait_ge(S("h3_ready"), 1)
            act.activation(flat(hhi[:, 0:8, :]), flat(h3), ACT.Copy).then_inc(S("h3_hi"), 1)
            act.wait_ge(S("beta_a_sum"), 1)
            act.activation(hm[:, 0, :], MB[0:DH, 0, 0:T], ACT.Sigmoid).then_inc(S("rows_act"), 1)
            act.wait_ge(S("rows_ready"), 1)
            exp_table()
            then(act.activation(hm[:, 4, :], hm[:, 1, :], ACT.Abs))
            then(act.activation(hm[:, 4, :], hm[:, 4, :], ACT.Exp, scale=-1.0))
            act.activation(hm[:, 4, :], hm[:, 4, :], ACT.Ln, bias=eps[0:DH, 2:3])
            act.activation(hrow[:, 0:1], hrow[:, 0:1], ACT.Exp).then_inc(S("rows_act"), 1)
            act.wait_ge(S("rows_ready"), 2)
            act.activation(hm[:, 3, :], hm[:, 5, :], ACT.Exp).then_inc(S("rows_act"), 1)
            for i in range(12):
                act.wait_ge(S("multiplied"), j + 1)
                b = bank()
                for m in range(2):
                    ins = act.activation(cy[:, i % 2, m, :], b[:, m * T:m * T + T], ACT.Identity,
                                         scale=col("conv_a_2", 72 + 2 * i + m))
                ins.then_inc(S("conv_begun"), 1)
                upper_parts(j + 2)
                act.wait_ge(S("conv_done"), i + 1)
                act.activation(qkv[:, 2 * i:2 * i + 2, :], cy[:, i % 2, :, :], ACT.Silu)\
                    .then_inc(S("panel_evacuated"), 1)
                j += 1
            for i in range(4):
                act.wait_ge(S("multiplied"), j + 1)
                act.activation(zs[:, 2 * i:2 * i + 2, :], pair(bank()), ACT.Silu).then_inc(S("panel_evacuated"), 1)
                upper_parts(j + 2)
                j += 1
            act.wait_ge(S("panel_evacuated"), turn)
            act.activation(sq3[:, 0:8, :], qkv[:, 0:8, :], ACT.Square).then_inc(S("qk_squares"), 1)
            act.activation(sq3[:, 8:16, :], qkv[:, 8:16, :], ACT.Square).then_inc(S("qk_squares"), 1)
            all_banks = MB[:].rearrange("p a b -> p (a b)")
            act.wait_ge(S("qk_sums"), 1)
            factor(rs2, all_banks, 1, 0, "qk_factor")
            act.wait_ge(S("qk_sums"), 2)
            act.wait_ge(S("qk_normed"), 1)
            factor(rs2, all_banks, 1, 0, "qk_factor")
            act.wait_ge(S("rows_spread"), 1)
            act.activation(flat(eg), all_banks, ACT.Exp).then_inc(S("eg_ready"), 1)
            act.wait_ge(S("decay_diff"), 1)
            act.activation(dm, dm, ACT.Exp).then_inc(S("decay_exp"), 1)
            for t in range(2):
                for p, dst, ready in ((1, s_n, 3), (2, s_nt, 3), (4, s_n, 6), (5, s_nt, 6), (7, s_n, 8),
                                      (9, s_t, 10), (10, s_u, 11), (12, s_t, 13), (13, s_u, 14)):
                    act.wait_ge(S("solve_product"), 15 * t + ready)
                    b0 = 2 * (p % 2)
                    act.activation(flat(dst), flat(MB[:, b0:b0 + 2, :]), ACT.Copy).then_inc(S("solve_copied"), 1)
            for c in range(NCH):
                rows = slice(CHUNK * (c % 2), CHUNK * (c % 2) + CHUNK)
                act.wait_ge(S("corrected"), c + 1)
                act.activation(vn[rows, :], flat(MB[rows, 2:4, :]), ACT.Copy).then_inc(S("v_new"), 1)
            act.wait_ge(S("delta_out"), 4)
            act.activation(flat(od), PB[:].rearrange("p a b -> p (a b)"), ACT.Copy).then_inc(S("delta_read"), 1)
            act.wait_ge(S("delta_read"), 1)
            act.activation(odq, od, ACT.Square).then_inc(S("delta_squares"), 1)
            act.wait_ge(S("delta_norm_sum"), 1)
            factor(rs2, all_banks, DDK, 0, "delta_factor")
            act.wait_ge(S("band_masked"), 1)
            src = bass.AP(rel_bias.tensor, 0, [[1, 64], [REL, BH], [1, T]])
            act.dma_start(bx[64:128, :, :], src).then_inc(S("bias_landed"), 16)
            src = bass.AP(rel_bias.tensor, 0, [[1, 64], [REL, BH], [1, T - 64]])
            act.dma_start(bx[0:64, :, 64:T], src).then_inc(S("bias_landed"), 16)
            act.wait_ge(S("delta_gated"), 1)
            act.activation(flat(hhi[:, 8:16, :]), flat(od), ACT.Copy).then_inc(S("oa_hi"), 1)
            for dst, scale in ((bq, BDH ** -0.5), (bk, 1.0)):
                for i in range(4):
                    act.wait_ge(S("multiplied"), j + 1)
                    act.activation(dst[:, 2 * i:2 * i + 2, :], pair(bank()), ACT.Copy, scale=scale)\
                        .then_inc(S("panel_evacuated"), 1)
                    upper_parts(j + 2)
                    j += 1
            act.wait_ge(S("oa_lo"), 1)
            for i in range(4):
                act.wait_ge(S("multiplied"), j + 1)
                act.activation(bv[:, :, i * 256:i * 256 + 256], pair(bank()), ACT.Copy)\
                    .then_inc(S("panel_evacuated"), 1)
                upper_parts(j + 2)
                j += 1

            def band_exp(h):
                act.wait_ge(S("band_negmax"), h + 1)
                for n, (a, b) in enumerate(((0, P), (P, 384))):
                    act.activation(bp[:, h % 2, a:b], bp[:, h % 2, a:b], ACT.Exp, bias=bst[:, h % 2, 2 + n:3 + n],
                                   accum_out=bst[:, h % 2, 4 + n:5 + n]).then_inc(S("band_exp"), 1)

            exp_table()
            band_exp(0)
            for h in range(BH):
                if h + 1 < BH:
                    band_exp(h + 1)
                act.wait_ge(S("probs_transposed"), h + 1)
                if h >= 2:
                    act.wait_ge(S("band_out"), h - 1)
                act.activation(bpt[:, h % 2, :], MB[:, 2 + h % 2, 0:384], ACT.Copy).then_inc(S("probs_turned"), 1)
            act.wait_ge(S("band_out"), BH)
            act.activation(flat(ob), PB[:].rearrange("p a b -> p (a b)"), ACT.Copy).then_inc(S("band_read"), 1)
            for i in range(8):
                act.wait_ge(S("multiplied"), j + 1)
                b = bank()
                for m in range(2):
                    ins = act.activation(ga[:, 2 * i + m, :], b[:, m * T:m * T + T], ACT.Sigmoid,
                                         bias=col("b_gate_2", 2 * i + m))
                ins.then_inc(S("panel_evacuated"), 1)
                upper_parts(j + 2)
                j += 1
            act.activation(flat(hhi[:, 0:8, :]), flat(ob), ACT.Copy).then_inc(S("ob_hi"), 1)
            for dst in (ya, yb):
                for i in range(4):
                    act.wait_ge(S("multiplied"), j + 1)
                    act.activation(dst[:, 2 * i:2 * i + 2, :], pair(bank()), ACT.Copy)\
                        .then_inc(S("panel_evacuated"), 1)
                    upper_parts(j + 2)
                    j += 1
            act.wait_ge(S("merged"), 1)
            act.activation(flat(hhi[:, 8:16, :]), flat(ya), ACT.Copy).then_inc(S("merged_hi"), 1)
            for i in range(4):
                act.wait_ge(S("multiplied"), j + 1)
                b = bank()
                for m in range(2):
                    f = 2 * i + m
                    ins = act.activation(y3[:, f, :], b[:, m * T:m * T + T], ACT.Identity,
                                         scale=mod2[:, 16 + f:17 + f])
                ins.then_inc(S("panel_evacuated"), 1)
                upper_parts(j + 2)
                j += 1

            def layer_norm(count, name, dst):
                act.wait_ge(S("ln_sum"), count)
                act.activation(rs[:, 0:T], MB[:, 0, 0:T], ACT.Copy, scale=1.0 / D).then_inc(S("ln_mean"), 1)
                act.wait_ge(S("ln_centred"), count)
                act.activation(sq2, y3, ACT.Square).then_inc(S("ln_squares"), 1)
                act.wait_ge(S("ln_var"), count)
                factor(rs[:, T:2 * T], MB[:, 1, 0:T], D, 1, "ln_factor")
                for k in range(KT):
                    act.wait_ge(S("ln_scaled"), 8 * (count - 1) + k + 1)
                    ins = act.activation(dst[:, k, :], y3[:, k, :], ACT.Identity, bias=col(name, k))
                return ins

            layer_norm(1, "ln1_b_2", xt).then_inc(S("x3_ready"), 1)
            act.wait_ge(S("h4_ready"), 1)
            act.activation(flat(hhi[:, 0:8, :]), flat(h2), ACT.Copy).then_inc(S("h4_hi"), 1)
            for i in range(22):
                act.wait_ge(S("multiplied"), j + 1)
                b = bank()
                for m in range(2):
                    ins = act.activation(f_u[:, i % 2, m, :], b[:, m * T:m * T + T], ACT.Identity,
                                         scale=col("conv_ffn_2", 88 + 22 * m + i),
                                         bias=col("b_conv_ffn_2", 22 * m + i))
                ins.then_inc(S("up_begun"), 1)
                upper_parts(j + 2)
                if i:
                    hidden_upper(i - 1, "hidden2_gated")
                act.wait_ge(S("up_done"), i + 1)
                act.activation(f_s[:, i % 2, :], f_u[:, i % 2, 0, :], ACT.Silu).then_inc(S("hidden2_silu"), 1)
                j += 1
            hidden_upper(21, "hidden2_gated")
            for i in range(11):
                upper_parts(j + 2)
                j += 1
            act.wait_ge(S("multiplied"), j)
            for r in range(4):
                b = bank()
                for m in range(2):
                    f = 2 * r + m
                    ins = act.activation(y3[:, f, :], b[:, m * T:m * T + T], ACT.Identity,
                                         scale=mod2[:, 40 + f:41 + f])
                ins.then_inc(S("panel_evacuated"), 1)
            layer_norm(2, "ln2_b_2", f_out).then_inc(S("out_ready"), 1)

        @block.vector
        def _(dve):
            done = [0]
            steps = [0]

            def then(ins):
                steps[0] += 1
                ins.then_inc(S("dve_step"), 1)
                dve.wait_ge(S("dve_step"), steps[0])

            def lower_parts(last):
                while done[0] <= min(last, N_SPLIT - 1):
                    j = done[0]
                    dve.wait_ge(S("upper_ready"), j + 1)
                    dve.tensor_tensor(wlo[:, j % PARTS, :], raw[:, place[("split", j)] % RAW, :],
                                      whi[:, j % PARTS, :].bitcast(F32), ALU.subtract).then_inc(S("parts_ready"), 1)
                    done[0] += 1

            def flat(v):
                return v.rearrange("p a b -> p (a b)")

            def lower(dst, full, upper, name):
                dve.tensor_tensor(dst, full, upper.bitcast(F32), ALU.subtract).then_inc(S(name), 1)

            def over_tokens(v, n=T):
                return v.unsqueeze(2).to_broadcast([v.shape[0], v.shape[1], n])

            def over_tiles(v, n):
                return v.unsqueeze(1).to_broadcast([v.shape[0], n, v.shape[1]])

            dve.wait_ge(S("constants"), CONSTANTS)
            dve.tensor_copy(mask_up[:], causal_t[:])
            then(dve.tensor_copy(mask_dn[:], causal_dn[:]))
            dve.wait_ge(S("x_landed"), 48)
            dve.wait_ge(S("matvec_done"), 8)
            then(dve.tensor_tensor(modc[:, 0:16, :], MB[:, 1, 0:32].rearrange("p (a b) -> p a b", b=2),
                                   over_tokens(col("mod_b", 0, 16), 2), ALU.add))
            for s in range(2):
                ins = dve.scalar_tensor_tensor(sc_a[:, s, :], modc[:, 8:16, s], 1.0, col("norm_g", 0, 8),
                                               ALU.add, ALU.mult)
            then(ins)
            dve.wait_ge(S("norm_factor"), 1)
            for k in range(KT):
                for s in range(2):
                    dve.scalar_tensor_tensor(h1[:, k, s * T:s * T + T], (xt[:], xc)[s][:, k, :],
                                             sc_a[:, s, k:k + 1], rs[:, s * T:s * T + T], ALU.mult, ALU.mult)\
                        .then_inc(S("h1_scaled"), 1)
            dve.wait_ge(S("h1_hi"), 1)
            lower(hlo[:].rearrange("p a b -> p (a b)"), flat(h1), hhi[:].rearrange("p a b -> p (a b)"), "h1_lo")
            lower_parts(1)
            dve.wait_ge(S("glr_sum"), 1)
            dve.tensor_copy(glr, MB[0:32, 0, :]).then_inc(S("glr_ready"), 1)
            lower_parts(2)
            for i in range(8):
                dve.wait_ge(S("gate_sum"), i + 1)
                dve.tensor_scalar(g_x[:, i, :], MB[:, i % 4, :], col("gla_b_gate", i), None, ALU.add)\
                    .then_inc(S("gate_biased"), 1)
            lower_parts(7)
            dve.wait_ge(S("gate_soft"), 1)
            then(dve.scalar_tensor_tensor(flat(g_x), flat(g_x), 0.0, flat(g_e3), ALU.min, ALU.subtract))
            for i in range(8):
                for a, n in [(c * CHUNK, CHUNK) for c in range(NCH)] + [(T, T)]:
                    v = g_x[:, i, a:a + n]
                    if i >= 4:
                        v = v[:, ::-1]
                    ins = dve.tensor_tensor_scan(v, ones_row[:, 0:n], v, 0.0, ALU.mult, ALU.add)
                if i == 3:
                    lower_parts(8)
            ins.then_inc(S("cumulated"), 1)
            dve.wait_ge(S("cumulated"), 1)
            for d in range(2):
                b = g_x[:, 4 * d:4 * d + 4, 0:T].rearrange("p h (c t) -> p h c t", t=CHUNK)
                e = CHUNK - 1 if d == 0 else 0
                dve.tensor_tensor(g_e3[:, 4 * d:4 * d + 4, 0:T].rearrange("p h (c t) -> p h c t", t=CHUNK),
                                  b[:, :, :, e:e + 1].to_broadcast([P, GH, NCH, CHUNK]), b, ALU.subtract)
                b = g_x[:, 4 * d:4 * d + 4, T:2 * T]
                e = T - 1 if d == 0 else 0
                ins = dve.tensor_tensor(g_e3[:, 4 * d:4 * d + 4, T:2 * T],
                                        b[:, :, e:e + 1].to_broadcast([P, GH, T]), b, ALU.subtract)
            ins.then_inc(S("end_diff"), 1)
            lower_parts(11)
            dve.wait_ge(S("panel_evacuated"), 18)
            dve.wait_ge(S("gate_exp"), 2)
            for d in range(2):
                e = g_e1[:, 4 * d:4 * d + 4, :].rearrange("p h (c t) -> p h c t", t=CHUNK)
                end = CHUNK - 1 if d == 0 else 0
                ins = dve.tensor_copy(dec[:, 4 * d:4 * d + 4, :], e[:, :, :, end])
            then(ins)
            for d in range(2):
                q4 = g_e1[:, 4 * d:4 * d + 4, :]
                dve.scalar_tensor_tensor(flat(q4), flat(q4), GDK ** -0.5, flat(g_q), ALU.mult, ALU.mult)
                k4 = g_e2[:, 4 * d:4 * d + 4, :]
                ins = dve.tensor_tensor(k4, k4, g_k[:, :, 0:T], ALU.mult)
            ins.then_inc(S("keys_decayed"), 1)
            dve.wait_ge(S("gate_exp"), 3)
            for d in range(2):
                k4 = g_e3[:, 4 * d:4 * d + 4, :]
                ins = dve.tensor_tensor(k4, k4, g_k, ALU.mult)
            ins.then_inc(S("end_keys"), 1)
            dve.wait_ge(S("matvec_done"), 24)
            then(dve.tensor_tensor(modc[:, 16:48, :], MB[:, 1, 32:96].rearrange("p (a b) -> p a b", b=2),
                                   over_tokens(col("mod_b", 16, 32), 2), ALU.add))
            dve.sem_inc(S("mod_ready"), 2)
            dve.wait_ge(S("scores_zeroed"), 1)
            for g in range(4):
                dve.wait_ge(S("scores"), g + 1)
                mask = (mask_up, mask_dn)[g // 2]
                dve.copy_predicated(g_sc[:, 4 * g:4 * g + 4, :], over_tiles(mask[:], 4),
                                    MB[:, g, :].rearrange("p (a b) -> p a b", a=4)).then_inc(S("scores_masked"), 1)
            for i in range(8):
                dve.wait_ge(S("state_sum"), i // 2 * 2 + 2)
                dve.tensor_copy(g_s[:, i, :], MB[:, i // 2, (i % 2) * 256:(i % 2) * 256 + 256])\
                    .then_inc(S("state_new"), 1)
            for s in range(NCH - 1):
                for i in range(8):
                    c = s if i < 4 else NCH - 1 - s
                    dve.wait_ge(S("state_sum"), 8 * (s + 1) + i // 2 * 2 + 2)
                    dve.scalar_tensor_tensor(g_s[:, i, :], g_s[:, i, :], dec[:, i, c:c + 1],
                                             MB[:, i // 2, (i % 2) * 256:(i % 2) * 256 + 256], ALU.mult, ALU.add)\
                        .then_inc(S("state_new"), 1)
            dve.wait_ge(S("gla_factor"), 1)
            for v in range(2):
                o = g_o[:, :, v, :]
                ins = dve.scalar_tensor_tensor(o, o, col("gla_norm_g", v), g_rs, ALU.mult, ALU.mult)
            then(ins)
            o = g_o.rearrange("p a b c -> p (a b c)")
            dve.tensor_tensor(o, o, flat(g_r), ALU.mult).then_inc(S("gla_gated"), 1)
            dve.wait_ge(S("gla_hi"), 1)
            lower(flat(hlo[:, 0:8, :]), o, flat(hhi[:, 0:8, :]), "gla_lo")
            j = 12
            lower_parts(13)
            for i in range(4):
                lower_parts(j + 2)
                j += 1

            def add_normed(count, gate, gain):
                then(dve.tensor_tensor(gcol[:], modc[:, gate:gate + 8, 0], col("norm_g", gain, 8), ALU.mult))
                dve.wait_ge(S("norm_factor"), count)
                for k in range(KT):
                    ins = dve.scalar_tensor_tensor(y1[:, k, :], y1[:, k, :], gcol[:, k:k + 1], rs[:, 0:T],
                                                   ALU.mult, ALU.mult)
                then(ins)
                dve.tensor_tensor(xt[:], xt[:], y1, ALU.add).then_inc(S("x_new"), 1)

            add_normed(2, 16, 8)
            then(dve.scalar_tensor_tensor(sc_a[:, 0, :], modc[:, 32:40, 0], 1.0, col("norm_g", 16, 8),
                                          ALU.add, ALU.mult))
            dve.wait_ge(S("x_new"), 1)
            dve.wait_ge(S("norm_factor"), 3)
            for k in range(KT):
                dve.scalar_tensor_tensor(h2[:, k, :], xt[:, k, :], sc_a[:, 0, k:k + 1], rs[:, 0:T],
                                         ALU.mult, ALU.mult).then_inc(S("h2_scaled"), 1)
            dve.wait_ge(S("h2_hi"), 1)
            lower(flat(hlo[:, 0:8, :]), flat(h2), flat(hhi[:, 0:8, :]), "h2_lo")

            def hidden_lower(i, evacuated, name):
                dve.wait_ge(S("panel_evacuated"), evacuated + i + 1)
                lower(flo[:, i, :], f_g[:, i % 2, :], fhi[:, i, :], name)

            t0 = first["ffn_in"][2]
            for i in range(22):
                if i >= 2:
                    dve.wait_ge(S("hidden_lo"), i - 1)
                dve.wait_ge(S("hidden_silu"), i + 1)
                dve.tensor_tensor(f_g[:, i % 2, :], f_s[:, i % 2, :], PB[:, (t0 + i) % TURNS, T:2 * T], ALU.mult)\
                    .then_inc(S("hidden_gated"), 1)
                lower_parts(j + 2)
                if i:
                    hidden_lower(i - 1, t0, "hidden_lo")
                j += 1
            hidden_lower(21, t0, "hidden_lo")
            for i in range(11):
                lower_parts(j + 2)
                j += 1
            add_normed(4, 40, 24)
            dve.wait_ge(S("matvec_done"), 48)
            then(dve.tensor_tensor(mod2[:], MB[:, 3, 0:48], col("b_ada_2", 0, 48), ALU.add))
            then(dve.tensor_scalar(sc_a[:, 1, :], mod2[:, 8:16], 1.0, None, ALU.add))
            dve.wait_ge(S("x_new"), 2)
            for k in range(KT):
                ins = dve.tensor_scalar(h3[:, k, :], xt[:, k, :], sc_a[:, 1, k:k + 1], mod2[:, k:k + 1],
                                        ALU.mult, ALU.add)
            ins.then_inc(S("h3_ready"), 1)
            dve.wait_ge(S("h3_hi"), 1)
            lower(flat(hlo[:, 0:8, :]), flat(h3), flat(hhi[:, 0:8, :]), "h3_lo")
            dve.wait_ge(S("rows_act"), 1)
            dve.tensor_scalar(hm[:, 1, :], MB[0:DH, 0, T:2 * T], hrow[:, 1:2], None, ALU.add)\
                .then_inc(S("rows_ready"), 1)
            dve.wait_ge(S("rows_act"), 2)
            then(dve.scalar_tensor_tensor(hm[:, 6, :], hm[:, 1, :], 0.0, hm[:, 4, :], ALU.max, ALU.add))
            then(dve.tensor_scalar(hm[:, 1, :], hm[:, 6, :], hrow[:, 0:1], -1.0, ALU.mult, ALU.mult))
            for c in range(NCH):
                cs = slice(c * CHUNK, c * CHUNK + CHUNK)
                ins = dve.tensor_tensor_scan(hm[:, 2, cs], ones[0:DH, 0:CHUNK], hm[:, 1, cs], 0.0,
                                             ALU.mult, ALU.add)
            then(ins)
            rows = hm[:, 2, :].rearrange("p (c t) -> p c t", t=CHUNK)
            dve.tensor_tensor(hm[:, 5, :].rearrange("p (c t) -> p c t", t=CHUNK),
                              rows[:, :, CHUNK - 1:CHUNK].to_broadcast([DH, NCH, CHUNK]), rows, ALU.subtract)\
                .then_inc(S("rows_ready"), 1)
            t0 = first["qkv"][2]
            for i in range(12):
                dve.wait_ge(S("conv_begun"), i + 1)
                b = PB[:, (t0 + i) % TURNS, :]
                for s in range(1, 4):
                    for m in range(2):
                        o = cy[:, i % 2, m, s:T]
                        ins = dve.scalar_tensor_tensor(o, b[:, m * T:m * T + T - s],
                                                       col("conv_a_2", 24 * (3 - s) + 2 * i + m), o,
                                                       ALU.mult, ALU.add)
                    if s < 3:
                        then(ins)
                ins.then_inc(S("conv_done"), 1)
                lower_parts(j + 2)
                j += 1
            for i in range(4):
                lower_parts(j + 2)
                j += 1
            dve.wait_ge(S("qk_factor"), 1)
            dve.scalar_tensor_tensor(flat(qkv[:, 0:8, :]), flat(qkv[:, 0:8, :]), DDK ** -0.5, rs2,
                                     ALU.mult, ALU.mult).then_inc(S("qk_normed"), 1)
            dve.wait_ge(S("qk_factor"), 2)
            kc = qkv[:, 8:16, :]
            dve.tensor_tensor(flat(kc), flat(kc), rs2, ALU.mult).then_inc(S("qk_normed"), 1)
            dve.wait_ge(S("tok_rows"), 1)
            dve.tensor_copy(gl_tok[:].rearrange("p a b c -> p (a b c)"), MB[:, 0, 0:48]).then_inc(S("tok_ready"), 1)
            dve.wait_ge(S("tok_ready"), 1)
            dve.wait_ge(S("rows_spread"), 1)
            dve.wait_ge(S("eg_ready"), 1)
            for t in range(2):
                for h in range(DH):
                    a = (h % 2) * T + t * P
                    ins = dve.tensor_scalar(dm[:, t * 8 + h, :], MB[:, h // 2, a:a + P],
                                            gl_tok[:, 0, t, h:h + 1], 0.0, ALU.subtract, ALU.min)
            ins.then_inc(S("decay_diff"), 1)
            dve.wait_ge(S("decay_exp"), 1)
            then(dve.tensor_tensor(dm, dm, over_tiles(causal_t[:], 16), ALU.mult))
            dve.tensor_copy(gl_end[:], eg.rearrange("p h (c t) -> p h c t", t=CHUNK)[:, :, :, CHUNK - 1])
            dve.wait_ge(S("rows_spread"), 2)
            dve.tensor_tensor(flat(kb), flat(kc), MB[:].rearrange("p a b -> p (a b)"), ALU.mult)\
                .then_inc(S("kb_ready"), 1)
            for t in range(2):
                dve.wait_ge(S("qk_products"), t + 1)
                prod = MB[:].rearrange("p a (b c) -> p (a b) c", c=256)
                dmt = dm[:, 8 * t:8 * t + 8, :]
                dve.tensor_tensor(qkt[:, 8 * t:8 * t + 8, :], prod[:, :, 0:P], dmt, ALU.mult)
                then(dve.tensor_tensor(s_u, prod[:, :, P:2 * P], dmt, ALU.mult))
                dve.sem_inc(S("at_ready"), 1)
                tt8 = tt_[:, 8 * t:8 * t + 8, :]
                then(dve.scalar_tensor_tensor(s_nt, s_u, -1.0, over_tiles(m16t[:], 8), ALU.mult, ALU.mult))
                dve.tensor_tensor(tt8, s_nt, over_tiles(ident[:], 8), ALU.add)

                def pair_banks(p):
                    b0 = 2 * (p % 2)
                    return MB[:, b0:b0 + 2, :].rearrange("p a (b c) -> p (a b) c", c=P)

                dve.wait_ge(S("solve_product"), 15 * t + 1)
                dve.scalar_tensor_tensor(s_n, pair_banks(0), -1.0, over_tiles(m16[:], 8), ALU.mult, ALU.mult)
                dve.tensor_tensor(s_b32, pair_banks(0), over_tiles(d32[:], 8), ALU.mult)
                dve.tensor_tensor(s_b64, pair_banks(0), over_tiles(d64[:], 8), ALU.mult)\
                    .then_inc(S("solve_masked"), 1)
                for p, op in ((3, ALU.add), (6, ALU.add), (8, ALU.add), (11, ALU.subtract), (14, ALU.subtract)):
                    dve.wait_ge(S("solve_product"), 15 * t + p + 1)
                    dve.tensor_tensor(tt8, tt8, pair_banks(p), op).then_inc(S("tt_ready"), 1)
            then(dve.tensor_tensor(flat(kb), flat(kb), flat(eg), ALU.mult))
            dve.tensor_tensor(flat(eg), flat(eg), flat(qkv[:, 0:8, :]), ALU.mult)
            for n, dst in enumerate((vb, kd)):
                for t in range(2):
                    dve.wait_ge(S("vk_turned"), 2 * n + t + 1)
                    dve.tensor_tensor(dst[:, t, :].rearrange("p (a b) -> p a b", b=P), pair_banks(t),
                                      over_tokens(gl_tok[:, 1 + n, t, :], P), ALU.mult)\
                        .then_inc(S("tok_major"), 1)
            dve.wait_ge(S("tok_major"), 4)
            for c in range(NCH):
                rows = slice(CHUNK * (c % 2), CHUNK * (c % 2) + CHUNK)
                t = c // 2
                if c == 0:
                    dve.tensor_copy(rr[rows, :], vb[rows, t, :]).then_inc(S("rhs_ready"), 1)
                else:
                    dve.wait_ge(S("predicted"), c)
                    dve.tensor_tensor(rr[rows, :], vb[rows, t, :], flat(MB[rows, 0:2, :]), ALU.subtract)\
                        .then_inc(S("rhs_ready"), 1)
                if c < NCH - 1:
                    if c:
                        dve.wait_ge(S("delta_out"), c + 1)
                        then(dve.tensor_tensor(st, st, over_tokens(gl_end[:, :, c], P), ALU.mult))
                    dve.wait_ge(S("state_step"), c + 1)
                    if c:
                        ins = dve.tensor_tensor(flat(st), flat(st), flat(MB[:, 0:2, :]), ALU.add)
                    else:
                        ins = dve.tensor_copy(flat(st), flat(MB[:, 0:2, :]))
                    ins.then_inc(S("delta_state"), 1)
            dve.wait_ge(S("delta_norm_sum"), 1)
            dve.memset(bx[0:64, :, 0:64], NEG).then_inc(S("band_masked"), 1)
            dve.wait_ge(S("delta_factor"), 1)
            then(dve.scalar_tensor_tensor(flat(od), flat(od), col("norm_a_2"), rs2, ALU.mult, ALU.mult))
            dve.tensor_tensor(flat(od), flat(od), flat(zs), ALU.mult).then_inc(S("delta_gated"), 1)
            dve.wait_ge(S("oa_hi"), 1)
            lower(flat(hlo[:, 8:16, :]), flat(od), flat(hhi[:, 8:16, :]), "oa_lo")
            for i in range(12):
                lower_parts(j + 2)
                j += 1
            dve.wait_ge(S("bias_landed"), 32)

            def band_shift(h):
                dve.wait_ge(S("band_scores"), h + 1)
                if h >= 2:
                    dve.wait_ge(S("probs_transposed"), h - 1)
                for n, (a, b) in enumerate(((0, P), (P, 384))):
                    dve.tensor_tensor_reduce(bp[:, h % 2, a:b], MB[:, h % 2, a:b], bx[:, h, 0:b - a][:, ::-1],
                                             1.0, NEG, ALU.add, ALU.max, bst[:, h % 2, n:n + 1])\
                        .then_inc(S("band_shifted"), 1)
                dve.wait_ge(S("band_shifted"), 2 * h + 2)
                dve.tensor_scalar(bst[:, h % 2, 2:4], bst[:, h % 2, 0:2], -1.0, None, ALU.mult)\
                    .then_inc(S("band_negmax"), 1)

            band_shift(0)
            for h in range(BH):
                if h + 1 < BH:
                    band_shift(h + 1)
                dve.wait_ge(S("band_exp"), 2 * h + 2)
                then(dve.reciprocal(bst[:, h % 2, 6:8], bst[:, h % 2, 4:6]))
                for n, (a, b) in enumerate(((0, P), (P, 384))):
                    ins = dve.tensor_scalar(bp[:, h % 2, a:b], bp[:, h % 2, a:b], bst[:, h % 2, 6 + n:7 + n],
                                            None, ALU.mult)
                ins.then_inc(S("band_probs"), 1)
            for i in range(8):
                lower_parts(j + 2)
                j += 1
            dve.wait_ge(S("ob_hi"), 1)
            lower(flat(hlo[:, 0:8, :]), flat(ob), flat(hhi[:, 0:8, :]), "ob_lo")
            for i in range(8):
                lower_parts(j + 2)
                if i == 3:
                    dve.wait_ge(S("panel_evacuated"), first["branch_b"][2])
                    dve.tensor_tensor(ya, ya, ga[:, 0:8, :], ALU.mult)
                j += 1
            dve.wait_ge(S("panel_evacuated"), first["mix"][2])
            then(dve.tensor_tensor(yb, yb, ga[:, 8:16, :], ALU.mult))
            dve.tensor_tensor(ya, ya, yb, ALU.add).then_inc(S("merged"), 1)
            dve.wait_ge(S("merged_hi"), 1)
            lower(flat(hlo[:, 8:16, :]), flat(ya), flat(hhi[:, 8:16, :]), "merged_lo")
            for i in range(4):
                lower_parts(j + 2)
                j += 1

            def layer_norm(count, gain):
                dve.scalar_tensor_tensor(flat(y3), xt[:].rearrange("p a b -> p (a b)"), ALPHA, flat(y3),
                                         ALU.mult, ALU.add).then_inc(S("ln_in"), 1)
                dve.wait_ge(S("ln_mean"), count)
                dve.tensor_tensor(y3, y3, over_tiles(rs[:, 0:T], KT), ALU.subtract).then_inc(S("ln_centred"), 1)
                dve.wait_ge(S("ln_centred"), count)
                dve.wait_ge(S("ln_factor"), count)
                for k in range(KT):
                    dve.scalar_tensor_tensor(y3[:, k, :], y3[:, k, :], col(gain, k), rs[:, T:2 * T],
                                             ALU.mult, ALU.mult).then_inc(S("ln_scaled"), 1)

            dve.wait_ge(S("panel_evacuated"), first["up"][2])
            layer_norm(1, "ln1_g_2")
            then(dve.tensor_scalar(sc_a[:, 1, :], mod2[:, 32:40], 1.0, None, ALU.add))
            dve.wait_ge(S("x3_ready"), 1)
            for k in range(KT):
                ins = dve.tensor_scalar(h2[:, k, :], xt[:, k, :], sc_a[:, 1, k:k + 1], mod2[:, 24 + k:25 + k],
                                        ALU.mult, ALU.add)
            ins.then_inc(S("h4_ready"), 1)
            dve.wait_ge(S("h4_hi"), 1)
            lower(flat(hlo[:, 0:8, :]), flat(h2), flat(hhi[:, 0:8, :]), "h4_lo")
            t0 = first["up"][2]
            for i in range(22):
                dve.wait_ge(S("up_begun"), i + 1)
                b = PB[:, (t0 + i) % TURNS, :]
                for s in range(1, 3):
                    for m in range(2):
                        o = f_u[:, i % 2, m, s:T]
                        ins = dve.scalar_tensor_tensor(o, b[:, m * T:m * T + T - s],
                                                       col("conv_ffn_2", 44 * (2 - s) + 22 * m + i), o,
                                                       ALU.mult, ALU.add)
                    if s < 2:
                        then(ins)
                ins.then_inc(S("up_done"), 1)
                lower_parts(j + 2)
                if i:
                    hidden_lower(i - 1, t0, "hidden2_lo")
                if i >= 2:
                    dve.wait_ge(S("hidden2_lo"), i - 1)
                dve.wait_ge(S("hidden2_silu"), i + 1)
                dve.tensor_tensor(f_g[:, i % 2, :], f_s[:, i % 2, :], f_u[:, i % 2, 1, :], ALU.mult)\
                    .then_inc(S("hidden2_gated"), 1)
                j += 1
            hidden_lower(21, t0, "hidden2_lo")
            for i in range(11):
                lower_parts(j + 2)
                j += 1
            dve.wait_ge(S("panel_evacuated"), first["down"][2] + 4)
            layer_norm(2, "ln2_g_2")


_ARGS = ["panels", "x", "ctx_x", "columns", "w_glr", "w_gate", "w_beta_a", "head_rows", "rel_bias"]


def _lay_out(inputs):
    a = {k: np.asarray(v) for k, v in inputs.items()}

    def wide(w, cols=None):
        n = w.shape[1] // 256
        return w.reshape(KT, P, n, 256).transpose(2, 1, 0, 3).reshape(n, P, 2048)

    def gate_up(w):
        v = w.reshape(KT, P, 2, FT, P).transpose(3, 1, 0, 2, 4)
        return v.reshape(FT, P, 2048)

    def tall(w):
        return w.reshape(FT // 2, 2, P, D).transpose(0, 2, 1, 3).reshape(FT // 2, P, 2048)

    gla, w2 = a["gla_w_in"][0], a["w_in_2"][0]
    mod, ada = wide(a["mod_w"][0]), wide(a["w_ada_2"][0])
    ffn = gate_up(a["ffn_w_in"][0])
    pieces = [mod[0:8], wide(gla[:, 512:1024]), wide(gla[:, 1024:2048]), wide(gla[:, 0:512]),
              wide(gla[:, 2048:3072]), mod[8:24], wide(a["gla_w_out"][0]),
              np.stack([ffn, ada[0:22]], axis=1).reshape(44, P, 2048), ada[22:24], tall(a["ffn_w_out"][0]),
              wide(w2[:, 0:4096]), wide(w2[:, 4112:9232]),
              wide(a["w_branch_a_2"][0]), wide(a["w_branch_b_2"][0]), wide(a["w_o_2"][0]),
              gate_up(a["w_up_2"][0]), tall(a["w_down_2"][0])]
    out = {"panels": np.concatenate(pieces)}

    def feature_major(v):
        return np.ascontiguousarray(v.T.reshape(KT, P, T).transpose(1, 0, 2))

    out["x"], out["ctx_x"] = feature_major(a["x"][0]), feature_major(a["ctx"][0])
    vectors = [a["c"], a["c_ctx"], a["c_2"]] + [a[name] for name, _ in COLUMNS[3:]]
    out["columns"] = np.concatenate([v.reshape(-1) for v in vectors]).reshape(NCOL, P).T.copy()
    out["w_glr"] = gla[:, 3072:3104].reshape(KT, P, 32).transpose(1, 0, 2).copy()
    out["w_gate"] = a["gla_w_gate"][0].copy()
    out["w_beta_a"] = w2[:, 4096:4112].reshape(KT, P, 16).transpose(1, 0, 2).copy()
    out["head_rows"] = np.stack([a["a_log_2"][0], a["dt_bias_2"][0]], axis=1)
    out["rel_bias"] = a["rel_bias_2"][0].copy()
    return out


def kernel(**inputs):
    import concourse.bacc as _bacc
    from concourse.bass_utils import run_bass_kernel_spmd as _run

    nc = _bacc.Bacc("TRN2", target_bir_lowering=False, num_devices=1)
    laid = _lay_out(inputs)
    arrays, args = {}, []
    for name in _ARGS:
        v = laid[name]
        arrays[f"in_{name}"] = v
        args.append(nc.dram_tensor(f"in_{name}", v.shape, mybir.dt.from_np(v.dtype), kind="ExternalInput").ap())
    args.append(nc.dram_tensor("out_x", (P, KT, T), F32, kind="ExternalOutput").ap())
    two_blocks(nc, *args)
    r = _run(nc, [arrays], core_ids=[0])
    return r.results[0]["out_x"].transpose(1, 0, 2).reshape(1, D, T).transpose(0, 2, 1)
```

```python
from contextlib import ExitStack

import concourse.bass as bass
from concourse import mybir
import numpy as np

F32 = mybir.dt.float32
F32R = mybir.dt.float32r
I32 = mybir.dt.int32
ALU = mybir.AluOpType
ACT = mybir.ActivationFunctionType
AX_X = mybir.AxisListType.X

P = 128
D = 1024
KT = D // P
T = 256
CHUNK = 64
HALF = 1024
NCH = T // CHUNK
FFN = 2816
FT = FFN // P
GH, GDK, GDV = 4, 128, 256
DH, DDK = 8, 128
BH, BDH = 16, 64
REL = 320
EPS_RMS, EPS_LN = 1e-6, 1e-5
ALPHA = 2.0 ** 0.25
NEG = -1e30
RAW, PARTS, TURNS = 6, 4, 4

LAYERS = [("mod_first", "R", 8), ("gla_k", "SAA", 2), ("gla_v", "SAA", 4), ("gla_q", "S", 2),
          ("gla_r", "S", 4), ("gla_out", "SA", 4), ("ffn_in", "SA", 22),
          ("ffn_out", "SA", 2), ("ffn_out_rest", "S", 9), ("qkv", "S", 12), ("z", "S", 4),
          ("band_q", "S", 4), ("band_k", "S", 4), ("band_v", "S", 4), ("gates", "S", 8),
          ("branch_a", "S", 4), ("branch_b", "S", 4), ("mix", "S", 4), ("up", "S", 22),
          ("down", "S", 11)]


def plan_stream():
    stream, first, count_of = [], {}, {"S": 0, "R": 0, "A": 0}
    turn = 0
    for layer, pattern, count in LAYERS:
        first[layer] = (count_of["S"], turn)
        for _ in range(count):
            for kind in pattern:
                stream.append((kind, count_of[kind]))
                count_of[kind] += 1
        turn += {"gla_k": 2 * count, "gla_v": 2 * count, "mod_first": 0, "ffn_out": 4, "ffn_out_rest": 0,
                 "down": 4}.get(layer, count)
    return stream, first


COLUMNS = [("c", 8), ("c_ctx", 8), ("mod_b", 48), ("norm_g", 32), ("gla_b_gate", 8), ("gla_norm_g", 2),
           ("b_ada_2", 48), ("b_gate_2", 16), ("conv_a_2", 96), ("norm_a_2", 1), ("ln1_g_2", 8), ("ln1_b_2", 8),
           ("ln2_g_2", 8), ("ln2_b_2", 8), ("conv_ffn_2", 132), ("b_conv_ffn_2", 44)]
COL, NCOL = {}, 0
for _name, _n in COLUMNS:
    COL[_name] = NCOL
    NCOL += _n


CONSTANTS, ALL_CONSTANTS = 15, 33
N_SPLIT = sum(count * pattern.count("S") for _, pattern, count in LAYERS)
N_ROWS = 8
RELEASE = {"S": "parts_ready", "R": "row_product", "A": "accumulated"}

SOLVE_COUNTS = {"at_ready": 1, "solve_masked": 1, "solve_copied": 9, "tt_ready": 5}
SOLVE_WAITS = [
    [("at_ready", 1)],
    [("solve_masked", 1)],
    [("solve_masked", 1)],
    [("solve_copied", 1)],
    [("solve_copied", 2)],
    [("tt_ready", 1)],
    [("solve_copied", 3), ("tt_ready", 1)],
    [("solve_copied", 4)],
    [("solve_copied", 5), ("tt_ready", 2)],
    [("tt_ready", 3)],
    [("tt_ready", 3)],
    [("solve_copied", 7)],
    [("tt_ready", 4)],
    [("tt_ready", 4)],
    [("solve_copied", 9)],
]


def two_blocks(nc, panels, x, ctx_x, columns, c_rows, w_glr, w_gate, w_beta_a, head_rows, rel_bias, out):
    stream, first = plan_stream()
    place = {entry: n for n, entry in enumerate(stream)}

    with ExitStack() as ctx:
        def sb(name, shape, dt=F32, scope=ctx):
            return scope.enter_context(nc.sbuf_tensor(name, shape, dt))

        signals = {}

        def S(name):
            if name not in signals:
                signals[name] = ctx.enter_context(nc.semaphore(name))
            return signals[name]

        PB = ctx.enter_context(nc.psum_tensor("panel_banks", [P, TURNS, 512], F32))
        MB = ctx.enter_context(nc.psum_tensor("work_banks", [P, 4, 512], F32))

        raw = sb("raw", [P, RAW, HALF])
        whi = sb("w_hi", [P, PARTS, HALF], F32R)
        wlo = sb("w_lo", [P, PARTS, HALF], F32R)
        hhi = sb("act_hi", [P, 16, T], F32R)
        hlo = sb("act_lo", [P, 16, T], F32R)
        xt = sb("x_t", [P, KT, T])
        cols = sb("columns", [P, NCOL])
        ident = sb("ident", [P, P])
        ones = sb("ones", [P, T])
        causal_t = sb("causal_t", [P, P])
        causal_dn = sb("causal_dn", [P, P])
        cwide = sb("c_wide", [P, D])
        masks = cwide[:].rearrange("p (a b) -> p a b", a=8)
        m16t = masks[:, 0, :]
        m16 = masks[:, 1, :]
        d32 = masks[:, 2, :]
        d64 = masks[:, 3, :]
        modc = sb("mod_cols", [P, 48, 2])
        mod2 = sb("mod2_cols", [P, 48])
        cact = sb("c_act", [P, 2, 8])
        sc_a = sb("scale_a", [P, 2, 8])
        gcol = sb("gate_cols", [P, 8])
        rs = sb("rs", [P, 512])
        eps = sb("eps", [P, 4])
        dec = sb("g_decay", [P, 8, NCH])
        mod_flat = modc[:].rearrange("p a b -> p (a b)")
        gl_tok = mod_flat[:, 0:48].rearrange("p (a b c) -> p a b c", a=3, b=2)
        gl_end = mod_flat[:, 48:80].rearrange("p (a b) -> p a b", a=DH)
        w_ba = sb("w_beta_a", [P, KT, 16])
        hrow = sb("head_rows", [DH, 2])

        def col(name, i=0, n=1):
            return cols[:, COL[name] + i:COL[name] + i + n]

        def arena(name, size, scope):
            tensor, at = sb(name, [P, size], F32, scope), [0]

            def take(*shape, at_=None):
                n = int(np.prod(shape))
                start = at[0] if at_ is None else at_
                if at_ is None:
                    at[0] += n
                assert start + n <= size, (name, start + n, size)
                names = "abcd"[:len(shape)]
                view = tensor[:, start:start + n]
                if len(shape) > 1:
                    view = view.rearrange(f"p ({' '.join(names)}) -> p {' '.join(names)}",
                                          **{k: v for k, v in zip(names, shape)})
                return view
            take.at = at
            return take

        WORK = 25600
        with ExitStack() as scope:
            take = arena("gla_work", WORK, scope)
            g_q = take(GH, T)
            g_k = take(GH, 2 * T)
            g_v = take(4, D)
            g_r = take(KT, T)
            g_x = take(8, 2 * T)
            g_kt = take(4, 8, P, at_=take.at[0] - 4096)
            e_at = take.at[0]
            g_e1 = take(8, T)
            g_e2 = take(8, T)
            g_e3 = take(8, 2 * T)
            s_at = take.at[0]
            g_s = take(8, GDV)
            g_sc = take(16, P)
            g_o = take(GH, 2, T, at_=s_at)
            wgp = take(8 * P, at_=e_at)[0:32, :]
            glr = take(2 * T, at_=e_at + 1024)[0:32, :]
            wgl = take(KT, 32, at_=e_at + 1536)
            xc = take(KT, T, at_=e_at + 2048)
            sq1 = take(KT, 2 * T, at_=e_at + 4096)
            mod_rows = take(8, 256, at_=GH * T)[0:2]
            h1 = take(KT, 2 * T, at_=s_at)
            g_sq = take(GH, 2, T, at_=e_at + 2048)
            g_rs = take(GH, T, at_=e_at + 4096)
            assert s_at + 4096 <= WORK
        with ExitStack() as scope:
            fhi = sb("hidden_hi", [P, FT, T], F32R, scope)
            flo = sb("hidden_lo", [P, FT, T], F32R, scope)
            take = arena("ffn_work", 14000, scope)
            y1 = take(KT, T)
            sq2 = take(KT, T)
            h2 = take(KT, T)
            f_s = take(2, T)
            f_g = take(2, T)
            y3 = take(KT, T)
            f_u = take(2, 2, T)
            f_out = take(KT, T)
        with ExitStack() as scope:
            take = arena("mix_work", WORK, scope)
            m_at = take.at[0]
            qkv = take(24, T)
            zs = take(KT, T)
            kb = take(DH, T)
            eg = take(DH, T)
            vb = take(2, D)
            kd = take(2, D)
            dm = kd.rearrange("p a (b c) -> p (a b) c", c=P)
            rs2 = vb.rearrange("p a b -> p (a b)")
            qkt = take(16, P)
            tt_ = take(16, P)
            t_at = take.at[0]
            s_n, s_nt, s_b32, s_b64, s_u = (take(8, P) for _ in range(5))
            s_t = s_nt
            sq3 = take(16, T, at_=t_at)
            h3 = take(KT, T, at_=m_at + 10240)
            cy = take(2, 2, T, at_=m_at + 12288)
            st = take(DH, P, at_=t_at)
            rr = take(D, at_=t_at + 1024)
            vn = take(D, at_=t_at + 2048)
            sel = take(DH, P, at_=t_at)[0:DH]
            hm = take(8, T, at_=m_at + 16384)[0:DH]
            vt_ = qkv[:, 16:24, :]
            od = take(DH, T, at_=m_at + 4096)
            odq = take(DH, T, at_=m_at)
            bq = take(KT, T, at_=m_at)
            bk = take(KT, T, at_=m_at + 2048)
            bv = take(2, D, at_=m_at + 4096)
            bx = take(BH, T, at_=m_at + 8192)
            bp = take(2, 384, at_=m_at + 12288)
            bpt = take(2, 384, at_=m_at + 13056)
            bst = take(2, 8, at_=m_at + 13824)
            ga = take(16, T, at_=m_at + 14336)
            ya = take(KT, T, at_=m_at + 18432)
            yb = take(KT, T, at_=m_at + 20480)
            ob = take(KT, T, at_=m_at + 22528)

        block = ctx.enter_context(nc.Block())

        @block.sync
        def _(sp):
            for u in range(2 * len(stream)):
                if u >= RAW:
                    kind, i = stream[(u - RAW) // 2]
                    sp.wait_ge(S(RELEASE[kind]), 2 * i + u % 2 + 1)
                sp.dma_start(raw[:, u % RAW], panels[u // 2][:, u % 2 * HALF:u % 2 * HALF + HALF])\
                    .then_inc(S(f"landed{u % RAW}"), 16)
            sp.wait_ge(S("out_ready"), 1)
            sp.dma_start(out, f_out).then_inc(S("out_stored"), 16)
            sp.wait_ge(S("out_stored"), 16)

        @block.gpsimd
        def _(pool):
            made = [0]

            def step(ins):
                made[0] += 1
                ins.then_inc(S("constants"), 1)
                pool.wait_ge(S("constants"), made[0])

            def keep(t, compare, base, pattern, cm, fill=0.0):
                step(pool.affine_select(out=t, in_=t, compare_op=compare, fill=fill, base=base,
                                        pattern=pattern, channel_multiplier=cm))

            def same_block(t, size):
                v = t.rearrange("p (b c) -> p b c", c=size)
                keep(v, ALU.is_ge, 0, [[-size, P // size], [0, size]], 1)
                keep(v, ALU.is_ge, size - 1, [[size, P // size], [0, size]], -1)

            step(pool.memset(ones[:], 1.0))
            step(pool.memset(ident[:], 0.0))
            keep(ident[:], ALU.not_equal, 0, [[-1, P]], 1, 1.0)

            def make_masks(which):
                for t, base, pattern, cm, size in which:
                    step(pool.memset(t, 1.0))
                    same_block(t, size)
                    if pattern:
                        keep(t, ALU.is_ge, base, pattern, cm)
                    else:
                        v = t.rearrange("p (b c) -> p b c", c=size)
                        keep(v, ALU.is_ge, -(size // 2), [[-size, P // size], [0, size]], 1)
                        keep(v, ALU.is_ge, size // 2 - 1, [[0, P // size], [-1, size]], 0)

            make_masks([(causal_t[:], 0, [[1, P]], -1, 64), (causal_dn[:], 0, [[-1, P]], 1, 64)])
            step(pool.memset(eps[:, 0:1], EPS_RMS))
            step(pool.memset(eps[:, 1:2], EPS_LN))
            step(pool.memset(eps[:, 2:3], 1.0))
            step(pool.memset(wgp, 0.0))
            assert made[0] == CONSTANTS, made[0]
            for d in range(2):
                pool.dma_start(wgp[16 * d:16 * d + 16, 512 * d:512 * d + 512], w_gate[d])\
                    .then_inc(S("gate_w_landed"), 16)
            pool.wait_ge(S("h1_lo"), 1)
            pool.wait_ge(S("glr_sum"), 1)
            pool.memset(g_sc, 0.0).then_inc(S("scores_zeroed"), 1)
            pool.wait_ge(S("accumulated"), 80)
            make_masks([(m16t, -1, [[1, P]], -1, 16), (m16, -1, [[-1, P]], 1, 16),
                        (d32, 0, None, 0, 32), (d64, 0, None, 0, 64)])
            assert made[0] == ALL_CONSTANTS, made[0]
            pool.wait_ge(S("qk_sums"), 2)
            pool.memset(sel, 1.0).then_inc(S("selectors"), 1)
            pool.wait_ge(S("selectors"), 1)
            pool.affine_select(out=sel, in_=sel, compare_op=ALU.is_equal, fill=0.0, base=0,
                               pattern=[[-1, DH], [0, P]], channel_multiplier=1).then_inc(S("selectors"), 1)

        @block.tensor
        def _(pe):
            split = [0]
            turn = [0]

            def parts_of(j, k):
                s = (2 * j + k // 4) % PARTS
                return whi[:, s], wlo[:, s]

            def open_half(j, h):
                pe.wait_ge(S("parts_ready"), 2 * j + h + 1)

            def take_turn():
                t = turn[0]
                turn[0] += 1
                if t >= TURNS:
                    pe.wait_ge(S("panel_evacuated"), t - TURNS + 1)
                return t % TURNS

            def three_pass(out_, weights, moving, start, stop):
                (a_hi, a_lo), (b_hi, b_lo) = weights, moving
                for p, (a, b) in enumerate(((a_hi, b_hi), (a_hi, b_lo), (a_lo, b_hi))):
                    ins = pe.matmul(out_, a, b, start=start and p == 0, stop=stop and p == 2,
                                    skip_group_check=True)
                return ins

            def panel(j, x_unit, nf=1):
                b = [take_turn() for _ in range(nf)]
                for h in range(2):
                    open_half(j, h)
                    for m in range(2):
                        o = PB[:, b[m], :] if nf == 2 else PB[:, b[0], m * T:m * T + T]
                        for k in range(4 * h, 4 * h + 4):
                            w0 = k % 4 * 256 + m * P
                            ins = three_pass(o, tuple(w[:, w0:w0 + P] for w in parts_of(j, k)),
                                             tuple(v[:, x_unit(k):x_unit(k) + nf, :] for v in (hhi, hlo)),
                                             start=(k == 0 and (nf == 2 or m == 0)), stop=(k == KT - 1))
                    ins.then_inc(S("multiplied"), 1)

            def token_panel(j, x_unit, tiles):
                b = [take_turn() for _ in range(len(tiles) // 2)]
                for h in range(2):
                    open_half(j, h)
                    for n, (unit, t0) in enumerate(tiles):
                        for k in range(4 * h, 4 * h + 4):
                            ins = three_pass(PB[:, b[n // 2], (n % 2) * 256:(n % 2) * 256 + 256],
                                             tuple(v[:, x_unit(k) + unit, t0:t0 + P] for v in (hhi, hlo)),
                                             tuple(w[:, k % 4 * 256:k % 4 * 256 + 256] for w in parts_of(j, k)),
                                             start=(k == 0 and n % 2 == 0), stop=(k == KT - 1))
                    ins.then_inc(S("multiplied"), 1)

            def row_product(a):
                if a >= TURNS:
                    pe.wait_ge(S("rows_read"), a - TURNS + 1)
                for h in range(2):
                    u = 2 * place[("R", a)] + h
                    pe.wait_ge(S(f"landed{u % RAW}"), 16 * (u // RAW + 1))
                    for k in range(4):
                        ins = pe.matmul(PB[0:2, a % TURNS, 0:256], cact[:, 0:2, 4 * h + k],
                                        raw[:, u % RAW, k * 256:k * 256 + 256],
                                        start=(h == 0 and k == 0), stop=(h == 1 and k == 3))
                    ins.then_inc(S("row_product"), 1)

            def turn_rows(a):
                pe.wait_ge(S("rows_read"), a + 1)
                for m in range(2):
                    f = 2 * a + m
                    ins = pe.transpose(MB[:, 1, 2 * f:2 * f + 2], mod_rows[:, a, m * P:m * P + P], ident[0:2, 0:2])
                if a == N_ROWS - 1:
                    ins.then_inc(S("rows_turned"), 1)

            def sum_tiles(out_, tiles, name):
                for n, tile in enumerate(tiles):
                    ins = pe.matmul(out_, ones[:, 0:P], tile, start=(n == 0), stop=(n == len(tiles) - 1))
                ins.then_inc(S(name), 1)

            pe.wait_ge(S("constants"), CONSTANTS)
            pe.wait_ge(S("squares"), 1)
            sum_tiles(MB[:, 0, :], [sq1[:, k, :] for k in range(KT)], "norm_sum")
            pe.wait_ge(S("c_ready"), 1)
            for a in range(N_ROWS):
                row_product(a)
                if a:
                    turn_rows(a - 1)
            turn_rows(N_ROWS - 1)
            pe.wait_ge(S("wgl_landed"), 16)
            pe.wait_ge(S("h1_ready"), 1)
            pe.wait_ge(S("norm_factor"), 1)
            for k in range(KT):
                ins = pe.matmul(MB[0:32, 0, :], wgl[:, k, :], h1[:, k, :], start=(k == 0), stop=(k == KT - 1))
            ins.then_inc(S("glr_sum"), 1)
            pe.wait_ge(S("h1_lo"), 1)
            pair = lambda k: 2 * k
            j = 0
            panel(j, pair, 2)
            j += 1
            pe.wait_ge(S("gate_w_landed"), 32)
            pe.wait_ge(S("glr_ready"), 1)
            for i in range(8):
                if i >= 3:
                    pe.wait_ge(S("gate_biased"), i - 2)
                pe.matmul(MB[:, i % 3, :], wgp[:, i * P:i * P + P], glr, start=True, stop=True)\
                    .then_inc(S("gate_sum"), 1)
            panel(j, pair, 2)
            j += 1
            for _ in range(4):
                token_panel(j, pair, [(0, 0), (0, P), (1, 0), (1, P)])
                j += 1
            for _ in range(6):
                panel(j, pair)
                j += 1
            pe.wait_ge(S("gate_biased"), 8)
            pe.wait_ge(S("keys_decayed"), 1)
            for d in range(2):
                for t in range(2):
                    for h in range(GH):
                        ins = pe.matmul(MB[:, d * 2 + t, h * P:h * P + P], g_e2[:, d * 4 + h, t * P:t * P + P],
                                        g_e1[:, d * 4 + h, t * P:t * P + P], start=True, stop=True)
                    ins.then_inc(S("scores"), 1)
            pe.wait_ge(S("end_keys"), 1)
            for n in range(8):
                t, half = (2, 3, 0, 1)[n // 2], n % 2
                if n < 4:
                    pe.wait_ge(S("scores_masked"), n + 1)
                else:
                    pe.wait_ge(S("keys_turned"), n - 3)
                for i in range(4):
                    ins = pe.transpose(MB[:, n % 4, i * P:i * P + P],
                                       g_e3[:, half * 4 + i, t * P:t * P + P], ident[:])
                ins.then_inc(S("keys_transposed"), 1)
            pe.wait_ge(S("panel_evacuated"), 18)
            for h in range(GH):
                begun = False
                for t in range(2):
                    for v in range(2):
                        for d in range(2):
                            pe.matmul(PB[:, h, v * T + t * P:v * T + t * P + P],
                                      g_v[:, t, h * GDV + v * P:h * GDV + v * P + P],
                                      g_sc[:, (d * 2 + t) * 4 + h, :], start=not begun, stop=False,
                                      skip_group_check=True)
                            begun = True
            pe.wait_ge(S("keys_turned"), 8)
            for i in range(8):
                for t in (2, 3):
                    ins = pe.matmul(MB[:, i // 2, (i % 2) * 256:(i % 2) * 256 + 256], g_kt[:, t, i, :],
                                    g_v[:, t, (i % 4) * GDV:(i % 4) * GDV + GDV], start=(t == 2), stop=(t == 3))
                ins.then_inc(S("state_sum"), 1)
            for s in range(NCH):
                for i in range(8):
                    d, h = i // 4, i % 4
                    c = s if d == 0 else NCH - 1 - s
                    pe.wait_ge(S("state_new"), 8 * s + i // 2 * 2 + 2)
                    for v in range(2):
                        ins = pe.matmul(PB[:, h, v * T + c * CHUNK:v * T + c * CHUNK + CHUNK],
                                        g_s[:, i, v * P:v * P + P], g_e1[:, i, c * CHUNK:c * CHUNK + CHUNK],
                                        start=False, stop=(s == NCH - 1 and d == 1), skip_group_check=True)
                    if s < NCH - 1:
                        p0 = CHUNK * (c % 2)
                        ins = pe.matmul(MB[:, i // 2, (i % 2) * 256:(i % 2) * 256 + 256],
                                        g_kt[p0:p0 + CHUNK, c // 2, i, :],
                                        g_v[p0:p0 + CHUNK, c // 2, h * GDV:h * GDV + GDV], start=True, stop=True)
                        ins.then_inc(S("state_sum"), 1)
                    else:
                        ins.then_inc(S("gla_done"), 1)
            pe.wait_ge(S("gla_squares"), 1)
            for h in range(GH):
                for v in range(2):
                    ins = pe.matmul(MB[:, h // 2, (h % 2) * T:(h % 2) * T + T], ones[:, 0:P], g_sq[:, h, v, :],
                                    start=(v == 0), stop=(v == 1))
            ins.then_inc(S("gla_norm_sum"), 1)
            pe.wait_ge(S("gla_lo"), 1)
            single = lambda k: k
            turn[0] = first["gla_out"][1]
            for n in range(4):
                if n == 0:
                    pe.wait_ge(S("gla_read"), 4)
                panel(j, single)
                j += 1

            def norm(count):
                pe.wait_ge(S("squares"), count)
                sum_tiles(MB[:, 0, 0:T], [sq2[:, k, :] for k in range(KT)], "norm_sum")

            norm(2)
            norm(3)
            pe.wait_ge(S("h2_lo"), 1)
            for i in range(22):
                panel(j, single)
                j += 1

            def project_hidden(j, first_turn, name):
                turn[0] = first_turn
                banks = [take_turn() for _ in range(4)]
                for i in range(11):
                    for h in range(2):
                        f = 2 * i + h
                        open_half(j, h)
                        pe.wait_ge(S(name), f + 1)
                        for m in range(KT):
                            ins = three_pass(PB[:, banks[m // 2], (m % 2) * T:(m % 2) * T + T],
                                             tuple(w[:, m * P:m * P + P] for w in parts_of(j, 4 * h)),
                                             (fhi[:, f, :], flo[:, f, :]),
                                             start=(f == 0 and m % 2 == 0), stop=(f == FT - 1))
                        ins.then_inc(S("multiplied"), 1)
                    j += 1
                return j

            j = project_hidden(j, first["ffn_out"][1], "hidden_lo")
            norm(4)

            pe.wait_ge(S("h3_ready"), 1)
            pe.wait_ge(S("small_landed"), 32)
            pe.wait_ge(S("norm_factor"), 4)
            for part in range(2):
                for k in range(KT):
                    ins = pe.matmul(MB[0:DH, 0, part * T:part * T + T], w_ba[:, k, part * 8:part * 8 + 8],
                                    h3[:, k, :], start=(k == 0), stop=(k == KT - 1))
            ins.then_inc(S("beta_a_sum"), 1)
            pe.wait_ge(S("h3_lo"), 1)
            for _ in range(16):
                panel(j, single)
                j += 1
            for part in range(2):
                pe.wait_ge(S("qk_squares"), part + 1)
                pe.wait_ge(S("rows_ready"), 1)
                if part:
                    pe.wait_ge(S("qk_factor"), 1)
                for b in range(4):
                    ins = pe.matmul(MB[:, b, :], ones[:, 0:P], sq3[:, part * 8 + 2 * b:part * 8 + 2 * b + 2, :],
                                    start=True, stop=True)
                ins.then_inc(S("qk_sums"), 1)
            pe.wait_ge(S("selectors"), 2)
            pe.wait_ge(S("rows_ready"), 2)
            pe.wait_ge(S("rows_act"), 3)
            pe.wait_ge(S("qk_factor"), 2)
            for n, row in enumerate((2, 0, 3)):
                for t in range(2):
                    ins = pe.transpose(MB[:, 0, (n * 2 + t) * DH:(n * 2 + t) * DH + DH],
                                       hm[:, row, t * P:t * P + P], ident[0:DH, 0:DH])
            ins.then_inc(S("tok_rows"), 1)
            pe.wait_ge(S("tok_ready"), 1)
            for n, row in enumerate((2, 0)):
                if n:
                    pe.wait_ge(S("decay_diff"), 1)
                    pe.wait_ge(S("eg_ready"), 1)
                for h in range(DH):
                    ins = pe.matmul(MB[:, h // 2, (h % 2) * T:(h % 2) * T + T], sel[:, h, :], hm[:, row, :],
                                    start=True, stop=True)
                ins.then_inc(S("rows_spread"), 1)
            pe.wait_ge(S("kb_ready"), 1)

            steps = [("A", None, s_u), ("N2", s_nt, s_n), ("N2T", s_n, s_nt), ("T2", s_n, None), ("N4", s_nt, s_n),
                     ("N4T", s_n, s_nt), ("T4", s_n, None), ("N8", s_nt, s_n), ("T8", s_n, None),
                     ("T", None, None), ("U", s_b32, None), ("W", s_t, s_u), ("T", None, None),
                     ("U", s_b64, None), ("W", s_t, s_u)]
            for t in range(2):
                if t:
                    pe.wait_ge(S("tt_ready"), 5)
                    pe.wait_ge(S("solve_copied"), 9)
                for h in range(DH):
                    for n, rhs in enumerate((qkv, kb)):
                        ins = pe.matmul(MB[:, h // 2, (h % 2) * 256 + n * P:(h % 2) * 256 + n * P + P],
                                        qkv[:, 8 + h, t * P:t * P + P], rhs[:, h, t * P:t * P + P],
                                        start=True, stop=True)
                ins.then_inc(S("qk_products"), 1)
                tt_of = lambda m: tt_[:, 8 * t + m, :]
                for p, (name, lhs, rhs) in enumerate(steps):
                    for sem, count in SOLVE_WAITS[p]:
                        pe.wait_ge(S(sem), count + t * SOLVE_COUNTS[sem])
                    bank = 2 * (p % 2)
                    for m in range(8):
                        o = MB[:, bank + m // 4, (m % 4) * P:(m % 4) * P + P]
                        if lhs is None:
                            ins = pe.transpose(o, s_u[:, m, :] if name == "A" else tt_of(m), ident[:])
                        else:
                            ins = pe.matmul(o, lhs[:, m, :], tt_of(m) if rhs is None else rhs[:, m, :],
                                            start=True, stop=True)
                    ins.then_inc(S("solve_product"), 1)
            pe.wait_ge(S("tt_ready"), 10)
            pe.wait_ge(S("solve_copied"), 18)
            for n, base in enumerate((16, 8)):
                for t in range(2):
                    b0 = 2 * (t % 2)
                    if n:
                        pe.wait_ge(S("tok_major"), t + 1)
                    for h in range(DH):
                        ins = pe.transpose(MB[:, b0 + h // 4, (h % 4) * P:(h % 4) * P + P],
                                           qkv[:, base + h, t * P:t * P + P], ident[:])
                    ins.then_inc(S("vk_turned"), 1)
            pe.wait_ge(S("panel_evacuated"), 64)
            pe.wait_ge(S("tok_major"), 4)
            for c in range(NCH):
                p0, t = CHUNK * (c % 2), c // 2
                rows = slice(p0, p0 + CHUNK)
                cs = slice(c * CHUNK, c * CHUNK + CHUNK)
                if c:
                    pe.wait_ge(S("delta_state"), c)
                    for h in range(DH):
                        ins = pe.matmul(MB[rows, h // 4, (h % 4) * P:(h % 4) * P + P], kb[:, h, cs], st[:, h, :],
                                        start=True, stop=True)
                    ins.then_inc(S("predicted"), 1)
                pe.wait_ge(S("rhs_ready"), c + 1)
                for h in range(DH):
                    ins = pe.matmul(MB[rows, 2 + h // 4, (h % 4) * P:(h % 4) * P + P],
                                    tt_[rows, 8 * t + h, p0:p0 + CHUNK], rr[rows, h * P:h * P + P],
                                    start=True, stop=True)
                ins.then_inc(S("corrected"), 1)
                pe.wait_ge(S("v_new"), c + 1)
                for h in range(DH):
                    o = PB[:, h // 2, (h % 2) * T + c * CHUNK:(h % 2) * T + c * CHUNK + CHUNK]
                    if c:
                        pe.matmul(o, st[:, h, :], eg[:, h, cs], start=True, stop=False)
                    ins = pe.matmul(o, vn[rows, h * P:h * P + P], qkt[rows, 8 * t + h, p0:p0 + CHUNK],
                                    start=(c == 0), stop=True)
                ins.then_inc(S("delta_out"), 1)
                if c < NCH - 1:
                    for h in range(DH):
                        ins = pe.matmul(MB[:, h // 4, (h % 4) * P:(h % 4) * P + P], kd[rows, t, h * P:h * P + P],
                                        vn[rows, h * P:h * P + P], start=True, stop=True)
                    ins.then_inc(S("state_step"), 1)
            pe.wait_ge(S("delta_squares"), 1)
            for b in range(4):
                ins = pe.matmul(MB[:, b, :], ones[:, 0:P], odq[:, 2 * b:2 * b + 2, :], start=True, stop=True)
            ins.then_inc(S("delta_norm_sum"), 1)
            turn[0] = first["band_q"][1]
            pe.wait_ge(S("delta_read"), 1)
            for _ in range(8):
                panel(j, single)
                j += 1
            for _ in range(4):
                token_panel(j, single, [(0, 0), (0, P)])
                j += 1
            pe.wait_ge(S("delta_factor"), 1)
            pe.wait_ge(S("panel_evacuated"), 76)

            def band_scores(h):
                r = slice(BDH * (h % 2), BDH * (h % 2) + BDH)
                if h >= 2:
                    pe.wait_ge(S("band_shifted"), 2 * (h - 1))
                pe.matmul(MB[:, h % 2, 0:P], bq[r, h // 2, 0:P], bk[r, h // 2, 0:P], start=True, stop=True)
                pe.matmul(MB[:, h % 2, P:384], bq[r, h // 2, P:T], bk[r, h // 2, :], start=True, stop=True)\
                    .then_inc(S("band_scores"), 1)

            def band_values(h):
                pe.wait_ge(S("band_probs"), h + 1)
                if h >= 2:
                    pe.wait_ge(S("probs_turned"), h - 1)
                for n in range(3):
                    ins = pe.transpose(MB[:, 2 + h % 2, (0, P, 256)[n]:(0, P, 256)[n] + P],
                                       bp[:, h % 2, n * P:n * P + P], ident[:])
                ins.then_inc(S("probs_transposed"), 1)

            def band_out(h):
                pe.wait_ge(S("probs_turned"), h + 1)
                r = slice(BDH * (h % 2), BDH * (h % 2) + BDH)
                o = PB[r, h // 4, (h // 2 % 2) * T:(h // 2 % 2) * T + T]
                vcols = slice(h * BDH, h * BDH + BDH)
                pe.matmul(o[:, P:T], bv[:, 1, vcols], bpt[:, h % 2, 256:384], start=True, stop=True)
                pe.matmul(o, bv[:, 0, vcols], bpt[:, h % 2, 0:T], start=False, stop=True,
                          skip_group_check=True).then_inc(S("band_out"), 1)

            band_scores(0)
            band_scores(1)
            for h in range(BH):
                band_values(h)
                if h + 2 < BH:
                    band_scores(h + 2)
                band_out(h)
            turn[0] = first["gates"][1]
            pe.wait_ge(S("band_read"), 1)
            for _ in range(8):
                panel(j, single)
                j += 1
            pe.wait_ge(S("oa_lo"), 1)
            upper = lambda k: 8 + k
            for _ in range(4):
                panel(j, upper)
                j += 1
            pe.wait_ge(S("ob_lo"), 1)
            for _ in range(4):
                panel(j, single)
                j += 1
            pe.wait_ge(S("merged_lo"), 1)
            for _ in range(4):
                panel(j, upper)
                j += 1

            def layer_norm(count):
                pe.wait_ge(S("ln_in"), count)
                sum_tiles(MB[:, 0, 0:T], [y3[:, k, :] for k in range(KT)], "ln_sum")
                pe.wait_ge(S("ln_squares"), count)
                sum_tiles(MB[:, 1, 0:T], [sq2[:, k, :] for k in range(KT)], "ln_var")

            layer_norm(1)
            pe.wait_ge(S("h4_lo"), 1)
            for i in range(22):
                panel(j, single)
                j += 1
            j = project_hidden(j, first["down"][1], "hidden2_lo")
            layer_norm(2)
            assert j == N_SPLIT

        @block.scalar
        def _(act):
            def exp_table():
                act.preload_act_table_set("natural_log_exp_and_others")

            act.dma_start(xt[:], x).then_inc(S("x_landed"), 16)
            act.dma_start(cols[:], columns).then_inc(S("x_landed"), 16)
            act.dma_start(xc, ctx_x).then_inc(S("x_landed"), 16)
            act.dma_start(cwide[:], bass.AP(c_rows.tensor, 0, [[0, P], [1, D]])).then_inc(S("c_landed"), 16)
            act.dma_start(wgl, w_glr).then_inc(S("wgl_landed"), 16)
            act.dma_start(w_ba[:], w_beta_a).then_inc(S("small_landed"), 16)
            act.dma_start(hrow[:], head_rows).then_inc(S("small_landed"), 16)

            done = [0]
            steps = [0]

            def then(ins):
                steps[0] += 1
                ins.then_inc(S("act_step"), 1)
                act.wait_ge(S("act_step"), steps[0])

            def upper_half(v):
                while done[0] <= min(v, 2 * N_SPLIT - 1):
                    v_, (j, h) = done[0], divmod(done[0], 2)
                    u = 2 * place[("S", j)] + h
                    act.wait_ge(S(f"landed{u % RAW}"), 16 * (u // RAW + 1))
                    if v_ >= PARTS:
                        act.wait_ge(S("multiplied"), v_ - PARTS + 1)
                    act.activation(whi[:, v_ % PARTS, :], raw[:, u % RAW, :], ACT.Copy)\
                        .then_inc(S("upper_ready"), 1)
                    done[0] += 1

            def upper_parts(j):
                upper_half(2 * j + 1)

            def product(j):
                upper_half(2 * j + 4)
                act.wait_ge(S("multiplied"), 2 * j + 2)

            def factor(out_, sums, n, which, name):
                exp_table()
                then(act.activation(out_, sums, ACT.Ln, scale=1.0 / n, bias=eps[:, which:which + 1]))
                act.activation(out_, out_, ACT.Exp, scale=-0.5).then_inc(S(name), 1)

            def widen_c(n):
                act.wait_ge(S("c_landed"), 16 * n)
                act.activation(cwide[:], cwide[:], ACT.Silu).then_inc(S("c_wide"), 1)

            act.wait_ge(S("x_landed"), 48)
            act.wait_ge(S("constants"), CONSTANTS)
            act.activation(sq1[:, :, 0:T], xt[:], ACT.Square)
            act.activation(sq1[:, :, T:2 * T], xc, ACT.Square).then_inc(S("squares"), 1)
            act.activation(cact[:].rearrange("p a b -> p (a b)"), cols[:, 0:16], ACT.Silu).then_inc(S("c_ready"), 1)
            act.wait_ge(S("norm_sum"), 1)
            factor(rs[:], MB[:, 0, :], D, 0, "norm_factor")
            for a in range(N_ROWS):
                act.wait_ge(S("row_product"), 2 * a + 2)
                act.activation(mod_rows[:, a, :], PB[0:2, a % TURNS, 0:256], ACT.Copy).then_inc(S("rows_read"), 1)
            for k in range(KT):
                for s in range(2):
                    act.wait_ge(S("h1_scaled"), 2 * k + s + 1)
                    o = h1[:, k, s * T:s * T + T]
                    ins = act.activation(o, o, ACT.Identity, bias=modc[:, k, s:s + 1])
            ins.then_inc(S("h1_ready"), 1)
            act.wait_ge(S("h1_ready"), 1)
            act.activation(hhi[:].rearrange("p a b -> p (a b)"), h1.rearrange("p a b -> p (a b)"), ACT.Copy)\
                .then_inc(S("h1_hi"), 1)
            widen_c(1)
            upper_parts(1)
            j = 0
            for i in range(2):
                product(j)
                for m in range(2):
                    act.activation(g_k[:, 2 * i + m, :], PB[:, (2 * j + m) % TURNS, :], ACT.Copy)\
                        .then_inc(S("panel_evacuated"), 1)
                upper_parts(j + 2)
                j += 1
            for i in range(4):
                product(j)
                for m in range(2):
                    act.activation(g_v[:, 2 * m:2 * m + 2, i * GDV:i * GDV + GDV],
                                   PB[:, (2 * j + m) % TURNS, :].rearrange("p (a b) -> p a b", a=2), ACT.Copy)\
                        .then_inc(S("panel_evacuated"), 1)
                upper_parts(j + 2)
                j += 1
            act.wait_ge(S("gate_biased"), 8)
            exp_table()
            then(act.activation(g_e3, g_x, ACT.Abs))
            then(act.activation(g_e3, g_e3, ACT.Exp, scale=-1.0))
            act.activation(g_e3, g_e3, ACT.Ln, bias=eps[:, 2:3]).then_inc(S("gate_soft"), 1)
            turn = first["gla_q"][1]

            def bank():
                nonlocal turn
                turn += 1
                return PB[:, (turn - 1) % TURNS, :]

            def pair(b):
                return b.rearrange("p (a b) -> p a b", a=2)

            for dst, func in ((g_q, ACT.Copy), (g_r, ACT.Silu)):
                for i in range(dst.shape[1] // 2):
                    product(j)
                    act.activation(dst[:, 2 * i:2 * i + 2, :], pair(bank()), func).then_inc(S("panel_evacuated"), 1)
                    upper_parts(j + 2)
                    j += 1
            exp_table()
            act.wait_ge(S("cumulated"), 1)
            act.activation(g_e1, g_x[:, :, 0:T], ACT.Exp, scale=1 / 16).then_inc(S("gate_exp"), 1)
            act.activation(g_e2, g_x[:, :, 0:T], ACT.Exp, scale=-1 / 16).then_inc(S("gate_exp"), 1)
            act.wait_ge(S("end_diff"), 1)
            act.activation(g_e3, g_e3, ACT.Exp, scale=1 / 16).then_inc(S("gate_exp"), 1)
            for n in range(8):
                t, half = (2, 3, 0, 1)[n // 2], n % 2
                act.wait_ge(S("keys_transposed"), n + 1)
                act.activation(g_kt[:, t, half * 4:half * 4 + 4, :].rearrange("p a b -> p (a b)"),
                               MB[:, n % 4, :], ACT.Copy).then_inc(S("keys_turned"), 1)
            act.wait_ge(S("gla_done"), 8)
            for h in range(GH):
                act.activation(g_o[:, h].rearrange("p a b -> p (a b)"), PB[:, h, :], ACT.Copy)\
                    .then_inc(S("gla_read"), 1)
            act.wait_ge(S("gla_read"), 4)
            act.activation(g_sq, g_o, ACT.Square).then_inc(S("gla_squares"), 1)
            upper_parts(13)
            act.wait_ge(S("gla_norm_sum"), 1)
            factor(g_rs.rearrange("p a b -> p (a b)"), MB[:, 0:2, :].rearrange("p a b -> p (a b)"), GDV, 0,
                   "gla_factor")
            act.wait_ge(S("gla_gated"), 1)
            act.activation(hhi[:, 0:8, :].rearrange("p a b -> p (a b)"),
                           g_o.rearrange("p a b c -> p (a b c)"), ACT.Copy).then_inc(S("gla_hi"), 1)
            for i in range(4):
                product(j)
                act.activation(y1[:, 2 * i:2 * i + 2, :], pair(bank()), ACT.Copy).then_inc(S("panel_evacuated"), 1)
                upper_parts(j + 2)
                j += 1

            def norm(src, count):
                act.activation(sq2, src, ACT.Square).then_inc(S("squares"), 1)
                act.wait_ge(S("norm_sum"), count)
                factor(rs[:, 0:T], MB[:, 0, 0:T], D, 0, "norm_factor")

            def flat(v):
                return v.rearrange("p a b -> p (a b)")

            act.wait_ge(S("accumulated"), 32)
            act.dma_start(cwide[:], bass.AP(c_rows.tensor, D, [[0, P], [1, D]])).then_inc(S("c_landed"), 16)
            act.wait_ge(S("panel_evacuated"), 22)
            norm(y1, 2)
            act.wait_ge(S("x_new"), 1)
            norm(xt[:], 3)
            for k in range(KT):
                act.wait_ge(S("h2_scaled"), k + 1)
                ins = act.activation(h2[:, k, :], h2[:, k, :], ACT.Identity, bias=modc[:, 24 + k, 0:1])
            ins.then_inc(S("h2_ready"), 1)
            act.wait_ge(S("h2_ready"), 1)
            act.activation(flat(hhi[:, 0:8, :]), flat(h2), ACT.Copy).then_inc(S("h2_hi"), 1)

            widen_c(2)

            def hidden_upper(i, name):
                act.wait_ge(S(name), i + 1)
                act.activation(fhi[:, i, :], f_g[:, i % 2, :], ACT.Copy).then_inc(S("panel_evacuated"), 1)

            for i in range(22):
                product(j)
                act.activation(f_s[:, i % 2, :], bank()[:, 0:T], ACT.Silu).then_inc(S("hidden_silu"), 1)
                upper_parts(j + 2)
                if i:
                    hidden_upper(i - 1, "hidden_gated")
                j += 1
            hidden_upper(21, "hidden_gated")
            for i in range(11):
                upper_parts(j + 2)
                j += 1
            act.wait_ge(S("multiplied"), 2 * j)
            for r in range(4):
                act.activation(y1[:, 2 * r:2 * r + 2, :], pair(bank()), ACT.Copy).then_inc(S("panel_evacuated"), 1)
            act.wait_ge(S("panel_evacuated"), turn)
            norm(y1, 4)

            act.wait_ge(S("h3_ready"), 1)
            act.activation(flat(hhi[:, 0:8, :]), flat(h3), ACT.Copy).then_inc(S("h3_hi"), 1)
            act.wait_ge(S("beta_a_sum"), 1)
            act.activation(hm[:, 0, :], MB[0:DH, 0, 0:T], ACT.Sigmoid).then_inc(S("rows_act"), 1)
            act.wait_ge(S("rows_ready"), 1)
            exp_table()
            then(act.activation(hm[:, 4, :], hm[:, 1, :], ACT.Abs))
            then(act.activation(hm[:, 4, :], hm[:, 4, :], ACT.Exp, scale=-1.0))
            act.activation(hm[:, 4, :], hm[:, 4, :], ACT.Ln, bias=eps[0:DH, 2:3])
            act.activation(hrow[:, 0:1], hrow[:, 0:1], ACT.Exp).then_inc(S("rows_act"), 1)
            act.wait_ge(S("rows_ready"), 2)
            act.activation(hm[:, 3, :], hm[:, 5, :], ACT.Exp).then_inc(S("rows_act"), 1)
            for i in range(12):
                product(j)
                b = bank()
                for m in range(2):
                    ins = act.activation(cy[:, i % 2, m, :], b[:, m * T:m * T + T], ACT.Identity,
                                         scale=col("conv_a_2", 72 + 2 * i + m))
                ins.then_inc(S("conv_begun"), 1)
                upper_parts(j + 2)
                act.wait_ge(S("conv_done"), i + 1)
                act.activation(qkv[:, 2 * i:2 * i + 2, :], cy[:, i % 2, :, :], ACT.Silu)\
                    .then_inc(S("panel_evacuated"), 1)
                j += 1
            for i in range(4):
                product(j)
                act.activation(zs[:, 2 * i:2 * i + 2, :], pair(bank()), ACT.Silu).then_inc(S("panel_evacuated"), 1)
                upper_parts(j + 2)
                j += 1
            act.wait_ge(S("panel_evacuated"), turn)
            act.activation(sq3[:, 0:8, :], qkv[:, 0:8, :], ACT.Square).then_inc(S("qk_squares"), 1)
            act.activation(sq3[:, 8:16, :], qkv[:, 8:16, :], ACT.Square).then_inc(S("qk_squares"), 1)
            all_banks = MB[:].rearrange("p a b -> p (a b)")
            act.wait_ge(S("qk_sums"), 1)
            factor(rs2, all_banks, 1, 0, "qk_factor")
            act.wait_ge(S("qk_sums"), 2)
            act.wait_ge(S("qk_normed"), 1)
            factor(rs2, all_banks, 1, 0, "qk_factor")
            act.wait_ge(S("rows_spread"), 1)
            act.activation(flat(eg), all_banks, ACT.Exp).then_inc(S("eg_ready"), 1)
            act.wait_ge(S("decay_diff"), 1)
            act.activation(dm, dm, ACT.Exp).then_inc(S("decay_exp"), 1)
            for t in range(2):
                for p, dst, ready in ((1, s_n, 3), (2, s_nt, 3), (4, s_n, 6), (5, s_nt, 6), (7, s_n, 8),
                                      (9, s_t, 10), (10, s_u, 11), (12, s_t, 13), (13, s_u, 14)):
                    act.wait_ge(S("solve_product"), 15 * t + ready)
                    b0 = 2 * (p % 2)
                    act.activation(flat(dst), flat(MB[:, b0:b0 + 2, :]), ACT.Copy).then_inc(S("solve_copied"), 1)
            for c in range(NCH):
                rows = slice(CHUNK * (c % 2), CHUNK * (c % 2) + CHUNK)
                act.wait_ge(S("corrected"), c + 1)
                act.activation(vn[rows, :], flat(MB[rows, 2:4, :]), ACT.Copy).then_inc(S("v_new"), 1)
            act.wait_ge(S("delta_out"), 4)
            act.activation(flat(od), PB[:].rearrange("p a b -> p (a b)"), ACT.Copy).then_inc(S("delta_read"), 1)
            act.wait_ge(S("delta_read"), 1)
            act.activation(odq, od, ACT.Square).then_inc(S("delta_squares"), 1)
            act.wait_ge(S("delta_norm_sum"), 1)
            factor(rs2, all_banks, DDK, 0, "delta_factor")
            act.wait_ge(S("band_masked"), 1)
            src = bass.AP(rel_bias.tensor, 0, [[1, 64], [REL, BH], [1, T]])
            act.dma_start(bx[64:128, :, :], src).then_inc(S("bias_landed"), 16)
            src = bass.AP(rel_bias.tensor, 0, [[1, 64], [REL, BH], [1, T - 64]])
            act.dma_start(bx[0:64, :, 64:T], src).then_inc(S("bias_landed"), 16)
            act.wait_ge(S("delta_gated"), 1)
            act.activation(flat(hhi[:, 8:16, :]), flat(od), ACT.Copy).then_inc(S("oa_hi"), 1)
            for dst, scale in ((bq, BDH ** -0.5), (bk, 1.0)):
                for i in range(4):
                    product(j)
                    act.activation(dst[:, 2 * i:2 * i + 2, :], pair(bank()), ACT.Copy, scale=scale)\
                        .then_inc(S("panel_evacuated"), 1)
                    upper_parts(j + 2)
                    j += 1
            act.wait_ge(S("oa_lo"), 1)
            for i in range(4):
                product(j)
                act.activation(bv[:, :, i * 256:i * 256 + 256], pair(bank()), ACT.Copy)\
                    .then_inc(S("panel_evacuated"), 1)
                upper_parts(j + 2)
                j += 1

            def band_exp(h):
                act.wait_ge(S("band_negmax"), h + 1)
                for n, (a, b) in enumerate(((0, P), (P, 384))):
                    act.activation(bp[:, h % 2, a:b], bp[:, h % 2, a:b], ACT.Exp, bias=bst[:, h % 2, 2 + n:3 + n],
                                   accum_out=bst[:, h % 2, 4 + n:5 + n]).then_inc(S("band_exp"), 1)

            exp_table()
            band_exp(0)
            for h in range(BH):
                if h + 1 < BH:
                    band_exp(h + 1)
                act.wait_ge(S("probs_transposed"), h + 1)
                if h >= 2:
                    act.wait_ge(S("band_out"), h - 1)
                act.activation(bpt[:, h % 2, :], MB[:, 2 + h % 2, 0:384], ACT.Copy).then_inc(S("probs_turned"), 1)
            act.wait_ge(S("band_out"), BH)
            act.activation(flat(ob), PB[:].rearrange("p a b -> p (a b)"), ACT.Copy).then_inc(S("band_read"), 1)
            for i in range(8):
                product(j)
                b = bank()
                for m in range(2):
                    ins = act.activation(ga[:, 2 * i + m, :], b[:, m * T:m * T + T], ACT.Sigmoid,
                                         bias=col("b_gate_2", 2 * i + m))
                ins.then_inc(S("panel_evacuated"), 1)
                upper_parts(j + 2)
                j += 1
            act.activation(flat(hhi[:, 0:8, :]), flat(ob), ACT.Copy).then_inc(S("ob_hi"), 1)
            for dst in (ya, yb):
                for i in range(4):
                    product(j)
                    act.activation(dst[:, 2 * i:2 * i + 2, :], pair(bank()), ACT.Copy)\
                        .then_inc(S("panel_evacuated"), 1)
                    upper_parts(j + 2)
                    j += 1
            act.wait_ge(S("merged"), 1)
            act.activation(flat(hhi[:, 8:16, :]), flat(ya), ACT.Copy).then_inc(S("merged_hi"), 1)
            for i in range(4):
                product(j)
                b = bank()
                for m in range(2):
                    f = 2 * i + m
                    ins = act.activation(y3[:, f, :], b[:, m * T:m * T + T], ACT.Identity,
                                         scale=mod2[:, 16 + f:17 + f])
                ins.then_inc(S("panel_evacuated"), 1)
                upper_parts(j + 2)
                j += 1

            def layer_norm(count, name, dst):
                act.wait_ge(S("ln_sum"), count)
                act.activation(rs[:, 0:T], MB[:, 0, 0:T], ACT.Copy, scale=1.0 / D).then_inc(S("ln_mean"), 1)
                act.wait_ge(S("ln_centred"), count)
                act.activation(sq2, y3, ACT.Square).then_inc(S("ln_squares"), 1)
                act.wait_ge(S("ln_var"), count)
                factor(rs[:, T:2 * T], MB[:, 1, 0:T], D, 1, "ln_factor")
                for k in range(KT):
                    act.wait_ge(S("ln_scaled"), 8 * (count - 1) + k + 1)
                    ins = act.activation(dst[:, k, :], y3[:, k, :], ACT.Identity, bias=col(name, k))
                return ins

            layer_norm(1, "ln1_b_2", xt).then_inc(S("x3_ready"), 1)
            act.wait_ge(S("h4_ready"), 1)
            act.activation(flat(hhi[:, 0:8, :]), flat(h2), ACT.Copy).then_inc(S("h4_hi"), 1)
            for i in range(22):
                product(j)
                b = bank()
                for m in range(2):
                    ins = act.activation(f_u[:, i % 2, m, :], b[:, m * T:m * T + T], ACT.Identity,
                                         scale=col("conv_ffn_2", 88 + 22 * m + i),
                                         bias=col("b_conv_ffn_2", 22 * m + i))
                ins.then_inc(S("up_begun"), 1)
                upper_parts(j + 2)
                if i:
                    hidden_upper(i - 1, "hidden2_gated")
                act.wait_ge(S("up_done"), i + 1)
                act.activation(f_s[:, i % 2, :], f_u[:, i % 2, 0, :], ACT.Silu).then_inc(S("hidden2_silu"), 1)
                j += 1
            hidden_upper(21, "hidden2_gated")
            for i in range(11):
                upper_parts(j + 2)
                j += 1
            act.wait_ge(S("multiplied"), 2 * j)
            for r in range(4):
                b = bank()
                for m in range(2):
                    f = 2 * r + m
                    ins = act.activation(y3[:, f, :], b[:, m * T:m * T + T], ACT.Identity,
                                         scale=mod2[:, 40 + f:41 + f])
                ins.then_inc(S("panel_evacuated"), 1)
            layer_norm(2, "ln2_b_2", f_out).then_inc(S("out_ready"), 1)

        @block.vector
        def _(dve):
            done = [0]
            steps = [0]

            def then(ins):
                steps[0] += 1
                ins.then_inc(S("dve_step"), 1)
                dve.wait_ge(S("dve_step"), steps[0])

            def lower_half(v):
                while done[0] <= min(v, 2 * N_SPLIT - 1):
                    v_, (j, h) = done[0], divmod(done[0], 2)
                    u = 2 * place[("S", j)] + h
                    dve.wait_ge(S("upper_ready"), v_ + 1)
                    dve.tensor_tensor(wlo[:, v_ % PARTS, :], raw[:, u % RAW, :],
                                      whi[:, v_ % PARTS, :].bitcast(F32), ALU.subtract)\
                        .then_inc(S("parts_ready"), 1)
                    done[0] += 1

            def lower_parts(j):
                lower_half(2 * j + 1)

            def flat(v):
                return v.rearrange("p a b -> p (a b)")

            def lower(dst, full, upper, name):
                dve.tensor_tensor(dst, full, upper.bitcast(F32), ALU.subtract).then_inc(S(name), 1)

            def over_tokens(v, n=T):
                return v.unsqueeze(2).to_broadcast([v.shape[0], v.shape[1], n])

            def over_tiles(v, n):
                return v.unsqueeze(1).to_broadcast([v.shape[0], n, v.shape[1]])

            fed = [0]

            def accumulate(count=1):
                for _ in range(count):
                    n = fed[0]
                    fed[0] += 1
                    if n in (0, 16):
                        dve.wait_ge(S("c_wide"), 1 + n // 16)
                    for h in range(2):
                        u = 2 * place[("A", n)] + h
                        dst = modc[:, 16 + 2 * n + h, 0:1] if n < 16 else mod2[:, 2 * n - 32 + h:2 * n - 31 + h]
                        dve.wait_ge(S(f"landed{u % RAW}"), 16 * (u // RAW + 1))
                        dve.tensor_tensor_reduce(raw[:, u % RAW, :], raw[:, u % RAW, :], cwide[:], 1.0, 0.0,
                                                 ALU.mult, ALU.add, dst).then_inc(S("accumulated"), 1)

            dve.wait_ge(S("constants"), CONSTANTS)
            dve.wait_ge(S("x_landed"), 48)
            dve.wait_ge(S("rows_turned"), 1)
            then(dve.tensor_tensor(modc[:, 0:16, :], MB[:, 1, 0:32].rearrange("p (a b) -> p a b", b=2),
                                   over_tokens(col("mod_b", 0, 16), 2), ALU.add))
            for s in range(2):
                ins = dve.scalar_tensor_tensor(sc_a[:, s, :], modc[:, 8:16, s], 1.0, col("norm_g", 0, 8),
                                               ALU.add, ALU.mult)
            then(ins)
            dve.wait_ge(S("norm_factor"), 1)
            for k in range(KT):
                for s in range(2):
                    dve.scalar_tensor_tensor(h1[:, k, s * T:s * T + T], (xt[:], xc)[s][:, k, :],
                                             sc_a[:, s, k:k + 1], rs[:, s * T:s * T + T], ALU.mult, ALU.mult)\
                        .then_inc(S("h1_scaled"), 1)
            dve.wait_ge(S("h1_hi"), 1)
            lower(hlo[:].rearrange("p a b -> p (a b)"), flat(h1), hhi[:].rearrange("p a b -> p (a b)"), "h1_lo")
            lower_parts(0)
            dve.wait_ge(S("glr_sum"), 1)
            dve.tensor_copy(glr, MB[0:32, 0, :]).then_inc(S("glr_ready"), 1)
            accumulate(2)
            lower_parts(1)
            for i in range(8):
                dve.wait_ge(S("gate_sum"), i + 1)
                dve.tensor_scalar(g_x[:, i, :], MB[:, i % 3, :], col("gla_b_gate", i), None, ALU.add)\
                    .then_inc(S("gate_biased"), 1)
            for j in range(2, 7):
                accumulate(2)
                lower_parts(j)
            dve.wait_ge(S("gate_soft"), 1)
            then(dve.scalar_tensor_tensor(flat(g_x), flat(g_x), 0.0, flat(g_e3), ALU.min, ALU.subtract))
            for i in range(8):
                for a, n in [(c * CHUNK, CHUNK) for c in range(NCH)] + [(T, T)]:
                    v = g_x[:, i, a:a + n]
                    if i >= 4:
                        v = v[:, ::-1]
                    ins = dve.tensor_tensor_scan(v, ones[:, 0:n], v, 0.0, ALU.mult, ALU.add)
                if i % 3 == 2:
                    lower_parts(7 + i // 3)
            ins.then_inc(S("cumulated"), 1)
            dve.wait_ge(S("cumulated"), 1)
            for d in range(2):
                b = g_x[:, 4 * d:4 * d + 4, 0:T].rearrange("p h (c t) -> p h c t", t=CHUNK)
                e = CHUNK - 1 if d == 0 else 0
                dve.tensor_tensor(g_e3[:, 4 * d:4 * d + 4, 0:T].rearrange("p h (c t) -> p h c t", t=CHUNK),
                                  b[:, :, :, e:e + 1].to_broadcast([P, GH, NCH, CHUNK]), b, ALU.subtract)
                b = g_x[:, 4 * d:4 * d + 4, T:2 * T]
                e = T - 1 if d == 0 else 0
                ins = dve.tensor_tensor(g_e3[:, 4 * d:4 * d + 4, T:2 * T],
                                        b[:, :, e:e + 1].to_broadcast([P, GH, T]), b, ALU.subtract)
            ins.then_inc(S("end_diff"), 1)
            lower_parts(11)
            dve.wait_ge(S("panel_evacuated"), 18)
            dve.wait_ge(S("gate_exp"), 2)
            for d in range(2):
                e = g_e1[:, 4 * d:4 * d + 4, :].rearrange("p h (c t) -> p h c t", t=CHUNK)
                end = CHUNK - 1 if d == 0 else 0
                ins = dve.tensor_copy(dec[:, 4 * d:4 * d + 4, :], e[:, :, :, end])
            then(ins)
            for d in range(2):
                q4 = g_e1[:, 4 * d:4 * d + 4, :]
                dve.scalar_tensor_tensor(flat(q4), flat(q4), GDK ** -0.5, flat(g_q), ALU.mult, ALU.mult)
                k4 = g_e2[:, 4 * d:4 * d + 4, :]
                ins = dve.tensor_tensor(k4, k4, g_k[:, :, 0:T], ALU.mult)
            ins.then_inc(S("keys_decayed"), 1)
            dve.wait_ge(S("gate_exp"), 3)
            for d in range(2):
                k4 = g_e3[:, 4 * d:4 * d + 4, :]
                ins = dve.tensor_tensor(k4, k4, g_k, ALU.mult)
            ins.then_inc(S("end_keys"), 1)
            dve.wait_ge(S("accumulated"), 24)
            then(dve.tensor_tensor(modc[:, 16:40, 0], modc[:, 16:40, 0], col("mod_b", 16, 24), ALU.add))
            dve.wait_ge(S("scores_zeroed"), 1)
            for g in range(4):
                dve.wait_ge(S("scores"), g + 1)
                mask = (causal_t, causal_dn)[g // 2]
                dve.copy_predicated(g_sc[:, 4 * g:4 * g + 4, :], over_tiles(mask[:].bitcast(I32), 4),
                                    MB[:, g, :].rearrange("p (a b) -> p a b", a=4)).then_inc(S("scores_masked"), 1)
            for i in range(8):
                dve.wait_ge(S("state_sum"), i // 2 * 2 + 2)
                dve.tensor_copy(g_s[:, i, :], MB[:, i // 2, (i % 2) * 256:(i % 2) * 256 + 256])\
                    .then_inc(S("state_new"), 1)
            for s in range(NCH - 1):
                for i in range(8):
                    c = s if i < 4 else NCH - 1 - s
                    dve.wait_ge(S("state_sum"), 8 * (s + 1) + i // 2 * 2 + 2)
                    dve.scalar_tensor_tensor(g_s[:, i, :], g_s[:, i, :], dec[:, i, c:c + 1],
                                             MB[:, i // 2, (i % 2) * 256:(i % 2) * 256 + 256], ALU.mult, ALU.add)\
                        .then_inc(S("state_new"), 1)
            dve.wait_ge(S("gla_factor"), 1)
            for v in range(2):
                o = g_o[:, :, v, :]
                ins = dve.scalar_tensor_tensor(o, o, col("gla_norm_g", v), g_rs, ALU.mult, ALU.mult)
            then(ins)
            o = g_o.rearrange("p a b c -> p (a b c)")
            dve.tensor_tensor(o, o, flat(g_r), ALU.mult).then_inc(S("gla_gated"), 1)
            dve.wait_ge(S("gla_hi"), 1)
            lower(flat(hlo[:, 0:8, :]), o, flat(hhi[:, 0:8, :]), "gla_lo")
            j = 12
            lower_parts(13)
            for i in range(4):
                accumulate()
                lower_parts(j + 2)
                j += 1

            def add_normed(count, gate, gain):
                then(dve.tensor_tensor(gcol[:], modc[:, gate:gate + 8, 0], col("norm_g", gain, 8), ALU.mult))
                dve.wait_ge(S("norm_factor"), count)
                for k in range(KT):
                    ins = dve.scalar_tensor_tensor(y1[:, k, :], y1[:, k, :], gcol[:, k:k + 1], rs[:, 0:T],
                                                   ALU.mult, ALU.mult)
                then(ins)
                dve.tensor_tensor(xt[:], xt[:], y1, ALU.add).then_inc(S("x_new"), 1)

            add_normed(2, 16, 8)
            then(dve.scalar_tensor_tensor(sc_a[:, 0, :], modc[:, 32:40, 0], 1.0, col("norm_g", 16, 8),
                                          ALU.add, ALU.mult))
            dve.wait_ge(S("x_new"), 1)
            dve.wait_ge(S("norm_factor"), 3)
            for k in range(KT):
                dve.scalar_tensor_tensor(h2[:, k, :], xt[:, k, :], sc_a[:, 0, k:k + 1], rs[:, 0:T],
                                         ALU.mult, ALU.mult).then_inc(S("h2_scaled"), 1)
            dve.wait_ge(S("h2_hi"), 1)
            lower(flat(hlo[:, 0:8, :]), flat(h2), flat(hhi[:, 0:8, :]), "h2_lo")

            def hidden_lower(i, evacuated, name):
                dve.wait_ge(S("panel_evacuated"), evacuated + i + 1)
                lower(flo[:, i, :], f_g[:, i % 2, :], fhi[:, i, :], name)

            t0 = first["ffn_in"][1]
            for i in range(22):
                if i >= 2:
                    dve.wait_ge(S("hidden_lo"), i - 1)
                accumulate()
                lower_half(2 * j + 4)
                dve.wait_ge(S("hidden_silu"), i + 1)
                dve.tensor_tensor(f_g[:, i % 2, :], f_s[:, i % 2, :], PB[:, (t0 + i) % TURNS, T:2 * T], ALU.mult)\
                    .then_inc(S("hidden_gated"), 1)
                lower_parts(j + 2)
                if i:
                    hidden_lower(i - 1, t0, "hidden_lo")
                j += 1
            hidden_lower(21, t0, "hidden_lo")
            for i in range(11):
                if i < 2:
                    accumulate()
                lower_parts(j + 2)
                j += 1
            dve.wait_ge(S("accumulated"), 80)
            then(dve.tensor_tensor(modc[:, 40:48, 0], modc[:, 40:48, 0], col("mod_b", 40, 8), ALU.add))
            add_normed(4, 40, 24)
            then(dve.tensor_tensor(mod2[:], mod2[:], col("b_ada_2", 0, 48), ALU.add))
            then(dve.tensor_scalar(sc_a[:, 1, :], mod2[:, 8:16], 1.0, None, ALU.add))
            dve.wait_ge(S("x_new"), 2)
            for k in range(KT):
                ins = dve.tensor_scalar(h3[:, k, :], xt[:, k, :], sc_a[:, 1, k:k + 1], mod2[:, k:k + 1],
                                        ALU.mult, ALU.add)
            ins.then_inc(S("h3_ready"), 1)
            dve.wait_ge(S("h3_hi"), 1)
            lower(flat(hlo[:, 0:8, :]), flat(h3), flat(hhi[:, 0:8, :]), "h3_lo")
            dve.wait_ge(S("rows_act"), 1)
            dve.tensor_scalar(hm[:, 1, :], MB[0:DH, 0, T:2 * T], hrow[:, 1:2], None, ALU.add)\
                .then_inc(S("rows_ready"), 1)
            dve.wait_ge(S("rows_act"), 2)
            then(dve.scalar_tensor_tensor(hm[:, 6, :], hm[:, 1, :], 0.0, hm[:, 4, :], ALU.max, ALU.add))
            then(dve.tensor_scalar(hm[:, 1, :], hm[:, 6, :], hrow[:, 0:1], -1.0, ALU.mult, ALU.mult))
            for c in range(NCH):
                cs = slice(c * CHUNK, c * CHUNK + CHUNK)
                ins = dve.tensor_tensor_scan(hm[:, 2, cs], ones[0:DH, 0:CHUNK], hm[:, 1, cs], 0.0,
                                             ALU.mult, ALU.add)
            then(ins)
            rows = hm[:, 2, :].rearrange("p (c t) -> p c t", t=CHUNK)
            dve.tensor_tensor(hm[:, 5, :].rearrange("p (c t) -> p c t", t=CHUNK),
                              rows[:, :, CHUNK - 1:CHUNK].to_broadcast([DH, NCH, CHUNK]), rows, ALU.subtract)\
                .then_inc(S("rows_ready"), 1)
            dve.wait_ge(S("constants"), ALL_CONSTANTS)
            t0 = first["qkv"][1]
            for i in range(12):
                lower_half(2 * j + 4)
                dve.wait_ge(S("conv_begun"), i + 1)
                b = PB[:, (t0 + i) % TURNS, :]
                for s in range(1, 4):
                    for m in range(2):
                        o = cy[:, i % 2, m, s:T]
                        ins = dve.scalar_tensor_tensor(o, b[:, m * T:m * T + T - s],
                                                       col("conv_a_2", 24 * (3 - s) + 2 * i + m), o,
                                                       ALU.mult, ALU.add)
                    if s < 3:
                        then(ins)
                ins.then_inc(S("conv_done"), 1)
                lower_parts(j + 2)
                j += 1
            for i in range(4):
                lower_parts(j + 2)
                j += 1
            dve.wait_ge(S("qk_factor"), 1)
            dve.scalar_tensor_tensor(flat(qkv[:, 0:8, :]), flat(qkv[:, 0:8, :]), DDK ** -0.5, rs2,
                                     ALU.mult, ALU.mult).then_inc(S("qk_normed"), 1)
            dve.wait_ge(S("qk_factor"), 2)
            kc = qkv[:, 8:16, :]
            dve.tensor_tensor(flat(kc), flat(kc), rs2, ALU.mult).then_inc(S("qk_normed"), 1)
            dve.wait_ge(S("tok_rows"), 1)
            dve.tensor_copy(mod_flat[:, 0:48], MB[:, 0, 0:48]).then_inc(S("tok_ready"), 1)
            dve.wait_ge(S("tok_ready"), 1)
            dve.wait_ge(S("rows_spread"), 1)
            dve.wait_ge(S("eg_ready"), 1)
            for t in range(2):
                for h in range(DH):
                    a = (h % 2) * T + t * P
                    ins = dve.tensor_scalar(dm[:, t * 8 + h, :], MB[:, h // 2, a:a + P],
                                            gl_tok[:, 0, t, h:h + 1], 0.0, ALU.subtract, ALU.min)
            ins.then_inc(S("decay_diff"), 1)
            dve.wait_ge(S("decay_exp"), 1)
            then(dve.tensor_tensor(dm, dm, over_tiles(causal_t[:], 16), ALU.mult))
            dve.tensor_copy(gl_end, eg.rearrange("p h (c t) -> p h c t", t=CHUNK)[:, :, :, CHUNK - 1])
            dve.wait_ge(S("rows_spread"), 2)
            dve.tensor_tensor(flat(kb), flat(kc), MB[:].rearrange("p a b -> p (a b)"), ALU.mult)\
                .then_inc(S("kb_ready"), 1)
            for t in range(2):
                dve.wait_ge(S("qk_products"), t + 1)
                prod = MB[:].rearrange("p a (b c) -> p (a b) c", c=256)
                dmt = dm[:, 8 * t:8 * t + 8, :]
                dve.tensor_tensor(qkt[:, 8 * t:8 * t + 8, :], prod[:, :, 0:P], dmt, ALU.mult)
                then(dve.tensor_tensor(s_u, prod[:, :, P:2 * P], dmt, ALU.mult))
                dve.sem_inc(S("at_ready"), 1)
                tt8 = tt_[:, 8 * t:8 * t + 8, :]
                then(dve.scalar_tensor_tensor(s_nt, s_u, -1.0, over_tiles(m16t, 8), ALU.mult, ALU.mult))
                dve.tensor_tensor(tt8, s_nt, over_tiles(ident[:], 8), ALU.add)

                def pair_banks(p):
                    b0 = 2 * (p % 2)
                    return MB[:, b0:b0 + 2, :].rearrange("p a (b c) -> p (a b) c", c=P)

                dve.wait_ge(S("solve_product"), 15 * t + 1)
                dve.scalar_tensor_tensor(s_n, pair_banks(0), -1.0, over_tiles(m16, 8), ALU.mult, ALU.mult)
                dve.tensor_tensor(s_b32, pair_banks(0), over_tiles(d32, 8), ALU.mult)
                dve.tensor_tensor(s_b64, pair_banks(0), over_tiles(d64, 8), ALU.mult)\
                    .then_inc(S("solve_masked"), 1)
                for p, op in ((3, ALU.add), (6, ALU.add), (8, ALU.add), (11, ALU.subtract), (14, ALU.subtract)):
                    dve.wait_ge(S("solve_product"), 15 * t + p + 1)
                    dve.tensor_tensor(tt8, tt8, pair_banks(p), op).then_inc(S("tt_ready"), 1)
            then(dve.tensor_tensor(flat(kb), flat(kb), flat(eg), ALU.mult))
            dve.tensor_tensor(flat(eg), flat(eg), flat(qkv[:, 0:8, :]), ALU.mult)
            for n, dst in enumerate((vb, kd)):
                for t in range(2):
                    dve.wait_ge(S("vk_turned"), 2 * n + t + 1)
                    dve.tensor_tensor(dst[:, t, :].rearrange("p (a b) -> p a b", b=P), pair_banks(t),
                                      over_tokens(gl_tok[:, 1 + n, t, :], P), ALU.mult)\
                        .then_inc(S("tok_major"), 1)
            dve.wait_ge(S("tok_major"), 4)
            for c in range(NCH):
                rows = slice(CHUNK * (c % 2), CHUNK * (c % 2) + CHUNK)
                t = c // 2
                if c == 0:
                    dve.tensor_copy(rr[rows, :], vb[rows, t, :]).then_inc(S("rhs_ready"), 1)
                else:
                    dve.wait_ge(S("predicted"), c)
                    dve.tensor_tensor(rr[rows, :], vb[rows, t, :], flat(MB[rows, 0:2, :]), ALU.subtract)\
                        .then_inc(S("rhs_ready"), 1)
                if c < NCH - 1:
                    if c:
                        dve.wait_ge(S("delta_out"), c + 1)
                        then(dve.tensor_tensor(st, st, over_tokens(gl_end[:, :, c], P), ALU.mult))
                    dve.wait_ge(S("state_step"), c + 1)
                    if c:
                        ins = dve.tensor_tensor(flat(st), flat(st), flat(MB[:, 0:2, :]), ALU.add)
                    else:
                        ins = dve.tensor_copy(flat(st), flat(MB[:, 0:2, :]))
                    ins.then_inc(S("delta_state"), 1)
            dve.wait_ge(S("delta_norm_sum"), 1)
            dve.memset(bx[0:64, :, 0:64], NEG).then_inc(S("band_masked"), 1)
            dve.wait_ge(S("delta_factor"), 1)
            then(dve.scalar_tensor_tensor(flat(od), flat(od), col("norm_a_2"), rs2, ALU.mult, ALU.mult))
            dve.tensor_tensor(flat(od), flat(od), flat(zs), ALU.mult).then_inc(S("delta_gated"), 1)
            dve.wait_ge(S("oa_hi"), 1)
            lower(flat(hlo[:, 8:16, :]), flat(od), flat(hhi[:, 8:16, :]), "oa_lo")
            for i in range(12):
                lower_parts(j + 2)
                j += 1
            dve.wait_ge(S("bias_landed"), 32)

            def band_shift(h):
                dve.wait_ge(S("band_scores"), h + 1)
                if h >= 2:
                    dve.wait_ge(S("probs_transposed"), h - 1)
                for n, (a, b) in enumerate(((0, P), (P, 384))):
                    dve.tensor_tensor_reduce(bp[:, h % 2, a:b], MB[:, h % 2, a:b], bx[:, h, 0:b - a][:, ::-1],
                                             1.0, NEG, ALU.add, ALU.max, bst[:, h % 2, n:n + 1])\
                        .then_inc(S("band_shifted"), 1)
                dve.wait_ge(S("band_shifted"), 2 * h + 2)
                dve.tensor_scalar(bst[:, h % 2, 2:4], bst[:, h % 2, 0:2], -1.0, None, ALU.mult)\
                    .then_inc(S("band_negmax"), 1)

            band_shift(0)
            for h in range(BH):
                if h + 1 < BH:
                    band_shift(h + 1)
                dve.wait_ge(S("band_exp"), 2 * h + 2)
                then(dve.reciprocal(bst[:, h % 2, 6:8], bst[:, h % 2, 4:6]))
                for n, (a, b) in enumerate(((0, P), (P, 384))):
                    ins = dve.tensor_scalar(bp[:, h % 2, a:b], bp[:, h % 2, a:b], bst[:, h % 2, 6 + n:7 + n],
                                            None, ALU.mult)
                ins.then_inc(S("band_probs"), 1)
            for i in range(8):
                lower_parts(j + 2)
                j += 1
            dve.wait_ge(S("ob_hi"), 1)
            lower(flat(hlo[:, 0:8, :]), flat(ob), flat(hhi[:, 0:8, :]), "ob_lo")
            for i in range(8):
                lower_parts(j + 2)
                if i == 3:
                    dve.wait_ge(S("panel_evacuated"), first["branch_b"][1])
                    dve.tensor_tensor(ya, ya, ga[:, 0:8, :], ALU.mult)
                j += 1
            dve.wait_ge(S("panel_evacuated"), first["mix"][1])
            then(dve.tensor_tensor(yb, yb, ga[:, 8:16, :], ALU.mult))
            dve.tensor_tensor(ya, ya, yb, ALU.add).then_inc(S("merged"), 1)
            dve.wait_ge(S("merged_hi"), 1)
            lower(flat(hlo[:, 8:16, :]), flat(ya), flat(hhi[:, 8:16, :]), "merged_lo")
            for i in range(4):
                lower_parts(j + 2)
                j += 1

            def layer_norm(count, gain):
                dve.scalar_tensor_tensor(flat(y3), xt[:].rearrange("p a b -> p (a b)"), ALPHA, flat(y3),
                                         ALU.mult, ALU.add).then_inc(S("ln_in"), 1)
                dve.wait_ge(S("ln_mean"), count)
                dve.tensor_tensor(y3, y3, over_tiles(rs[:, 0:T], KT), ALU.subtract).then_inc(S("ln_centred"), 1)
                dve.wait_ge(S("ln_centred"), count)
                dve.wait_ge(S("ln_factor"), count)
                for k in range(KT):
                    dve.scalar_tensor_tensor(y3[:, k, :], y3[:, k, :], col(gain, k), rs[:, T:2 * T],
                                             ALU.mult, ALU.mult).then_inc(S("ln_scaled"), 1)

            dve.wait_ge(S("panel_evacuated"), first["up"][1])
            layer_norm(1, "ln1_g_2")
            then(dve.tensor_scalar(sc_a[:, 1, :], mod2[:, 32:40], 1.0, None, ALU.add))
            dve.wait_ge(S("x3_ready"), 1)
            for k in range(KT):
                ins = dve.tensor_scalar(h2[:, k, :], xt[:, k, :], sc_a[:, 1, k:k + 1], mod2[:, 24 + k:25 + k],
                                        ALU.mult, ALU.add)
            ins.then_inc(S("h4_ready"), 1)
            dve.wait_ge(S("h4_hi"), 1)
            lower(flat(hlo[:, 0:8, :]), flat(h2), flat(hhi[:, 0:8, :]), "h4_lo")
            t0 = first["up"][1]
            for i in range(22):
                lower_half(2 * j + 4)
                dve.wait_ge(S("up_begun"), i + 1)
                b = PB[:, (t0 + i) % TURNS, :]
                for s in range(1, 3):
                    for m in range(2):
                        o = f_u[:, i % 2, m, s:T]
                        ins = dve.scalar_tensor_tensor(o, b[:, m * T:m * T + T - s],
                                                       col("conv_ffn_2", 44 * (2 - s) + 22 * m + i), o,
                                                       ALU.mult, ALU.add)
                    if s < 2:
                        then(ins)
                ins.then_inc(S("up_done"), 1)
                lower_parts(j + 2)
                if i:
                    hidden_lower(i - 1, t0, "hidden2_lo")
                if i >= 2:
                    dve.wait_ge(S("hidden2_lo"), i - 1)
                dve.wait_ge(S("hidden2_silu"), i + 1)
                dve.tensor_tensor(f_g[:, i % 2, :], f_s[:, i % 2, :], f_u[:, i % 2, 1, :], ALU.mult)\
                    .then_inc(S("hidden2_gated"), 1)
                j += 1
            hidden_lower(21, t0, "hidden2_lo")
            for i in range(11):
                lower_parts(j + 2)
                j += 1
            dve.wait_ge(S("panel_evacuated"), first["down"][1] + 4)
            layer_norm(2, "ln2_g_2")


_ARGS = ["panels", "x", "ctx_x", "columns", "c_rows", "w_glr", "w_gate", "w_beta_a", "head_rows", "rel_bias"]


def _lay_out(inputs):
    a = {k: np.asarray(v) for k, v in inputs.items()}

    def wide(w, cols=None):
        n = w.shape[1] // 256
        return w.reshape(KT, P, n, 256).transpose(2, 1, 0, 3).reshape(n, P, 2048)

    def across(w):
        n = w.shape[1] // 256
        return w.T.reshape(n, 2, P, D).transpose(0, 2, 1, 3).reshape(n, P, 2048)

    def gate_up(w):
        v = w.reshape(KT, P, 2, FT, P).transpose(3, 1, 0, 2, 4)
        return v.reshape(FT, P, 2048)

    def tall(w):
        return w.reshape(FT // 2, 2, P, D).transpose(0, 2, 1, 3).reshape(FT // 2, P, 2048)

    gla, w2 = a["gla_w_in"][0], a["w_in_2"][0]
    mod, ada = a["mod_w"][0], a["w_ada_2"][0]
    split = [wide(gla[:, 512:1024]), wide(gla[:, 1024:2048]), wide(gla[:, 0:512]),
             wide(gla[:, 2048:3072]), wide(a["gla_w_out"][0]), gate_up(a["ffn_w_in"][0]), tall(a["ffn_w_out"][0]),
             wide(w2[:, 0:4096]), wide(w2[:, 4112:9232]),
             wide(a["w_branch_a_2"][0]), wide(a["w_branch_b_2"][0]), wide(a["w_o_2"][0]),
             gate_up(a["w_up_2"][0]), tall(a["w_down_2"][0])]
    of_kind = {"S": np.concatenate(split), "R": wide(mod[:, 0:2 * D]),
               "A": np.concatenate([across(mod[:, 2 * D:]), across(ada)])}
    out = {"panels": np.stack([of_kind[kind][n] for kind, n in plan_stream()[0]])}

    def feature_major(v):
        return np.ascontiguousarray(v.T.reshape(KT, P, T).transpose(1, 0, 2))

    out["x"], out["ctx_x"] = feature_major(a["x"][0]), feature_major(a["ctx"][0])
    vectors = [a["c"], a["c_ctx"]] + [a[name] for name, _ in COLUMNS[2:]]
    out["columns"] = np.concatenate([v.reshape(-1) for v in vectors]).reshape(NCOL, P).T.copy()
    out["c_rows"] = np.stack([a["c"].reshape(-1), a["c_2"].reshape(-1)])
    out["w_glr"] = gla[:, 3072:3104].reshape(KT, P, 32).transpose(1, 0, 2).copy()
    out["w_gate"] = a["gla_w_gate"][0].copy()
    out["w_beta_a"] = w2[:, 4096:4112].reshape(KT, P, 16).transpose(1, 0, 2).copy()
    out["head_rows"] = np.stack([a["a_log_2"][0], a["dt_bias_2"][0]], axis=1)
    out["rel_bias"] = a["rel_bias_2"][0].copy()
    return out


def kernel(**inputs):
    import concourse.bacc as _bacc
    from concourse.bass_utils import run_bass_kernel_spmd as _run

    nc = _bacc.Bacc("TRN2", target_bir_lowering=False, num_devices=1)
    laid = _lay_out(inputs)
    arrays, args = {}, []
    for name in _ARGS:
        v = laid[name]
        arrays[f"in_{name}"] = v
        args.append(nc.dram_tensor(f"in_{name}", v.shape, mybir.dt.from_np(v.dtype), kind="ExternalInput").ap())
    args.append(nc.dram_tensor("out_x", (P, KT, T), F32, kind="ExternalOutput").ap())
    two_blocks(nc, *args)
    r = _run(nc, [arrays], core_ids=[0])
    return r.results[0]["out_x"].transpose(1, 0, 2).reshape(1, D, T).transpose(0, 2, 1)
```

```python
from contextlib import ExitStack

import concourse.bass as bass
from concourse import mybir
import numpy as np

F32 = mybir.dt.float32
F32R = mybir.dt.float32r
I32 = mybir.dt.int32
ALU = mybir.AluOpType
ACT = mybir.ActivationFunctionType
AX_X = mybir.AxisListType.X

P = 128
D = 1024
KT = D // P
T = 256
CHUNK = 64
HALF = 1024
NCH = T // CHUNK
FFN = 2816
FT = FFN // P
GH, GDK, GDV = 4, 128, 256
DH, DDK = 8, 128
BH, BDH = 16, 64
REL = 320
EPS_RMS, EPS_LN = 1e-6, 1e-5
ALPHA = 2.0 ** 0.25
NEG = -1e30
RAW, PARTS, TURNS = 6, 4, 4

LAYERS = [("mod_first", "R", 8), ("gla_k", "SAA", 2), ("gla_v", "SAA", 4), ("gla_q", "S", 2),
          ("gla_r", "S", 4), ("gla_out", "SA", 4), ("ffn_in", "SA", 22),
          ("ffn_out", "SA", 2), ("ffn_out_rest", "S", 9), ("qkv", "S", 12), ("z", "S", 4),
          ("band_q", "S", 4), ("band_k", "S", 4), ("band_v", "S", 4), ("gates", "S", 8),
          ("branch_a", "S", 4), ("branch_b", "S", 4), ("mix", "S", 4), ("up", "S", 22),
          ("down", "S", 11)]


def plan_stream():
    stream, first, count_of = [], {}, {"S": 0, "R": 0, "A": 0}
    turn = 0
    for layer, pattern, count in LAYERS:
        first[layer] = (count_of["S"], turn)
        for _ in range(count):
            for kind in pattern:
                stream.append((kind, count_of[kind]))
                count_of[kind] += 1
        turn += {"gla_k": 2 * count, "gla_v": 2 * count, "mod_first": 0, "ffn_out": 4, "ffn_out_rest": 0, "band_v": 2 * count,
                 "down": 4, "gates": count + BH // 4}.get(layer, count)
    return stream, first


COLUMNS = [("c", 8), ("c_ctx", 8), ("mod_b", 48), ("norm_g", 32), ("gla_b_gate", 8), ("gla_norm_g", 2),
           ("b_ada_2", 48), ("b_gate_2", 16), ("conv_a_2", 96), ("norm_a_2", 1), ("ln1_g_2", 8), ("ln1_b_2", 8),
           ("ln2_g_2", 8), ("ln2_b_2", 8), ("conv_ffn_2", 132), ("b_conv_ffn_2", 44)]
COL, NCOL = {}, 0
for _name, _n in COLUMNS:
    COL[_name] = NCOL
    NCOL += _n


CONSTANTS, ALL_CONSTANTS = 15, 33
N_SPLIT = sum(count * pattern.count("S") for _, pattern, count in LAYERS)
N_ROWS = 8
RELEASE = {"S": "parts_ready", "R": "row_product", "A": "accumulated"}

SOLVE_COUNTS = {"at_ready": 1, "solve_masked": 1, "solve_copied": 9, "tt_ready": 5}
SOLVE_WAITS = [
    [("at_ready", 1)],
    [("solve_masked", 1)],
    [("solve_masked", 1)],
    [("solve_copied", 1)],
    [("solve_copied", 2)],
    [("tt_ready", 1)],
    [("solve_copied", 3), ("tt_ready", 1)],
    [("solve_copied", 4)],
    [("solve_copied", 5), ("tt_ready", 2)],
    [("tt_ready", 3)],
    [("tt_ready", 3)],
    [("solve_copied", 7)],
    [("tt_ready", 4)],
    [("tt_ready", 4)],
    [("solve_copied", 9)],
]


FILL = {"q_sums": 4, "k_sums": 8, "gates_spread": 12, "betas_spread": 14, ("products", 0): 16, (0, 0): 20, (0, 5): 21,
        (0, 8): 22, (0, 11): 23, ("products", 1): 25, (1, 0): 29, (1, 5): 30, (1, 8): 31, (1, 11): 32}
for _c in range(NCH):
    FILL.update({("begun", _c): 33 + 4 * _c, ("predicted", _c): 34 + 4 * _c, ("corrected", _c): 36 + 4 * _c})


FILL["delta_norm"] = 52
FILL.update({("head", _h): 54 + 2 * _h for _h in range(12)})
FILL["heads_done"] = 80


def tended(step):
    order = [s for s in FILL if isinstance(s, tuple) and (isinstance(s[0], int) or s[0] == "head")]
    if step == ("head", 0):
        return FILL["delta_norm"]
    if step in order[1:]:
        return FILL[order[order.index(step) - 1]]
    return FILL.get(step, 0)


def two_blocks(nc, panels, x, ctx_x, columns, c_rows, w_glr, w_gate, w_beta_a, head_rows, rel_bias, out):
    stream, first = plan_stream()
    place = {entry: n for n, entry in enumerate(stream)}

    with ExitStack() as ctx:
        def sb(name, shape, dt=F32, scope=ctx):
            return scope.enter_context(nc.sbuf_tensor(name, shape, dt))

        signals = {}

        def S(name):
            if name not in signals:
                signals[name] = ctx.enter_context(nc.semaphore(name))
            return signals[name]

        PB = ctx.enter_context(nc.psum_tensor("panel_banks", [P, TURNS, 512], F32))
        MB = ctx.enter_context(nc.psum_tensor("work_banks", [P, 4, 512], F32))

        raw = sb("raw", [P, RAW, HALF])
        whi = sb("w_hi", [P, PARTS, HALF], F32R)
        wlo = sb("w_lo", [P, PARTS, HALF], F32R)
        xt = sb("x_t", [P, KT, T])
        cols = sb("columns", [P, NCOL])
        ident = sb("ident", [P, P])
        ones = sb("ones", [P, T])
        causal_t = sb("causal_t", [P, P])
        causal_dn = sb("causal_dn", [P, P])
        cwide = sb("c_wide", [P, D])
        masks = cwide[:].rearrange("p (a b) -> p a b", a=8)
        m16t = masks[:, 0, :]
        m16 = masks[:, 1, :]
        d32 = masks[:, 2, :]
        d64 = masks[:, 3, :]
        modc = sb("mod_cols", [P, 48, 2])
        mod2 = sb("mod2_cols", [P, 48])
        cact = sb("c_act", [P, 2, 8])
        sc_a = sb("scale_a", [P, 2, 8])
        gcol = sb("gate_cols", [P, 8])
        rs = sb("rs", [P, 512])
        eps = sb("eps", [P, 4])
        dec = sb("g_decay", [P, 8, NCH])
        mod_flat = modc[:].rearrange("p a b -> p (a b)")
        gl_tok = mod_flat[:, 0:48].rearrange("p (a b c) -> p a b c", a=3, b=2)
        gl_end = mod_flat[:, 48:80].rearrange("p (a b) -> p a b", a=DH)
        w_ba = sb("w_beta_a", [P, KT, 16])
        hrow = sb("head_rows", [DH, 2])

        def col(name, i=0, n=1):
            return cols[:, COL[name] + i:COL[name] + i + n]

        with ExitStack() as scope:
            hhi = sb("act_hi", [P, 16, T], F32R, scope)
            hlo = sb("act_lo", [P, 16, T], F32R, scope)
        sb("under_hi", [P, KT, T])
        bq = sb("band_q", [P, KT, T])
        sb("under_lo", [P, KT, T])
        bk = sb("band_k", [P, KT, T])

        def arena(name, size, scope):
            tensor, at = sb(name, [P, size], F32, scope), [0]

            def take(*shape, at_=None):
                n = int(np.prod(shape))
                start = at[0] if at_ is None else at_
                if at_ is None:
                    at[0] += n
                assert start + n <= size, (name, start + n, size)
                names = "abcd"[:len(shape)]
                view = tensor[:, start:start + n]
                if len(shape) > 1:
                    view = view.rearrange(f"p ({' '.join(names)}) -> p {' '.join(names)}",
                                          **{k: v for k, v in zip(names, shape)})
                return view
            take.at = at
            return take

        WORK = 25600
        with ExitStack() as scope:
            take = arena("gla_work", WORK, scope)
            g_q = take(GH, T)
            g_k = take(GH, 2 * T)
            g_v = take(4, D)
            g_r = take(KT, T)
            g_x = take(8, 2 * T)
            g_kt = take(4, 8, P, at_=take.at[0] - 4096)
            e_at = take.at[0]
            g_e1 = take(8, T)
            g_e2 = take(8, T)
            g_e3 = take(8, 2 * T)
            s_at = take.at[0]
            g_s = take(8, GDV)
            g_sc = take(16, P)
            g_o = take(GH, 2, T, at_=s_at)
            wgp = take(8 * P, at_=e_at)[0:32, :]
            glr = take(2 * T, at_=e_at + 1024)[0:32, :]
            wgl = take(KT, 32, at_=e_at + 1536)
            xc = take(KT, T, at_=e_at + 2048)
            sq1 = take(KT, 2 * T, at_=e_at + 4096)
            mod_rows = take(8, 256, at_=GH * T)[0:2]
            h1 = take(KT, 2 * T, at_=s_at)
            g_sq = take(GH, 2, T, at_=e_at + 2048)
            g_rs = take(GH, T, at_=e_at + 4096)
            assert s_at + 4096 <= WORK
        with ExitStack() as scope:
            fhi = sb("hidden_hi", [P, FT, T], F32R, scope)
            flo = sb("hidden_lo", [P, FT, T], F32R, scope)
            take = arena("ffn_work", 14000, scope)
            y1 = take(KT, T)
            sq2 = take(KT, T)
            h2 = take(KT, T)
            f_s = take(2, T)
            f_g = take(2, T)
            y3 = take(KT, T)
            f_u = take(2, 2, T)
            f_out = take(KT, T)
        with ExitStack() as scope:
            take = arena("mix_work", WORK, scope)
            m_at = take.at[0]
            qkv = take(24, T)
            zs = take(KT, T)
            kb = take(DH, T)
            eg = take(DH, T)
            vb = take(2, D)
            kd = take(2, D)
            dm = kd.rearrange("p a (b c) -> p (a b) c", c=P)
            rs2 = vb.rearrange("p a b -> p (a b)")
            qkt = take(16, P)
            tt_ = take(16, P)
            t_at = take.at[0]
            s_n, s_nt, s_b32, s_b64, s_u = (take(8, P) for _ in range(5))
            s_t = s_nt
            sq3 = take(16, T, at_=t_at)
            h3 = take(KT, T, at_=m_at + 10240)
            cy = take(2, 2, T, at_=m_at + 12288)
            st = take(DH, P, at_=t_at)
            rr = take(D, at_=t_at + 1024)
            vn = take(D, at_=t_at + 2048)
            sel = take(DH, P, at_=t_at)[0:DH]
            hm = take(8, T, at_=m_at + 16384)[0:DH]
            vt_ = qkv[:, 16:24, :]
            od = take(DH, T, at_=m_at + 4096)
            odq = take(DH, T, at_=m_at)
            bv = take(2, D, at_=m_at + 2048)
            bx = take(BH, T, at_=m_at + 8192)
            bp = take(2, 384, at_=m_at + 12288)
            bpt = take(2, 384, at_=m_at + 13056)
            bst = take(2, 8, at_=m_at + 13824)
            ga = take(16, T, at_=m_at + 14336)
            ya = take(KT, T, at_=m_at + 18432)
            yb = take(KT, T, at_=m_at + 20480)
            ob = take(KT, T, at_=m_at + 22528)

        block = ctx.enter_context(nc.Block())

        @block.sync
        def _(sp):
            for u in range(2 * len(stream)):
                if u >= RAW:
                    kind, i = stream[(u - RAW) // 2]
                    sp.wait_ge(S(RELEASE[kind]), 2 * i + u % 2 + 1)
                sp.dma_start(raw[:, u % RAW], panels[u // 2][:, u % 2 * HALF:u % 2 * HALF + HALF])\
                    .then_inc(S(f"landed{u % RAW}"), 16)
            for k in (0, 4):
                sp.wait_ge(S("out_ready"), k + 4)
                sp.dma_start(out[:, k:k + 4], f_out[:, k:k + 4]).then_inc(S("out_stored"), 16)
            sp.wait_ge(S("out_stored"), 32)

        @block.gpsimd
        def _(pool):
            made = [0]

            def step(ins):
                made[0] += 1
                ins.then_inc(S("constants"), 1)
                pool.wait_ge(S("constants"), made[0])

            def keep(t, compare, base, pattern, cm, fill=0.0):
                step(pool.affine_select(out=t, in_=t, compare_op=compare, fill=fill, base=base,
                                        pattern=pattern, channel_multiplier=cm))

            def same_block(t, size):
                v = t.rearrange("p (b c) -> p b c", c=size)
                keep(v, ALU.is_ge, 0, [[-size, P // size], [0, size]], 1)
                keep(v, ALU.is_ge, size - 1, [[size, P // size], [0, size]], -1)

            step(pool.memset(ones[:], 1.0))
            step(pool.memset(ident[:], 0.0))
            keep(ident[:], ALU.not_equal, 0, [[-1, P]], 1, 1.0)

            def make_masks(which):
                for t, base, pattern, cm, size in which:
                    step(pool.memset(t, 1.0))
                    same_block(t, size)
                    if pattern:
                        keep(t, ALU.is_ge, base, pattern, cm)
                    else:
                        v = t.rearrange("p (b c) -> p b c", c=size)
                        keep(v, ALU.is_ge, -(size // 2), [[-size, P // size], [0, size]], 1)
                        keep(v, ALU.is_ge, size // 2 - 1, [[0, P // size], [-1, size]], 0)

            make_masks([(causal_t[:], 0, [[1, P]], -1, 64), (causal_dn[:], 0, [[-1, P]], 1, 64)])
            step(pool.memset(eps[:, 0:1], EPS_RMS))
            step(pool.memset(eps[:, 1:2], EPS_LN))
            step(pool.memset(eps[:, 2:3], 1.0))
            step(pool.memset(wgp, 0.0))
            assert made[0] == CONSTANTS, made[0]
            for d in range(2):
                pool.dma_start(wgp[16 * d:16 * d + 16, 512 * d:512 * d + 512], w_gate[d])\
                    .then_inc(S("gate_w_landed"), 16)
            pool.wait_ge(S("h1_lo"), KT)
            pool.wait_ge(S("glr_sum"), 1)
            pool.memset(g_sc, 0.0).then_inc(S("scores_zeroed"), 1)
            pool.wait_ge(S("accumulated"), 80)
            make_masks([(m16t, -1, [[1, P]], -1, 16), (m16, -1, [[-1, P]], 1, 16),
                        (d32, 0, None, 0, 32), (d64, 0, None, 0, 64)])
            assert made[0] == ALL_CONSTANTS, made[0]
            pool.wait_ge(S("qk_sums"), 2)
            pool.memset(sel, 1.0).then_inc(S("selectors"), 1)
            pool.wait_ge(S("selectors"), 1)
            pool.affine_select(out=sel, in_=sel, compare_op=ALU.is_equal, fill=0.0, base=0,
                               pattern=[[-1, DH], [0, P]], channel_multiplier=1).then_inc(S("selectors"), 1)

        @block.tensor
        def _(pe):
            split = [0]
            turn = [0]

            def parts_of(j, k):
                s = (2 * j + k // 4) % PARTS
                return whi[:, s], wlo[:, s]

            def open_half(j, h):
                pe.wait_ge(S("parts_ready"), 2 * j + h + 1)

            def take_turn():
                t = turn[0]
                turn[0] += 1
                if t >= TURNS:
                    pe.wait_ge(S("panel_evacuated"), t - TURNS + 1)
                return t % TURNS

            def three_pass(out_, weights, moving, start, stop):
                (a_hi, a_lo), (b_hi, b_lo) = weights, moving
                for p, (a, b) in enumerate(((a_hi, b_hi), (a_hi, b_lo), (a_lo, b_hi))):
                    ins = pe.matmul(out_, a, b, start=start and p == 0, stop=stop and p == 2,
                                    skip_group_check=True)
                return ins

            def quarter(j, h, m, b, x_unit, nf=1, ready=None):
                o = PB[:, b[m], :] if nf == 2 else PB[:, b[0], m * T:m * T + T]
                for k in range(4 * h, 4 * h + 4):
                    w0 = k % 4 * 256 + m * P
                    if ready and m == 0:
                        pe.wait_ge(S(ready), k + 1)
                    ins = three_pass(o, tuple(w[:, w0:w0 + P] for w in parts_of(j, k)),
                                     tuple(v[:, x_unit(k):x_unit(k) + nf, :] for v in (hhi, hlo)),
                                     start=(k == 0 and (nf == 2 or m == 0)), stop=(k == KT - 1))
                if m:
                    ins.then_inc(S("multiplied"), 1)

            def panel(j, x_unit, nf=1, ready=None):
                b = [take_turn() for _ in range(nf)]
                for h in range(2):
                    open_half(j, h)
                    for m in range(2):
                        quarter(j, h, m, b, x_unit, nf, ready)

            def token_quarter(j, h, n, b, x_unit, tile):
                unit, t0 = tile
                for k in range(4 * h, 4 * h + 4):
                    ins = three_pass(PB[:, b, (n % 2) * 256:(n % 2) * 256 + 256],
                                     tuple(v[:, x_unit(k) + unit, t0:t0 + P] for v in (hhi, hlo)),
                                     tuple(w[:, k % 4 * 256:k % 4 * 256 + 256] for w in parts_of(j, k)),
                                     start=(k == 0 and n % 2 == 0), stop=(k == KT - 1))
                return ins

            def token_panel(j, x_unit, tiles):
                b = [take_turn() for _ in range(len(tiles) // 2)]
                for h in range(2):
                    open_half(j, h)
                    for n, tile in enumerate(tiles):
                        ins = token_quarter(j, h, n, b[n // 2], x_unit, tile)
                    ins.then_inc(S("multiplied"), 1)

            def row_product(a):
                if a >= TURNS:
                    pe.wait_ge(S("rows_read"), a - TURNS + 1)
                for h in range(2):
                    u = 2 * place[("R", a)] + h
                    pe.wait_ge(S(f"landed{u % RAW}"), 16 * (u // RAW + 1))
                    for k in range(4):
                        ins = pe.matmul(PB[0:2, a % TURNS, 0:256], cact[:, 0:2, 4 * h + k],
                                        raw[:, u % RAW, k * 256:k * 256 + 256],
                                        start=(h == 0 and k == 0), stop=(h == 1 and k == 3))
                    ins.then_inc(S("row_product"), 1)

            def turn_rows(a):
                pe.wait_ge(S("rows_read"), a + 1)
                for m in range(2):
                    f = 2 * a + m
                    ins = pe.transpose(MB[:, 1, 2 * f:2 * f + 2], mod_rows[:, a, m * P:m * P + P], ident[0:2, 0:2])
                if a == N_ROWS - 1:
                    ins.then_inc(S("rows_turned"), 1)

            pe.wait_ge(S("c_ready"), 1)
            for a in range(TURNS):
                row_product(a)
            pe.wait_ge(S("constants"), CONSTANTS)
            for k in range(KT):
                if k % 4 == 0:
                    pe.wait_ge(S("input_squares"), k // 4 + 1)
                ins = pe.matmul(MB[:, 0, :], ones[:, 0:P], sq1[:, k, :], start=(k == 0), stop=(k == KT - 1))
            ins.then_inc(S("norm_sum"), 1)
            for a in range(TURNS, N_ROWS):
                row_product(a)
                turn_rows(a - TURNS)
            for a in range(N_ROWS - TURNS, N_ROWS):
                turn_rows(a)
            pe.wait_ge(S("wgl_landed"), 16)
            pe.wait_ge(S("norm_factor"), 1)
            for k in range(KT):
                pe.wait_ge(S("h1_ready"), k + 1)
                ins = pe.matmul(MB[0:32, 0, :], wgl[:, k, :], h1[:, k, :], start=(k == 0), stop=(k == KT - 1))
            ins.then_inc(S("glr_sum"), 1)
            pair = lambda k: 2 * k
            j = 0
            panel(j, pair, 2, "h1_lo")
            j += 1
            pe.wait_ge(S("gate_w_landed"), 32)
            pe.wait_ge(S("glr_ready"), 1)
            for i in range(8):
                if i >= 3:
                    pe.wait_ge(S("gate_biased"), i - 2)
                pe.matmul(MB[:, i % 3, :], wgp[:, i * P:i * P + P], glr, start=True, stop=True)\
                    .then_inc(S("gate_sum"), 1)
            panel(j, pair, 2)
            j += 1
            for _ in range(4):
                token_panel(j, pair, [(0, 0), (0, P), (1, 0), (1, P)])
                j += 1
            for _ in range(6):
                panel(j, pair)
                j += 1
            pe.wait_ge(S("gate_biased"), 8)
            pe.wait_ge(S("keys_decayed"), 1)
            for d in range(2):
                for t in range(2):
                    for h in range(GH):
                        ins = pe.matmul(MB[:, d * 2 + t, h * P:h * P + P], g_e2[:, d * 4 + h, t * P:t * P + P],
                                        g_e1[:, d * 4 + h, t * P:t * P + P], start=True, stop=True)
                    ins.then_inc(S("scores"), 1)
            pe.wait_ge(S("end_keys"), 1)
            for n in range(8):
                t, half = (2, 3, 0, 1)[n // 2], n % 2
                if n < 4:
                    pe.wait_ge(S("scores_masked"), n + 1)
                else:
                    pe.wait_ge(S("keys_turned"), n - 3)
                for i in range(4):
                    ins = pe.transpose(MB[:, n % 4, i * P:i * P + P],
                                       g_e3[:, half * 4 + i, t * P:t * P + P], ident[:])
                ins.then_inc(S("keys_transposed"), 1)
            pe.wait_ge(S("panel_evacuated"), 18)
            for h in range(GH):
                begun = False
                for t in range(2):
                    for v in range(2):
                        for d in range(2):
                            pe.matmul(PB[:, h, v * T + t * P:v * T + t * P + P],
                                      g_v[:, t, h * GDV + v * P:h * GDV + v * P + P],
                                      g_sc[:, (d * 2 + t) * 4 + h, :], start=not begun, stop=False,
                                      skip_group_check=True)
                            begun = True
            pe.wait_ge(S("keys_turned"), 8)
            for i in range(8):
                for t in (2, 3):
                    ins = pe.matmul(MB[:, i // 2, (i % 2) * 256:(i % 2) * 256 + 256], g_kt[:, t, i, :],
                                    g_v[:, t, (i % 4) * GDV:(i % 4) * GDV + GDV], start=(t == 2), stop=(t == 3))
                ins.then_inc(S("state_sum"), 1)
            for s in range(NCH):
                for i in range(8):
                    d, h = i // 4, i % 4
                    c = s if d == 0 else NCH - 1 - s
                    pe.wait_ge(S("state_new"), 8 * s + i // 2 * 2 + 2)
                    for v in range(2):
                        ins = pe.matmul(PB[:, h, v * T + c * CHUNK:v * T + c * CHUNK + CHUNK],
                                        g_s[:, i, v * P:v * P + P], g_e1[:, i, c * CHUNK:c * CHUNK + CHUNK],
                                        start=False, stop=(s == NCH - 1 and d == 1), skip_group_check=True)
                    if s < NCH - 1:
                        p0 = CHUNK * (c % 2)
                        ins = pe.matmul(MB[:, i // 2, (i % 2) * 256:(i % 2) * 256 + 256],
                                        g_kt[p0:p0 + CHUNK, c // 2, i, :],
                                        g_v[p0:p0 + CHUNK, c // 2, h * GDV:h * GDV + GDV], start=True, stop=True)
                        ins.then_inc(S("state_sum"), 1)
                    else:
                        ins.then_inc(S("gla_done"), 1)
            for h in range(GH):
                pe.wait_ge(S("gla_squares"), h + 1)
                for v in range(2):
                    ins = pe.matmul(MB[:, h // 2, (h % 2) * T:(h % 2) * T + T], ones[:, 0:P], g_sq[:, h, v, :],
                                    start=(v == 0), stop=(v == 1))
            ins.then_inc(S("gla_norm_sum"), 1)

            def norm_part(name, count, r, src, bank=0, signal="norm_sum"):
                pe.wait_ge(S(name), count + r + 1)
                for k in (2 * r, 2 * r + 1):
                    ins = pe.matmul(MB[:, bank, 0:T], ones[:, 0:P], src[:, k, :], start=(k == 0),
                                    stop=(k == KT - 1))
                if r == 3:
                    ins.then_inc(S(signal), 1)

            single = lambda k: k
            turn[0] = first["gla_out"][1]
            pe.wait_ge(S("gla_read"), 4)
            for n in range(4):
                panel(j, single, ready=None if n else "gla_lo")
                j += 1
                if n == 0:
                    pe.wait_ge(S("gla_factor"), 1)
                else:
                    norm_part("squares", 0, n - 1, sq2)
            norm_part("squares", 0, 3, sq2)

            for r in range(4):
                if r == 0:
                    pe.wait_ge(S("norm_factor"), 2)
                norm_part("squares", 4, r, sq2)
            for i in range(22):
                panel(j, single, ready=None if i else "h2_lo")
                j += 1

            def project_hidden(j, first_turn, name):
                turn[0] = first_turn
                banks = []
                for i in range(11):
                    for h in range(2):
                        f = 2 * i + h
                        open_half(j, h)
                        pe.wait_ge(S(name), f + 1)
                        for m in range(KT):
                            if f == 0 and m % 2 == 0:
                                banks.append(take_turn())
                            ins = three_pass(PB[:, banks[m // 2], (m % 2) * T:(m % 2) * T + T],
                                             tuple(w[:, m * P:m * P + P] for w in parts_of(j, 4 * h)),
                                             (fhi[:, f, :], flo[:, f, :]),
                                             start=(f == 0 and m % 2 == 0), stop=(f == FT - 1))
                        ins.then_inc(S("multiplied"), 1)
                    j += 1
                return j

            j = project_hidden(j, first["ffn_out"][1], "hidden_lo")
            pe.wait_ge(S("norm_factor"), 3)
            for r in range(4):
                norm_part("squares", 8, r, sq2)

            for i in range(12):
                panel(j, single, ready=None if i else "h3_lo")
                j += 1
                if i:
                    continue
                pe.wait_ge(S("small_landed"), 32)
                pe.wait_ge(S("norm_factor"), 4)
                for part in range(2):
                    for k in range(KT):
                        ins = pe.matmul(MB[0:DH, 0, part * T:part * T + T], w_ba[:, k, part * 8:part * 8 + 8],
                                        h3[:, k, :], start=(k == 0), stop=(k == KT - 1))
                ins.then_inc(S("beta_a_sum"), 1)
            def qk_norm(part):
                pe.wait_ge(S("qk_squares"), part + 1)
                pe.wait_ge(S("rows_ready"), 1)
                if part:
                    pe.wait_ge(S("qk_factor"), 1)
                for b in range(4):
                    ins = pe.matmul(MB[:, b, :], ones[:, 0:P], sq3[:, part * 8 + 2 * b:part * 8 + 2 * b + 2, :],
                                    start=True, stop=True)
                ins.then_inc(S("qk_sums"), 1)

            filled, held = [0], []

            def fill(step):
                while filled[0] < FILL.get(step, 0):
                    q = filled[0]
                    if q % 4 == 0:
                        held[:] = [take_turn()]
                    if q % 2 == 0:
                        open_half(j + q // 4, q // 2 % 2)
                    if not 32 <= q < 48:
                        quarter(j + q // 4, q // 2 % 2, q % 2, held, single)
                    else:
                        ins = token_quarter(j + q // 4, q // 2 % 2, q % 2, held[0], single, (0, q % 2 * P))
                        if q % 2:
                            ins.then_inc(S("multiplied"), 1)
                    filled[0] += 1

            for i in range(4):
                if i == 3:
                    qk_norm(0)
                panel(j, single)
                j += 1
            fill("q_sums")
            qk_norm(1)
            fill("k_sums")
            pe.wait_ge(S("selectors"), 2)
            pe.wait_ge(S("rows_ready"), 2)
            pe.wait_ge(S("rows_act"), 3)
            pe.wait_ge(S("qk_factor"), 2)
            for n, row in enumerate((2, 0, 3)):
                for t in range(2):
                    ins = pe.transpose(MB[:, 0, (n * 2 + t) * DH:(n * 2 + t) * DH + DH],
                                       hm[:, row, t * P:t * P + P], ident[0:DH, 0:DH])
            ins.then_inc(S("tok_rows"), 1)
            pe.wait_ge(S("tok_ready"), 1)
            for n, row in enumerate((2, 0)):
                if n:
                    pe.wait_ge(S("decay_diff"), 1)
                    pe.wait_ge(S("eg_ready"), 1)
                for h in range(DH):
                    ins = pe.matmul(MB[:, h // 2, (h % 2) * T:(h % 2) * T + T], sel[:, h, :], hm[:, row, :],
                                    start=True, stop=True)
                ins.then_inc(S("rows_spread"), 1)
                fill(("gates_spread", "betas_spread")[n])
            pe.wait_ge(S("kb_ready"), 1)

            steps = [("A", None, s_u), ("N2", s_nt, s_n), ("N2T", s_n, s_nt), ("T2", s_n, None), ("N4", s_nt, s_n),
                     ("N4T", s_n, s_nt), ("T4", s_n, None), ("N8", s_nt, s_n), ("T8", s_n, None),
                     ("T", None, None), ("U", s_b32, None), ("W", s_t, s_u), ("T", None, None),
                     ("U", s_b64, None), ("W", s_t, s_u)]
            for t in range(2):
                if t:
                    pe.wait_ge(S("tt_ready"), 5)
                    pe.wait_ge(S("solve_copied"), 9)
                for h in range(DH):
                    for n, rhs in enumerate((qkv, kb)):
                        ins = pe.matmul(MB[:, h // 2, (h % 2) * 256 + n * P:(h % 2) * 256 + n * P + P],
                                        qkv[:, 8 + h, t * P:t * P + P], rhs[:, h, t * P:t * P + P],
                                        start=True, stop=True)
                ins.then_inc(S("qk_products"), 1)
                fill(("products", t))
                tt_of = lambda m: tt_[:, 8 * t + m, :]
                for p, (name, lhs, rhs) in enumerate(steps):
                    for sem, count in SOLVE_WAITS[p]:
                        pe.wait_ge(S(sem), count + t * SOLVE_COUNTS[sem])
                    bank = 2 * (p % 2)
                    for m in range(8):
                        o = MB[:, bank + m // 4, (m % 4) * P:(m % 4) * P + P]
                        if lhs is None:
                            ins = pe.transpose(o, s_u[:, m, :] if name == "A" else tt_of(m), ident[:])
                        else:
                            ins = pe.matmul(o, lhs[:, m, :], tt_of(m) if rhs is None else rhs[:, m, :],
                                            start=True, stop=True)
                    ins.then_inc(S("solve_product"), 1)
                    fill((t, p))
            pe.wait_ge(S("tt_ready"), 10)
            pe.wait_ge(S("solve_copied"), 18)
            for n, base in enumerate((16, 8)):
                for t in range(2):
                    b0 = 2 * (t % 2)
                    if n:
                        pe.wait_ge(S("tok_major"), t + 1)
                    for h in range(DH):
                        ins = pe.transpose(MB[:, b0 + h // 4, (h % 4) * P:(h % 4) * P + P],
                                           qkv[:, base + h, t * P:t * P + P], ident[:])
                    ins.then_inc(S("vk_turned"), 1)
            pe.wait_ge(S("tok_major"), 4)
            for c in range(NCH):
                p0, t = CHUNK * (c % 2), c // 2
                rows = slice(p0, p0 + CHUNK)
                cs = slice(c * CHUNK, c * CHUNK + CHUNK)
                fill(("begun", c))
                if c:
                    pe.wait_ge(S("delta_state"), c)
                    for h in range(DH):
                        ins = pe.matmul(MB[rows, h // 4, (h % 4) * P:(h % 4) * P + P], kb[:, h, cs], st[:, h, :],
                                        start=True, stop=True)
                    ins.then_inc(S("predicted"), 1)
                fill(("predicted", c))
                pe.wait_ge(S("rhs_ready"), c + 1)
                for h in range(DH):
                    ins = pe.matmul(MB[rows, 2 + h // 4, (h % 4) * P:(h % 4) * P + P],
                                    tt_[rows, 8 * t + h, p0:p0 + CHUNK], rr[rows, h * P:h * P + P],
                                    start=True, stop=True)
                ins.then_inc(S("corrected"), 1)
                fill(("corrected", c))
                b = take_turn()
                pe.wait_ge(S("v_new"), c + 1)
                for h in range(DH):
                    o = PB[:, b, h * CHUNK:h * CHUNK + CHUNK]
                    if c:
                        pe.matmul(o, st[:, h, :], eg[:, h, cs], start=True, stop=False)
                    ins = pe.matmul(o, vn[rows, h * P:h * P + P], qkt[rows, 8 * t + h, p0:p0 + CHUNK],
                                    start=(c == 0), stop=True)
                ins.then_inc(S("delta_out"), 1)
                if c < NCH - 1:
                    for h in range(DH):
                        ins = pe.matmul(MB[:, h // 4, (h % 4) * P:(h % 4) * P + P], kd[rows, t, h * P:h * P + P],
                                        vn[rows, h * P:h * P + P], start=True, stop=True)
                    ins.then_inc(S("state_step"), 1)
            j += 12
            pe.wait_ge(S("delta_squares"), 4)
            for b in range(4):
                ins = pe.matmul(MB[:, b, :], ones[:, 0:P], odq[:, 2 * b:2 * b + 2, :], start=True, stop=True)
            ins.then_inc(S("delta_norm_sum"), 1)
            j -= 12
            fill("delta_norm")
            pe.wait_ge(S("delta_factor"), 1)
            pe.wait_ge(S("panel_evacuated"), first["gates"][1])

            def band_scores(h):
                r = slice(BDH * (h % 2), BDH * (h % 2) + BDH)
                if h >= 2:
                    pe.wait_ge(S("band_shifted"), 2 * (h - 1))
                pe.matmul(MB[:, h % 2, 0:P], bq[r, h // 2, 0:P], bk[r, h // 2, 0:P], start=True, stop=True)
                pe.matmul(MB[:, h % 2, P:384], bq[r, h // 2, P:T], bk[r, h // 2, :], start=True, stop=True)\
                    .then_inc(S("band_scores"), 1)

            def band_values(h):
                pe.wait_ge(S("band_probs"), h + 1)
                if h >= 2:
                    pe.wait_ge(S("probs_turned"), h - 1)
                for n in range(3):
                    ins = pe.transpose(MB[:, 2 + h % 2, (0, P, 256)[n]:(0, P, 256)[n] + P],
                                       bp[:, h % 2, n * P:n * P + P], ident[:])
                ins.then_inc(S("probs_transposed"), 1)

            out_bank = []

            def band_out(h):
                pe.wait_ge(S("probs_turned"), h + 1)
                r = slice(BDH * (h % 2), BDH * (h % 2) + BDH)
                if h % 4 == 0:
                    out_bank[:] = [take_turn()]
                o = PB[r, out_bank[0], (h // 2 % 2) * T:(h // 2 % 2) * T + T]
                vcols = slice(h * BDH, h * BDH + BDH)
                pe.matmul(o[:, P:T], bv[:, 1, vcols], bpt[:, h % 2, 256:384], start=True, stop=True)
                pe.matmul(o, bv[:, 0, vcols], bpt[:, h % 2, 0:T], start=False, stop=True,
                          skip_group_check=True).then_inc(S("band_out"), 1)

            band_scores(0)
            band_scores(1)
            for h in range(BH):
                band_values(h)
                if h + 2 < BH:
                    band_scores(h + 2)
                band_out(h)
                fill(("head", h))
            fill("heads_done")
            j += 20
            pe.wait_ge(S("oa_lo"), 1)
            upper = lambda k: 8 + k
            for _ in range(4):
                panel(j, upper)
                j += 1
            pe.wait_ge(S("ob_lo"), 1)
            for _ in range(4):
                panel(j, single)
                j += 1
            for i in range(4):
                panel(j, upper, ready=None if i else "merged_lo")
                j += 1
                if i:
                    norm_part("ln_in", 0, i - 1, y3, 0, "ln_sum")
            norm_part("ln_in", 0, 3, y3, 0, "ln_sum")
            for r in range(4):
                norm_part("ln_squares", 0, r, sq2, 1, "ln_var")
            for i in range(22):
                panel(j, single, ready=None if i else "h4_lo")
                j += 1
            j = project_hidden(j, first["down"][1], "hidden2_lo")
            for r in range(4):
                norm_part("ln_in", 4, r, y3, 0, "ln_sum")
            for r in range(4):
                norm_part("ln_squares", 4, r, sq2, 1, "ln_var")
            assert j == N_SPLIT

        @block.scalar
        def _(act):
            def exp_table():
                act.preload_act_table_set("natural_log_exp_and_others")

            act.dma_start(cols[:], columns).then_inc(S("columns_landed"), 16)
            act.dma_start(xt[:], x).then_inc(S("x_landed"), 16)
            act.dma_start(xc, ctx_x).then_inc(S("x_landed"), 16)
            act.dma_start(cwide[:], bass.AP(c_rows.tensor, 0, [[0, P], [1, D]])).then_inc(S("c_landed"), 16)
            act.dma_start(wgl, w_glr).then_inc(S("wgl_landed"), 16)
            act.dma_start(w_ba[:], w_beta_a).then_inc(S("small_landed"), 16)
            act.dma_start(hrow[:], head_rows).then_inc(S("small_landed"), 16)

            done = [0]
            steps = [0]

            def then(ins):
                steps[0] += 1
                ins.then_inc(S("act_step"), 1)
                act.wait_ge(S("act_step"), steps[0])

            def upper_half(v):
                while done[0] <= min(v, 2 * N_SPLIT - 1):
                    v_, (j, h) = done[0], divmod(done[0], 2)
                    u = 2 * place[("S", j)] + h
                    act.wait_ge(S(f"landed{u % RAW}"), 16 * (u // RAW + 1))
                    if v_ >= PARTS:
                        act.wait_ge(S("multiplied"), v_ - PARTS + 1)
                    act.activation(whi[:, v_ % PARTS, :], raw[:, u % RAW, :], ACT.Copy)\
                        .then_inc(S("upper_ready"), 1)
                    done[0] += 1

            def upper_parts(j):
                upper_half(2 * j + 1)

            def product(j):
                upper_half(2 * j + 4)
                act.wait_ge(S("multiplied"), 2 * j + 2)

            def factor(out_, sums, n, which, name):
                then(act.activation(out_, sums, ACT.Ln, scale=1.0 / n, bias=eps[:, which:which + 1]))
                act.activation(out_, out_, ACT.Exp, scale=-0.5).then_inc(S(name), 1)

            def widen_c(n):
                act.wait_ge(S("c_landed"), 16 * n)
                act.activation(cwide[:], cwide[:], ACT.Silu).then_inc(S("c_wide"), 1)

            act.wait_ge(S("columns_landed"), 16)
            act.activation(cact[:].rearrange("p a b -> p (a b)"), cols[:, 0:16], ACT.Silu).then_inc(S("c_ready"), 1)
            exp_table()
            act.wait_ge(S("x_landed"), 32)
            act.wait_ge(S("constants"), CONSTANTS)
            for k in (0, 4):
                act.activation(sq1[:, k:k + 4, 0:T], xt[:, k:k + 4], ACT.Square)
                act.activation(sq1[:, k:k + 4, T:2 * T], xc[:, k:k + 4], ACT.Square).then_inc(S("input_squares"), 1)
            for a in range(N_ROWS):
                if a == TURNS:
                    act.wait_ge(S("norm_sum"), 1)
                    factor(rs[:], MB[:, 0, :], D, 0, "norm_factor")
                act.wait_ge(S("row_product"), 2 * a + 2)
                act.activation(mod_rows[:, a, :], PB[0:2, a % TURNS, 0:256], ACT.Copy).then_inc(S("rows_read"), 1)
            upper_parts(0)

            def h1_upper(k):
                act.wait_ge(S("h1_ready"), k + 1)
                act.activation(hhi[:, 2 * k:2 * k + 2, :].rearrange("p a b -> p (a b)"), h1[:, k, :], ACT.Copy)\
                    .then_inc(S("h1_hi"), 1)

            for k in range(KT):
                for s in range(2):
                    act.wait_ge(S("h1_scaled"), 2 * k + s + 1)
                    o = h1[:, k, s * T:s * T + T]
                    ins = act.activation(o, o, ACT.Identity, bias=modc[:, k, s:s + 1])
                ins.then_inc(S("h1_ready"), 1)
                if k:
                    h1_upper(k - 1)
            h1_upper(KT - 1)
            widen_c(1)
            upper_parts(1)
            j = 0
            for i in range(2):
                product(j)
                for m in range(2):
                    act.activation(g_k[:, 2 * i + m, :], PB[:, (2 * j + m) % TURNS, :], ACT.Copy)\
                        .then_inc(S("panel_evacuated"), 1)
                upper_parts(j + 2)
                j += 1
            for i in range(4):
                product(j)
                for m in range(2):
                    act.activation(g_v[:, 2 * m:2 * m + 2, i * GDV:i * GDV + GDV],
                                   PB[:, (2 * j + m) % TURNS, :].rearrange("p (a b) -> p a b", a=2), ACT.Copy)\
                        .then_inc(S("panel_evacuated"), 1)
                upper_parts(j + 2)
                j += 1
                x4, e4 = (v[:, i // 2 * 4:i // 2 * 4 + 4, :] for v in (g_x, g_e3))
                if i == 0:
                    act.wait_ge(S("gate_biased"), 8)
                    exp_table()
                if i % 2 == 0:
                    then(act.activation(e4, x4, ACT.Abs))
                if i in (1, 2):
                    then(act.activation(e4, e4, ACT.Exp, scale=-1.0))
                if i % 2:
                    act.activation(e4, e4, ACT.Ln, bias=eps[:, 2:3]).then_inc(S("gate_soft"), 1)
            turn = first["gla_q"][1]

            def bank():
                nonlocal turn
                turn += 1
                return PB[:, (turn - 1) % TURNS, :]

            def pair(b):
                return b.rearrange("p (a b) -> p a b", a=2)

            for i in range(2):
                product(j)
                act.activation(g_q[:, 2 * i:2 * i + 2, :], pair(bank()), ACT.Copy).then_inc(S("panel_evacuated"), 1)
                upper_parts(j + 2)
                j += 1
            act.wait_ge(S("cumulated"), 1)
            act.activation(g_e1, g_x[:, :, 0:T], ACT.Exp, scale=1 / 16).then_inc(S("gate_exp"), 1)
            act.activation(g_e2, g_x[:, :, 0:T], ACT.Exp, scale=-1 / 16).then_inc(S("gate_exp"), 1)
            upper_parts(j + 2)
            act.wait_ge(S("end_diff"), 1)
            act.activation(g_e3, g_e3, ACT.Exp, scale=1 / 16).then_inc(S("gate_exp"), 1)
            for i in range(4):
                product(j)
                act.activation(g_r[:, 2 * i:2 * i + 2, :], pair(bank()), ACT.Silu).then_inc(S("panel_evacuated"), 1)
                upper_parts(j + 2)
                j += 1
            exp_table()
            for n in range(8):
                t, half = (2, 3, 0, 1)[n // 2], n % 2
                act.wait_ge(S("keys_transposed"), n + 1)
                act.activation(g_kt[:, t, half * 4:half * 4 + 4, :].rearrange("p a b -> p (a b)"),
                               MB[:, n % 4, :], ACT.Copy).then_inc(S("keys_turned"), 1)
            act.wait_ge(S("gla_done"), 8)
            for h in range(GH):
                act.activation(g_sq[:, h].rearrange("p a b -> p (a b)"), PB[:, h, :], ACT.Square)\
                    .then_inc(S("gla_squares"), 1)
            upper_parts(13)
            act.wait_ge(S("gla_norm_sum"), 1)
            factor(g_rs.rearrange("p a b -> p (a b)"), MB[:, 0:2, :].rearrange("p a b -> p (a b)"), GDV, 0,
                   "gla_factor")
            def upper_tiles(name, src, done_name, base=0, ready=0, bias=None):
                for k in range(KT):
                    act.wait_ge(S(name), ready + k + 1)
                    if bias is None:
                        ins = act.activation(hhi[:, base + k, :], src(k), ACT.Copy)
                    else:
                        ins = act.activation(hhi[:, base + k, :], src(k), ACT.Identity, bias=bias(k))
                    ins.then_inc(S(done_name), 1)

            upper_tiles("gla_gated", lambda k: g_o[:, k // 2, k % 2, :], "gla_hi")

            def evacuate_scaled(b, r, scale):
                act.activation(sq2[:, 2 * r:2 * r + 2, :], pair(b), ACT.Square).then_inc(S("squares"), 1)
                for m in range(2):
                    f = 2 * r + m
                    ins = act.activation(y1[:, f, :], b[:, m * T:m * T + T], ACT.Identity, scale=scale[:, f:f + 1])
                ins.then_inc(S("panel_evacuated"), 1)

            act.wait_ge(S("gains_ready"), 1)
            for i in range(4):
                if i < 2:
                    product(j)
                act.wait_ge(S("multiplied"), 2 * j + 2)
                evacuate_scaled(bank(), i, gcol)
                if i < 3:
                    upper_parts(j + 2)
                j += 1

            def flat(v):
                return v.rearrange("p a b -> p (a b)")

            act.wait_ge(S("accumulated"), 32)
            act.dma_start(cwide[:], bass.AP(c_rows.tensor, D, [[0, P], [1, D]])).then_inc(S("c_landed"), 16)
            act.wait_ge(S("norm_sum"), 2)
            factor(rs[:, 0:T], MB[:, 0, 0:T], D, 0, "norm_factor")
            for r in range(4):
                act.wait_ge(S("x_new"), r + 1)
                act.activation(sq2[:, 2 * r:2 * r + 2, :], xt[:, 2 * r:2 * r + 2, :], ACT.Square)\
                    .then_inc(S("squares"), 1)
            upper_parts(j + 1)
            act.wait_ge(S("norm_sum"), 3)
            factor(rs[:, 0:T], MB[:, 0, 0:T], D, 0, "norm_factor")
            upper_tiles("h2_scaled", lambda k: h2[:, k, :], "h2_hi", bias=lambda k: modc[:, 24 + k, 0:1])
            widen_c(2)

            def hidden_upper(i, name):
                act.wait_ge(S(name), i + 1)
                act.activation(fhi[:, i, :], f_g[:, i % 2, :], ACT.Copy).then_inc(S("panel_evacuated"), 1)

            for i in range(22):
                product(j)
                act.activation(f_s[:, i % 2, :], bank()[:, 0:T], ACT.Silu).then_inc(S("hidden_silu"), 1)
                upper_parts(j + 2)
                if i:
                    hidden_upper(i - 1, "hidden_gated")
                j += 1
            hidden_upper(21, "hidden_gated")
            exp_table()
            for i in range(11):
                upper_parts(j + 2)
                j += 1
            act.wait_ge(S("multiplied"), 2 * j)
            banks = [bank() for _ in range(4)]
            for r in range(4):
                act.activation(sq2[:, 2 * r:2 * r + 2, :], pair(banks[r]), ACT.Square).then_inc(S("squares"), 1)
            act.wait_ge(S("gains_ready"), 2)
            for r in range(4):
                for m in range(2):
                    f = 2 * r + m
                    ins = act.activation(y1[:, f, :], banks[r][:, m * T:m * T + T], ACT.Identity,
                                         scale=gcol[:, f:f + 1])
                ins.then_inc(S("panel_evacuated"), 1)
            act.wait_ge(S("norm_sum"), 4)
            factor(rs[:, 0:T], MB[:, 0, 0:T], D, 0, "norm_factor")

            upper_tiles("h3_ready", lambda k: h3[:, k, :], "h3_hi")
            act.wait_ge(S("beta_a_sum"), 1)
            act.activation(hm[:, 0, :], MB[0:DH, 0, 0:T], ACT.Sigmoid).then_inc(S("rows_act"), 1)
            act.wait_ge(S("rows_ready"), 1)
            exp_table()
            then(act.activation(hm[:, 4, :], hm[:, 1, :], ACT.Abs))
            then(act.activation(hm[:, 4, :], hm[:, 4, :], ACT.Exp, scale=-1.0))
            act.activation(hm[:, 4, :], hm[:, 4, :], ACT.Ln, bias=eps[0:DH, 2:3])
            act.activation(hrow[:, 0:1], hrow[:, 0:1], ACT.Exp).then_inc(S("rows_act"), 1)
            act.wait_ge(S("rows_ready"), 2)
            act.activation(hm[:, 3, :], hm[:, 5, :], ACT.Exp).then_inc(S("rows_act"), 1)
            for i in range(12):
                product(j)
                b = bank()
                for m in range(2):
                    ins = act.activation(cy[:, i % 2, m, :], b[:, m * T:m * T + T], ACT.Identity,
                                         scale=col("conv_a_2", 72 + 2 * i + m))
                ins.then_inc(S("conv_begun"), 1)
                upper_parts(j + 2)
                act.wait_ge(S("conv_done"), i + 1)
                act.activation(qkv[:, 2 * i:2 * i + 2, :], cy[:, i % 2, :, :], ACT.Silu)\
                    .then_inc(S("panel_evacuated"), 1)
                j += 1
            for i in range(4):
                product(j)
                act.activation(zs[:, 2 * i:2 * i + 2, :], pair(bank()), ACT.Silu).then_inc(S("panel_evacuated"), 1)
                upper_parts(j + 2)
                if i < 2:
                    act.wait_ge(S("panel_evacuated"), first["z"][1])
                    act.activation(sq3[:, 8 * i:8 * i + 8, :], qkv[:, 8 * i:8 * i + 8, :], ACT.Square)\
                        .then_inc(S("qk_squares"), 1)
                j += 1

            taken = [0]

            def tend(step):
                while 2 * taken[0] + 2 <= tended(step):
                    g = taken[0]
                    upper_half(2 * j + g + PARTS)
                    if g % 2 and g < 24:
                        i = g // 2
                        act.wait_ge(S("multiplied"), 2 * j + g + 1)
                        dst = (bq, bk, bv)[i // 4]
                        dst = dst[:, :, i % 4 * 256:i % 4 * 256 + 256] if i >= 8 else dst[:, i % 4 * 2:i % 4 * 2 + 2, :]
                        act.activation(dst, pair(bank()), ACT.Copy, scale=BDH ** -0.5 if i < 4 else 1.0)\
                            .then_inc(S("panel_evacuated"), 1)
                    taken[0] += 1

            exp_table()
            all_banks = MB[:].rearrange("p a b -> p (a b)")
            act.wait_ge(S("qk_sums"), 1)
            factor(rs2, all_banks, 1, 0, "qk_factor")
            tend("q_sums")
            act.wait_ge(S("qk_sums"), 2)
            act.wait_ge(S("qk_normed"), 1)
            factor(rs2, all_banks, 1, 0, "qk_factor")
            tend("k_sums")
            act.wait_ge(S("rows_spread"), 1)
            act.activation(flat(eg), all_banks, ACT.Exp).then_inc(S("eg_ready"), 1)
            act.wait_ge(S("decay_diff"), 1)
            act.activation(dm, dm, ACT.Exp).then_inc(S("decay_exp"), 1)
            tend("gates_spread")
            tend("betas_spread")
            copied = {1: s_n, 2: s_nt, 4: s_n, 5: s_nt, 7: s_n, 9: s_t, 10: s_u, 12: s_t, 13: s_u}
            for t in range(2):
                tend(("products", t))
                for p in range(15):
                    if p in copied:
                        act.wait_ge(S("solve_product"), 15 * t + (p + 1 if p not in (1, 4) else p + 2))
                        b0 = 2 * (p % 2)
                        act.activation(flat(copied[p]), flat(MB[:, b0:b0 + 2, :]), ACT.Copy)\
                            .then_inc(S("solve_copied"), 1)
                    tend((t, p))
            for c in range(NCH):
                rows = slice(CHUNK * (c % 2), CHUNK * (c % 2) + CHUNK)
                cs = slice(c * CHUNK, c * CHUNK + CHUNK)
                tend(("begun", c))
                tend(("predicted", c))
                act.wait_ge(S("corrected"), c + 1)
                act.activation(vn[rows, :], flat(MB[rows, 2:4, :]), ACT.Copy).then_inc(S("v_new"), 1)
                tend(("corrected", c))
                act.wait_ge(S("delta_out"), c + 1)
                b = bank().rearrange("p (a b) -> p a b", a=DH)
                act.activation(odq[:, :, cs], b, ACT.Square).then_inc(S("delta_squares"), 1)
                act.activation(od[:, :, cs], b, ACT.Copy).then_inc(S("panel_evacuated"), 1)
            act.wait_ge(S("band_masked"), 1)
            src = bass.AP(rel_bias.tensor, 0, [[1, 64], [REL, BH], [1, T]])
            act.dma_start(bx[64:128, :, :], src).then_inc(S("bias_landed"), 16)
            src = bass.AP(rel_bias.tensor, 0, [[1, 64], [REL, BH], [1, T - 64]])
            act.dma_start(bx[0:64, :, 64:T], src).then_inc(S("bias_landed"), 16)
            act.wait_ge(S("delta_norm_sum"), 1)
            factor(rs2, all_banks, DDK, 0, "delta_factor")
            tend("delta_norm")

            def evacuate_gates(i):
                act.wait_ge(S("multiplied"), 2 * (j + 12 + i) + 2)
                b = bank()
                for m in range(2):
                    ins = act.activation(ga[:, 2 * i + m, :], b[:, m * T:m * T + T], ACT.Identity,
                                         bias=col("b_gate_2", 2 * i + m))
                ins.then_inc(S("panel_evacuated"), 1)

            def band_exp(h):
                act.wait_ge(S("band_negmax"), h + 1)
                for n, (a, b) in enumerate(((0, P), (P, 384))):
                    act.activation(bp[:, h % 2, a:b], bp[:, h % 2, a:b], ACT.Exp, bias=bst[:, h % 2, 2 + n:3 + n],
                                   accum_out=bst[:, h % 2, 4 + n:5 + n]).then_inc(S("band_exp"), 1)

            band_exp(0)
            for h in range(BH):
                if h + 1 < BH:
                    band_exp(h + 1)
                act.wait_ge(S("probs_transposed"), h + 1)
                if h >= 2:
                    act.wait_ge(S("band_out"), h - 1)
                act.activation(bpt[:, h % 2, :], MB[:, 2 + h % 2, 0:384], ACT.Copy).then_inc(S("probs_turned"), 1)
                tend(("head", h))
                g = h // 4
                if h % 4 == 0 and g < 4:
                    evacuate_gates(2 * g)
                if h % 4 == 3:
                    act.wait_ge(S("band_out"), h + 1)
                    act.activation(ob[:, 2 * g:2 * g + 2, :], pair(bank()), ACT.Copy).then_inc(S("panel_evacuated"), 1)
                    if g < 3:
                        evacuate_gates(2 * g + 1)
            tend("heads_done")
            act.wait_ge(S("band_scores"), BH)
            act.wait_ge(S("delta_gated"), 1)
            act.activation(flat(hhi[:, 8:16, :]), flat(od), ACT.Copy).then_inc(S("oa_hi"), 1)
            act.wait_ge(S("multiplied"), 2 * j + 40)
            evacuate_gates(7)
            j += 20
            act.wait_ge(S("panel_evacuated"), first["branch_a"][1])
            act.activation(ga, ga, ACT.Sigmoid).then_inc(S("gates_open"), 1)
            exp_table()
            act.activation(flat(hhi[:, 0:8, :]), flat(ob), ACT.Copy).then_inc(S("ob_hi"), 1)
            def merged_upper(i):
                act.wait_ge(S("merged"), i + 1)
                act.activation(hhi[:, 8 + 2 * i:10 + 2 * i, :], ya[:, 2 * i:2 * i + 2, :], ACT.Copy)\
                    .then_inc(S("merged_hi"), 1)

            for dst in (ya, yb):
                for i in range(4):
                    product(j)
                    act.activation(dst[:, 2 * i:2 * i + 2, :], pair(bank()), ACT.Copy)\
                        .then_inc(S("panel_evacuated"), 1)
                    if dst is yb and i == 3:
                        merged_upper(2)
                        merged_upper(3)
                    upper_parts(j + 2)
                    j += 1
                    if dst is yb and i in (1, 2):
                        merged_upper(i - 1)
            for i in range(4):
                product(j)
                b = bank()
                for m in range(2):
                    f = 2 * i + m
                    ins = act.activation(y3[:, f, :], b[:, m * T:m * T + T], ACT.Identity,
                                         scale=mod2[:, 16 + f:17 + f])
                ins.then_inc(S("panel_evacuated"), 1)
                upper_parts(j + 2)
                j += 1

            def layer_norm(count, name, dst, done_name):
                act.wait_ge(S("ln_sum"), count)
                act.activation(rs[:, 0:T], MB[:, 0, 0:T], ACT.Copy, scale=1.0 / D).then_inc(S("ln_mean"), 1)
                for r in range(4):
                    act.wait_ge(S("ln_centred"), 4 * count + r - 3)
                    act.activation(sq2[:, 2 * r:2 * r + 2, :], y3[:, 2 * r:2 * r + 2, :], ACT.Square)\
                        .then_inc(S("ln_squares"), 1)
                act.wait_ge(S("ln_var"), count)
                factor(rs[:, T:2 * T], MB[:, 1, 0:T], D, 1, "ln_factor")
                for k in range(KT):
                    act.wait_ge(S("ln_scaled"), 8 * (count - 1) + k + 1)
                    act.activation(dst[:, k, :], y3[:, k, :], ACT.Identity, bias=col(name, k))\
                        .then_inc(S(done_name), 1)
                    if count == 1 and k >= 2:
                        h4_upper(k - 2)

            def h4_upper(k):
                act.wait_ge(S("h4_ready"), k + 1)
                act.activation(hhi[:, k, :], h2[:, k, :], ACT.Copy).then_inc(S("h4_hi"), 1)

            layer_norm(1, "ln1_b_2", xt, "x3_ready")
            h4_upper(6)
            h4_upper(7)
            for i in range(22):
                product(j)
                b = bank()
                for m in range(2):
                    ins = act.activation(f_u[:, i % 2, m, :], b[:, m * T:m * T + T], ACT.Identity,
                                         scale=col("conv_ffn_2", 88 + 22 * m + i),
                                         bias=col("b_conv_ffn_2", 22 * m + i))
                ins.then_inc(S("up_begun"), 1)
                upper_parts(j + 2)
                if i:
                    hidden_upper(i - 1, "hidden2_gated")
                act.wait_ge(S("up_done"), i + 1)
                act.activation(f_s[:, i % 2, :], f_u[:, i % 2, 0, :], ACT.Silu).then_inc(S("hidden2_silu"), 1)
                j += 1
            hidden_upper(21, "hidden2_gated")
            exp_table()
            for i in range(11):
                upper_parts(j + 2)
                j += 1
            act.wait_ge(S("multiplied"), 2 * j)
            for r in range(4):
                b = bank()
                for m in range(2):
                    f = 2 * r + m
                    ins = act.activation(y3[:, f, :], b[:, m * T:m * T + T], ACT.Identity,
                                         scale=mod2[:, 40 + f:41 + f])
                ins.then_inc(S("panel_evacuated"), 1)
            layer_norm(2, "ln2_b_2", f_out, "out_ready")

        @block.vector
        def _(dve):
            done = [0]
            steps = [0]

            def then(ins):
                steps[0] += 1
                ins.then_inc(S("dve_step"), 1)
                dve.wait_ge(S("dve_step"), steps[0])

            def lower_half(v):
                while done[0] <= min(v, 2 * N_SPLIT - 1):
                    v_, (j, h) = done[0], divmod(done[0], 2)
                    u = 2 * place[("S", j)] + h
                    dve.wait_ge(S("upper_ready"), v_ + 1)
                    dve.tensor_tensor(wlo[:, v_ % PARTS, :], raw[:, u % RAW, :],
                                      whi[:, v_ % PARTS, :].bitcast(F32), ALU.subtract)\
                        .then_inc(S("parts_ready"), 1)
                    done[0] += 1

            def lower_parts(j):
                lower_half(2 * j + 1)

            def flat(v):
                return v.rearrange("p a b -> p (a b)")

            def lower(dst, full, upper, name):
                dve.tensor_tensor(dst, full, upper.bitcast(F32), ALU.subtract).then_inc(S(name), 1)

            def over_tokens(v, n=T):
                return v.unsqueeze(2).to_broadcast([v.shape[0], v.shape[1], n])

            def over_tiles(v, n):
                return v.unsqueeze(1).to_broadcast([v.shape[0], n, v.shape[1]])

            fed = [0]

            def accumulate(count=1):
                for _ in range(count):
                    n = fed[0]
                    fed[0] += 1
                    if n in (0, 16):
                        dve.wait_ge(S("c_wide"), 1 + n // 16)
                    for h in range(2):
                        u = 2 * place[("A", n)] + h
                        dst = modc[:, 16 + 2 * n + h, 0:1] if n < 16 else mod2[:, 2 * n - 32 + h:2 * n - 31 + h]
                        dve.wait_ge(S(f"landed{u % RAW}"), 16 * (u // RAW + 1))
                        dve.tensor_tensor_reduce(raw[:, u % RAW, :], raw[:, u % RAW, :], cwide[:], 1.0, 0.0,
                                                 ALU.mult, ALU.add, dst).then_inc(S("accumulated"), 1)

            dve.wait_ge(S("constants"), CONSTANTS)
            dve.wait_ge(S("columns_landed"), 16)
            dve.wait_ge(S("x_landed"), 32)
            lower_parts(0)
            dve.wait_ge(S("rows_turned"), 1)
            then(dve.tensor_tensor(modc[:, 0:16, :], MB[:, 1, 0:32].rearrange("p (a b) -> p a b", b=2),
                                   over_tokens(col("mod_b", 0, 16), 2), ALU.add))
            for s in range(2):
                ins = dve.scalar_tensor_tensor(sc_a[:, s, :], modc[:, 8:16, s], 1.0, col("norm_g", 0, 8),
                                               ALU.add, ALU.mult)
            then(ins)
            dve.wait_ge(S("norm_factor"), 1)
            def h1_lower(k):
                dve.wait_ge(S("h1_hi"), k + 1)
                lower(flat(hlo[:, 2 * k:2 * k + 2, :]), h1[:, k, :], flat(hhi[:, 2 * k:2 * k + 2, :]), "h1_lo")

            for k in range(KT):
                for s in range(2):
                    dve.scalar_tensor_tensor(h1[:, k, s * T:s * T + T], (xt[:], xc)[s][:, k, :],
                                             sc_a[:, s, k:k + 1], rs[:, s * T:s * T + T], ALU.mult, ALU.mult)\
                        .then_inc(S("h1_scaled"), 1)
                if k >= 2:
                    h1_lower(k - 2)
            h1_lower(6)
            h1_lower(7)
            dve.wait_ge(S("glr_sum"), 1)
            dve.tensor_copy(glr, MB[0:32, 0, :]).then_inc(S("glr_ready"), 1)
            accumulate(2)
            lower_parts(1)
            for i in range(8):
                dve.wait_ge(S("gate_sum"), i + 1)
                dve.tensor_scalar(g_x[:, i, :], MB[:, i % 3, :], col("gla_b_gate", i), None, ALU.add)\
                    .then_inc(S("gate_biased"), 1)
            for j in range(2, 7):
                accumulate(2)
                lower_parts(j)
            for i in range(8):
                if i % 4 == 0:
                    dve.wait_ge(S("gate_soft"), i // 4 + 1)
                    x4, e4 = g_x[:, i:i + 4, :], g_e3[:, i:i + 4, :]
                    then(dve.scalar_tensor_tensor(flat(x4), flat(x4), 0.0, flat(e4), ALU.min, ALU.subtract))
                for a, n in [(c * CHUNK, CHUNK) for c in range(NCH)] + [(T, T)]:
                    v = g_x[:, i, a:a + n]
                    if i >= 4:
                        v = v[:, ::-1]
                    ins = dve.tensor_tensor_scan(v, ones[:, 0:n], v, 0.0, ALU.mult, ALU.add)
                if i % 3 == 2:
                    lower_parts(7 + i // 3)
            ins.then_inc(S("cumulated"), 1)
            dve.wait_ge(S("cumulated"), 1)
            for d in range(2):
                b = g_x[:, 4 * d:4 * d + 4, 0:T].rearrange("p h (c t) -> p h c t", t=CHUNK)
                e = CHUNK - 1 if d == 0 else 0
                dve.tensor_tensor(g_e3[:, 4 * d:4 * d + 4, 0:T].rearrange("p h (c t) -> p h c t", t=CHUNK),
                                  b[:, :, :, e:e + 1].to_broadcast([P, GH, NCH, CHUNK]), b, ALU.subtract)
                b = g_x[:, 4 * d:4 * d + 4, T:2 * T]
                e = T - 1 if d == 0 else 0
                ins = dve.tensor_tensor(g_e3[:, 4 * d:4 * d + 4, T:2 * T],
                                        b[:, :, e:e + 1].to_broadcast([P, GH, T]), b, ALU.subtract)
            ins.then_inc(S("end_diff"), 1)
            dve.wait_ge(S("panel_evacuated"), first["gla_r"][1])
            dve.wait_ge(S("gate_exp"), 2)
            for d in range(2):
                e = g_e1[:, 4 * d:4 * d + 4, :].rearrange("p h (c t) -> p h c t", t=CHUNK)
                end = CHUNK - 1 if d == 0 else 0
                ins = dve.tensor_copy(dec[:, 4 * d:4 * d + 4, :], e[:, :, :, end])
            then(ins)
            for d in range(2):
                q4 = g_e1[:, 4 * d:4 * d + 4, :]
                dve.scalar_tensor_tensor(flat(q4), flat(q4), GDK ** -0.5, flat(g_q), ALU.mult, ALU.mult)
                k4 = g_e2[:, 4 * d:4 * d + 4, :]
                ins = dve.tensor_tensor(k4, k4, g_k[:, :, 0:T], ALU.mult)
            ins.then_inc(S("keys_decayed"), 1)
            lower_parts(10)
            dve.wait_ge(S("gate_exp"), 3)
            for d in range(2):
                k4 = g_e3[:, 4 * d:4 * d + 4, :]
                ins = dve.tensor_tensor(k4, k4, g_k, ALU.mult)
            ins.then_inc(S("end_keys"), 1)
            lower_parts(11)
            dve.wait_ge(S("accumulated"), 24)
            then(dve.tensor_tensor(modc[:, 16:40, 0], modc[:, 16:40, 0], col("mod_b", 16, 24), ALU.add))
            dve.wait_ge(S("scores_zeroed"), 1)
            for g in range(4):
                dve.wait_ge(S("scores"), g + 1)
                mask = (causal_t, causal_dn)[g // 2]
                dve.copy_predicated(g_sc[:, 4 * g:4 * g + 4, :], over_tiles(mask[:].bitcast(I32), 4),
                                    MB[:, g, :].rearrange("p (a b) -> p a b", a=4)).then_inc(S("scores_masked"), 1)
            for i in range(8):
                dve.wait_ge(S("state_sum"), i // 2 * 2 + 2)
                dve.tensor_copy(g_s[:, i, :], MB[:, i // 2, (i % 2) * 256:(i % 2) * 256 + 256])\
                    .then_inc(S("state_new"), 1)
            for s in range(NCH - 1):
                for i in range(8):
                    c = s if i < 4 else NCH - 1 - s
                    dve.wait_ge(S("state_sum"), 8 * (s + 1) + i // 2 * 2 + 2)
                    dve.scalar_tensor_tensor(g_s[:, i, :], g_s[:, i, :], dec[:, i, c:c + 1],
                                             MB[:, i // 2, (i % 2) * 256:(i % 2) * 256 + 256], ALU.mult, ALU.add)\
                        .then_inc(S("state_new"), 1)
            for h in range(GH):
                dve.wait_ge(S("gla_squares"), h + 1)
                for v in range(2):
                    ins = dve.scalar_tensor_tensor(g_o[:, h, v, :], PB[:, h, v * T:v * T + T],
                                                   col("gla_norm_g", v), g_r[:, 2 * h + v, :], ALU.mult, ALU.mult)
                ins.then_inc(S("gla_read"), 1)
            dve.wait_ge(S("gla_read"), 4)
            dve.tensor_tensor(gcol[:], modc[:, 16:24, 0], col("norm_g", 8, 8), ALU.mult)\
                .then_inc(S("gains_ready"), 1)
            lower_parts(13)
            dve.wait_ge(S("gla_factor"), 1)

            def lower_tile(k, src, name, base=0, bias=None):
                dve.wait_ge(S(name + "_hi"), k + 1)
                hi, lo = hhi[:, base + k, :].bitcast(F32), hlo[:, base + k, :]
                if bias is None:
                    ins = dve.tensor_tensor(lo, src, hi, ALU.subtract)
                else:
                    ins = dve.scalar_tensor_tensor(lo, src, bias, hi, ALU.add, ALU.subtract)
                ins.then_inc(S(name + "_lo"), 1)

            def staggered(make, split, behind=2, n=KT):
                for k in range(n + behind):
                    if k < n:
                        make(k)
                    if k >= behind:
                        split(k - behind)

            g_ot = lambda k: g_o[:, k // 2, k % 2, :]
            staggered(lambda k: dve.tensor_tensor(g_ot(k), g_ot(k), g_rs[:, k // 2, :], ALU.mult)
                      .then_inc(S("gla_gated"), 1),
                      lambda k: lower_tile(k, g_ot(k), "gla"))
            j = 12
            for i in range(4):
                accumulate()
                if i < 3:
                    lower_parts(j + 2)
                j += 1

            def group(v, r):
                return v[:, 2 * r:2 * r + 2, :]

            def add_normed(r):
                dve.wait_ge(S("dve_step"), steps[0])
                dve.tensor_tensor(group(xt, r), group(xt, r), group(y1, r), ALU.add).then_inc(S("x_new"), 1)

            def normed(count, r):
                if r == 0:
                    dve.wait_ge(S("norm_factor"), count)
                steps[0] += 1
                dve.tensor_tensor(group(y1, r), group(y1, r), over_tiles(rs[:, 0:T], 2), ALU.mult)\
                    .then_inc(S("dve_step"), 1)

            then(dve.scalar_tensor_tensor(sc_a[:, 0, :], modc[:, 32:40, 0], 1.0, col("norm_g", 16, 8),
                                          ALU.add, ALU.mult))
            dve.wait_ge(S("panel_evacuated"), 22)
            for r in range(4):
                normed(2, r)
                add_normed(r)
            lower_parts(j + 1)
            dve.wait_ge(S("x_new"), 4)
            dve.wait_ge(S("norm_factor"), 3)
            staggered(lambda k: dve.scalar_tensor_tensor(h2[:, k, :], xt[:, k, :], sc_a[:, 0, k:k + 1],
                                                         rs[:, 0:T], ALU.mult, ALU.mult)
                      .then_inc(S("h2_scaled"), 1),
                      lambda k: lower_tile(k, h2[:, k, :], "h2", bias=modc[:, 24 + k, 0:1]))

            def hidden_lower(i, evacuated, name):
                dve.wait_ge(S("panel_evacuated"), evacuated + i + 1)
                lower(flo[:, i, :], f_g[:, i % 2, :], fhi[:, i, :], name)

            t0 = first["ffn_in"][1]
            accumulate()
            for i in range(22):
                if i >= 2:
                    dve.wait_ge(S("hidden_lo"), i - 1)
                accumulate()
                lower_half(2 * j + 4)
                dve.wait_ge(S("hidden_silu"), i + 1)
                dve.tensor_tensor(f_g[:, i % 2, :], f_s[:, i % 2, :], PB[:, (t0 + i) % TURNS, T:2 * T], ALU.mult)\
                    .then_inc(S("hidden_gated"), 1)
                lower_parts(j + 2)
                if i:
                    hidden_lower(i - 1, t0, "hidden_lo")
                j += 1
            hidden_lower(21, t0, "hidden_lo")
            for i in range(11):
                if i < 1:
                    accumulate()
                lower_parts(j + 2)
                j += 1
                if i == 1:
                    dve.wait_ge(S("accumulated"), 80)
                    then(dve.tensor_tensor(modc[:, 40:48, 0], modc[:, 40:48, 0], col("mod_b", 40, 8), ALU.add))
                    dve.tensor_tensor(gcol[:], modc[:, 40:48, 0], col("norm_g", 24, 8), ALU.mult)\
                        .then_inc(S("gains_ready"), 1)
                    then(dve.tensor_tensor(mod2[:], mod2[:], col("b_ada_2", 0, 48), ALU.add))
                    then(dve.tensor_scalar(sc_a[:, 1, :], mod2[:, 8:16], 1.0, None, ALU.add))
            dve.wait_ge(S("panel_evacuated"), first["qkv"][1])

            def make_h3(k):
                if k % 2 == 0:
                    normed(4, k // 2)
                    add_normed(k // 2)
                    dve.wait_ge(S("x_new"), 5 + k // 2)
                dve.tensor_scalar(h3[:, k, :], xt[:, k, :], sc_a[:, 1, k:k + 1], mod2[:, k:k + 1],
                                  ALU.mult, ALU.add).then_inc(S("h3_ready"), 1)

            staggered(make_h3, lambda k: lower_tile(k, h3[:, k, :], "h3"), behind=1)
            dve.wait_ge(S("rows_act"), 1)
            dve.tensor_scalar(hm[:, 1, :], MB[0:DH, 0, T:2 * T], hrow[:, 1:2], None, ALU.add)\
                .then_inc(S("rows_ready"), 1)
            dve.wait_ge(S("rows_act"), 2)
            then(dve.scalar_tensor_tensor(hm[:, 6, :], hm[:, 1, :], 0.0, hm[:, 4, :], ALU.max, ALU.add))
            then(dve.tensor_scalar(hm[:, 1, :], hm[:, 6, :], hrow[:, 0:1], -1.0, ALU.mult, ALU.mult))
            for c in range(NCH):
                cs = slice(c * CHUNK, c * CHUNK + CHUNK)
                ins = dve.tensor_tensor_scan(hm[:, 2, cs], ones[0:DH, 0:CHUNK], hm[:, 1, cs], 0.0,
                                             ALU.mult, ALU.add)
            then(ins)
            rows = hm[:, 2, :].rearrange("p (c t) -> p c t", t=CHUNK)
            dve.tensor_tensor(hm[:, 5, :].rearrange("p (c t) -> p c t", t=CHUNK),
                              rows[:, :, CHUNK - 1:CHUNK].to_broadcast([DH, NCH, CHUNK]), rows, ALU.subtract)\
                .then_inc(S("rows_ready"), 1)
            dve.wait_ge(S("constants"), ALL_CONSTANTS)
            t0 = first["qkv"][1]
            for i in range(12):
                lower_half(2 * j + 4)
                dve.wait_ge(S("conv_begun"), i + 1)
                b = PB[:, (t0 + i) % TURNS, :]
                for s in range(1, 4):
                    for m in range(2):
                        o = cy[:, i % 2, m, s:T]
                        ins = dve.scalar_tensor_tensor(o, b[:, m * T:m * T + T - s],
                                                       col("conv_a_2", 24 * (3 - s) + 2 * i + m), o,
                                                       ALU.mult, ALU.add)
                    if s < 3:
                        then(ins)
                ins.then_inc(S("conv_done"), 1)
                lower_parts(j + 2)
                j += 1
            for i in range(4):
                lower_parts(j + 2)
                j += 1
            taken = [0]

            def tend(step):
                while 2 * taken[0] + 2 <= tended(step):
                    lower_half(2 * j + taken[0] + PARTS)
                    taken[0] += 1

            dve.wait_ge(S("qk_factor"), 1)
            dve.scalar_tensor_tensor(flat(qkv[:, 0:8, :]), flat(qkv[:, 0:8, :]), DDK ** -0.5, rs2,
                                     ALU.mult, ALU.mult).then_inc(S("qk_normed"), 1)
            tend("q_sums")
            dve.wait_ge(S("qk_factor"), 2)
            kc = qkv[:, 8:16, :]
            dve.tensor_tensor(flat(kc), flat(kc), rs2, ALU.mult).then_inc(S("qk_normed"), 1)
            tend("k_sums")
            dve.wait_ge(S("tok_rows"), 1)
            dve.tensor_copy(mod_flat[:, 0:48], MB[:, 0, 0:48]).then_inc(S("tok_ready"), 1)
            dve.wait_ge(S("tok_ready"), 1)
            dve.wait_ge(S("rows_spread"), 1)
            dve.wait_ge(S("eg_ready"), 1)
            for t in range(2):
                for h in range(DH):
                    a = (h % 2) * T + t * P
                    ins = dve.tensor_scalar(dm[:, t * 8 + h, :], MB[:, h // 2, a:a + P],
                                            gl_tok[:, 0, t, h:h + 1], 0.0, ALU.subtract, ALU.min)
            ins.then_inc(S("decay_diff"), 1)
            dve.wait_ge(S("decay_exp"), 1)
            then(dve.tensor_tensor(dm, dm, over_tiles(causal_t[:], 16), ALU.mult))
            dve.tensor_copy(gl_end, eg.rearrange("p h (c t) -> p h c t", t=CHUNK)[:, :, :, CHUNK - 1])
            tend("gates_spread")
            dve.wait_ge(S("rows_spread"), 2)
            dve.tensor_tensor(flat(kb), flat(kc), MB[:].rearrange("p a b -> p (a b)"), ALU.mult)\
                .then_inc(S("kb_ready"), 1)
            tend("betas_spread")
            for t in range(2):
                dve.wait_ge(S("qk_products"), t + 1)
                prod = MB[:].rearrange("p a (b c) -> p (a b) c", c=256)
                dmt = dm[:, 8 * t:8 * t + 8, :]
                dve.tensor_tensor(qkt[:, 8 * t:8 * t + 8, :], prod[:, :, 0:P], dmt, ALU.mult)
                then(dve.tensor_tensor(s_u, prod[:, :, P:2 * P], dmt, ALU.mult))
                dve.sem_inc(S("at_ready"), 1)
                tt8 = tt_[:, 8 * t:8 * t + 8, :]
                then(dve.scalar_tensor_tensor(s_nt, s_u, -1.0, over_tiles(m16t, 8), ALU.mult, ALU.mult))
                dve.tensor_tensor(tt8, s_nt, over_tiles(ident[:], 8), ALU.add)

                def pair_banks(p):
                    b0 = 2 * (p % 2)
                    return MB[:, b0:b0 + 2, :].rearrange("p a (b c) -> p (a b) c", c=P)

                tend(("products", t))
                dve.wait_ge(S("solve_product"), 15 * t + 1)
                dve.scalar_tensor_tensor(s_n, pair_banks(0), -1.0, over_tiles(m16, 8), ALU.mult, ALU.mult)
                dve.tensor_tensor(s_b32, pair_banks(0), over_tiles(d32, 8), ALU.mult)
                dve.tensor_tensor(s_b64, pair_banks(0), over_tiles(d64, 8), ALU.mult)\
                    .then_inc(S("solve_masked"), 1)
                tend((t, 0))
                for p, op in ((3, ALU.add), (6, ALU.add), (8, ALU.add), (11, ALU.subtract), (14, ALU.subtract)):
                    for before in range(1, p):
                        tend((t, before))
                    dve.wait_ge(S("solve_product"), 15 * t + p + 1)
                    dve.tensor_tensor(tt8, tt8, pair_banks(p), op).then_inc(S("tt_ready"), 1)
                    tend((t, p))
            then(dve.tensor_tensor(flat(kb), flat(kb), flat(eg), ALU.mult))
            dve.tensor_tensor(flat(eg), flat(eg), flat(qkv[:, 0:8, :]), ALU.mult)
            for n, dst in enumerate((vb, kd)):
                for t in range(2):
                    dve.wait_ge(S("vk_turned"), 2 * n + t + 1)
                    dve.tensor_tensor(dst[:, t, :].rearrange("p (a b) -> p a b", b=P), pair_banks(t),
                                      over_tokens(gl_tok[:, 1 + n, t, :], P), ALU.mult)\
                        .then_inc(S("tok_major"), 1)
            dve.wait_ge(S("tok_major"), 4)
            for c in range(NCH):
                rows = slice(CHUNK * (c % 2), CHUNK * (c % 2) + CHUNK)
                t = c // 2
                tend(("begun", c))
                if c == 0:
                    dve.tensor_copy(rr[rows, :], vb[rows, t, :]).then_inc(S("rhs_ready"), 1)
                else:
                    dve.wait_ge(S("predicted"), c)
                    dve.tensor_tensor(rr[rows, :], vb[rows, t, :], flat(MB[rows, 0:2, :]), ALU.subtract)\
                        .then_inc(S("rhs_ready"), 1)
                tend(("predicted", c))
                tend(("corrected", c))
                if c < NCH - 1:
                    if c:
                        dve.wait_ge(S("delta_out"), c + 1)
                        then(dve.tensor_tensor(st, st, over_tokens(gl_end[:, :, c], P), ALU.mult))
                    dve.wait_ge(S("state_step"), c + 1)
                    if c:
                        ins = dve.tensor_tensor(flat(st), flat(st), flat(MB[:, 0:2, :]), ALU.add)
                    else:
                        ins = dve.tensor_copy(flat(st), flat(MB[:, 0:2, :]))
                    ins.then_inc(S("delta_state"), 1)
                dve.wait_ge(S("panel_evacuated"), first["band_v"][1] + 2 * c + 2)
                oc = od[:, :, c * CHUNK:c * CHUNK + CHUNK]
                dve.scalar_tensor_tensor(oc, oc, col("norm_a_2"), zs[:, :, c * CHUNK:c * CHUNK + CHUNK],
                                         ALU.mult, ALU.mult).then_inc(S("delta_scaled"), 1)
            dve.wait_ge(S("delta_out"), 4)
            dve.memset(bx[0:64, :, 0:64], NEG).then_inc(S("band_masked"), 1)
            dve.wait_ge(S("delta_scaled"), 4)
            dve.wait_ge(S("delta_factor"), 1)
            dve.tensor_tensor(flat(od), flat(od), rs2, ALU.mult).then_inc(S("delta_gated"), 1)
            tend("delta_norm")
            dve.wait_ge(S("delta_gated"), 1)
            dve.wait_ge(S("bias_landed"), 32)

            def band_shift(h):
                dve.wait_ge(S("band_scores"), h + 1)
                if h >= 2:
                    dve.wait_ge(S("probs_transposed"), h - 1)
                for n, (a, b) in enumerate(((0, P), (P, 384))):
                    dve.tensor_tensor_reduce(bp[:, h % 2, a:b], MB[:, h % 2, a:b], bx[:, h, 0:b - a][:, ::-1],
                                             1.0, NEG, ALU.add, ALU.max, bst[:, h % 2, n:n + 1])\
                        .then_inc(S("band_shifted"), 1)
                dve.wait_ge(S("band_shifted"), 2 * h + 2)
                dve.tensor_scalar(bst[:, h % 2, 2:4], bst[:, h % 2, 0:2], -1.0, None, ALU.mult)\
                    .then_inc(S("band_negmax"), 1)

            band_shift(0)
            for h in range(BH):
                if h + 1 < BH:
                    band_shift(h + 1)
                dve.wait_ge(S("band_exp"), 2 * h + 2)
                then(dve.reciprocal(bst[:, h % 2, 6:8], bst[:, h % 2, 4:6]))
                for n, (a, b) in enumerate(((0, P), (P, 384))):
                    ins = dve.tensor_scalar(bp[:, h % 2, a:b], bp[:, h % 2, a:b], bst[:, h % 2, 6 + n:7 + n],
                                            None, ALU.mult)
                ins.then_inc(S("band_probs"), 1)
                tend(("head", h))
            tend("heads_done")
            j += 20
            dve.wait_ge(S("oa_hi"), 1)
            lower(flat(hlo[:, 8:16, :]), flat(od), flat(hhi[:, 8:16, :]), "oa_lo")
            dve.wait_ge(S("ob_hi"), 1)
            lower(flat(hlo[:, 0:8, :]), flat(ob), flat(hhi[:, 0:8, :]), "ob_lo")
            def merge(i):
                dve.wait_ge(S("panel_evacuated"), first["branch_b"][1] + i + 1)
                then(dve.tensor_tensor(group(yb, i), group(yb, i), ga[:, 8 + 2 * i:10 + 2 * i, :], ALU.mult))
                dve.tensor_tensor(group(ya, i), group(ya, i), group(yb, i), ALU.add).then_inc(S("merged"), 1)

            def residual(turn, r):
                dve.wait_ge(S("panel_evacuated"), turn + r + 1)
                dve.scalar_tensor_tensor(group(y3, r), group(xt, r), ALPHA, group(y3, r), ALU.mult, ALU.add)\
                    .then_inc(S("ln_in"), 1)

            def merged_lower(i):
                dve.wait_ge(S("merged_hi"), i + 1)
                for k in (2 * i, 2 * i + 1):
                    dve.tensor_tensor(hlo[:, 8 + k, :], ya[:, k, :], hhi[:, 8 + k, :].bitcast(F32), ALU.subtract)\
                        .then_inc(S("merged_lo"), 1)

            for i in range(4):
                lower_parts(j + 2)
                j += 1
            dve.wait_ge(S("gates_open"), 1)
            dve.wait_ge(S("panel_evacuated"), first["branch_b"][1])
            then(dve.tensor_tensor(ya, ya, ga[:, 0:8, :], ALU.mult))
            for i in range(4):
                if i < 3:
                    lower_parts(j + 2)
                merge(i)
                if i:
                    merged_lower(i - 1)
                j += 1
            merged_lower(3)
            lower_parts(j + 1)
            for i in range(4):
                lower_parts(j + 2)
                residual(first["mix"][1], i)
                j += 1

            def layer_norm(count, gain, after=None):
                dve.wait_ge(S("ln_in"), 4 * count)
                dve.wait_ge(S("ln_mean"), count)
                for r in range(4):
                    dve.tensor_tensor(group(y3, r), group(y3, r), over_tiles(rs[:, 0:T], 2), ALU.subtract)\
                        .then_inc(S("ln_centred"), 1)
                dve.wait_ge(S("ln_centred"), 4 * count)
                dve.wait_ge(S("ln_factor"), count)
                for k in range(KT):
                    dve.scalar_tensor_tensor(y3[:, k, :], y3[:, k, :], col(gain, k), rs[:, T:2 * T],
                                             ALU.mult, ALU.mult).then_inc(S("ln_scaled"), 1)
                    if after:
                        after(k)

            def h4(k):
                dve.wait_ge(S("x3_ready"), k + 1)
                dve.tensor_scalar(h2[:, k, :], xt[:, k, :], sc_a[:, 1, k:k + 1], mod2[:, 24 + k:25 + k],
                                  ALU.mult, ALU.add).then_inc(S("h4_ready"), 1)

            def after_ln1(k):
                if k >= 1:
                    h4(k - 1)
                if k >= 3:
                    lower_tile(k - 3, h2[:, k - 3, :], "h4")

            then(dve.tensor_scalar(sc_a[:, 1, :], mod2[:, 32:40], 1.0, None, ALU.add))
            layer_norm(1, "ln1_g_2", after_ln1)
            h4(7)
            for k in (5, 6, 7):
                lower_tile(k, h2[:, k, :], "h4")
            t0 = first["up"][1]
            for i in range(22):
                lower_half(2 * j + 4)
                dve.wait_ge(S("up_begun"), i + 1)
                b = PB[:, (t0 + i) % TURNS, :]
                for s in range(1, 3):
                    for m in range(2):
                        o = f_u[:, i % 2, m, s:T]
                        ins = dve.scalar_tensor_tensor(o, b[:, m * T:m * T + T - s],
                                                       col("conv_ffn_2", 44 * (2 - s) + 22 * m + i), o,
                                                       ALU.mult, ALU.add)
                    if s < 2:
                        then(ins)
                ins.then_inc(S("up_done"), 1)
                lower_parts(j + 2)
                if i:
                    hidden_lower(i - 1, t0, "hidden2_lo")
                if i >= 2:
                    dve.wait_ge(S("hidden2_lo"), i - 1)
                dve.wait_ge(S("hidden2_silu"), i + 1)
                dve.tensor_tensor(f_g[:, i % 2, :], f_s[:, i % 2, :], f_u[:, i % 2, 1, :], ALU.mult)\
                    .then_inc(S("hidden2_gated"), 1)
                j += 1
            hidden_lower(21, t0, "hidden2_lo")
            for i in range(11):
                lower_parts(j + 2)
                j += 1
            for r in range(4):
                residual(first["down"][1], r)
            layer_norm(2, "ln2_g_2")


_ARGS = ["panels", "x", "ctx_x", "columns", "c_rows", "w_glr", "w_gate", "w_beta_a", "head_rows", "rel_bias"]


def _lay_out(inputs):
    a = {k: np.asarray(v) for k, v in inputs.items()}

    def wide(w, cols=None):
        n = w.shape[1] // 256
        return w.reshape(KT, P, n, 256).transpose(2, 1, 0, 3).reshape(n, P, 2048)

    def across(w):
        n = w.shape[1] // 256
        return w.T.reshape(n, 2, P, D).transpose(0, 2, 1, 3).reshape(n, P, 2048)

    def gate_up(w):
        v = w.reshape(KT, P, 2, FT, P).transpose(3, 1, 0, 2, 4)
        return v.reshape(FT, P, 2048)

    def tall(w):
        return w.reshape(FT // 2, 2, P, D).transpose(0, 2, 1, 3).reshape(FT // 2, P, 2048)

    gla, w2 = a["gla_w_in"][0], a["w_in_2"][0]
    mod, ada = a["mod_w"][0], a["w_ada_2"][0]
    split = [wide(gla[:, 512:1024]), wide(gla[:, 1024:2048]), wide(gla[:, 0:512]),
             wide(gla[:, 2048:3072]), wide(a["gla_w_out"][0]), gate_up(a["ffn_w_in"][0]), tall(a["ffn_w_out"][0]),
             wide(w2[:, 0:4096]), wide(w2[:, 4112:9232]),
             wide(a["w_branch_a_2"][0]), wide(a["w_branch_b_2"][0]), wide(a["w_o_2"][0]),
             gate_up(a["w_up_2"][0]), tall(a["w_down_2"][0])]
    of_kind = {"S": np.concatenate(split), "R": wide(mod[:, 0:2 * D]),
               "A": np.concatenate([across(mod[:, 2 * D:]), across(ada)])}
    out = {"panels": np.stack([of_kind[kind][n] for kind, n in plan_stream()[0]])}

    def feature_major(v):
        return np.ascontiguousarray(v.T.reshape(KT, P, T).transpose(1, 0, 2))

    out["x"], out["ctx_x"] = feature_major(a["x"][0]), feature_major(a["ctx"][0])
    vectors = [a["c"], a["c_ctx"]] + [a[name] for name, _ in COLUMNS[2:]]
    out["columns"] = np.concatenate([v.reshape(-1) for v in vectors]).reshape(NCOL, P).T.copy()
    out["c_rows"] = np.stack([a["c"].reshape(-1), a["c_2"].reshape(-1)])
    out["w_glr"] = gla[:, 3072:3104].reshape(KT, P, 32).transpose(1, 0, 2).copy()
    out["w_gate"] = a["gla_w_gate"][0].copy()
    out["w_beta_a"] = w2[:, 4096:4112].reshape(KT, P, 16).transpose(1, 0, 2).copy()
    out["head_rows"] = np.stack([a["a_log_2"][0], a["dt_bias_2"][0]], axis=1)
    out["rel_bias"] = a["rel_bias_2"][0].copy()
    return out


def kernel(**inputs):
    import concourse.bacc as _bacc
    from concourse.bass_utils import run_bass_kernel_spmd as _run

    nc = _bacc.Bacc("TRN2", target_bir_lowering=False, num_devices=1)
    laid = _lay_out(inputs)
    arrays, args = {}, []
    for name in _ARGS:
        v = laid[name]
        arrays[f"in_{name}"] = v
        args.append(nc.dram_tensor(f"in_{name}", v.shape, mybir.dt.from_np(v.dtype), kind="ExternalInput").ap())
    args.append(nc.dram_tensor("out_x", (P, KT, T), F32, kind="ExternalOutput").ap())
    two_blocks(nc, *args)
    r = _run(nc, [arrays], core_ids=[0])
    return r.results[0]["out_x"].transpose(1, 0, 2).reshape(1, D, T).transpose(0, 2, 1)
```
